# Optimizing a Trainium2 kernel written in Bass

```python
import jax, jax.numpy as jnp
from jax import lax
import numpy as np

D_MODEL = 1024
BATCH = 1
SEQ = 512
DEPTH = 2

HEAD_DIM = 64
A_HEADS = 8
A_KV_HEADS = 2
B_HEADS = 8
B_KV_HEADS = 2
IDX_HEADS = 8
IDX_DIM = 64
WINDOW = 128
BLOCK = 128
TOPK_MAX = 256
ROPE_THETA = 10000.0
D_FF = ((-(-8 * D_MODEL // 3)) + 255) // 256 * 256
ALPHA = (2.0 * DEPTH) ** 0.25
BETA = (8.0 * DEPTH) ** -0.25

A_Q = A_HEADS * HEAD_DIM
A_KV = A_KV_HEADS * HEAD_DIM
B_Q = B_HEADS * HEAD_DIM
B_KV = B_KV_HEADS * HEAD_DIM
I_Q = IDX_HEADS * IDX_DIM
I_K = IDX_DIM
I_W = IDX_HEADS
_PIECES = [A_Q, A_KV, A_KV, B_Q, B_KV, B_KV, I_Q, I_K]
SPLITS = [int(v) for v in np.cumsum(_PIECES)]
D_IN = SPLITS[-1] + I_W

kernel_name = "hybrid_swa_sink_dsa_deepnorm_adaln"

def layer_norm(x, g, b, eps=1e-5):
    xf = x.astype(jnp.float32)
    mu = jnp.mean(xf, -1, keepdims=True)
    var = jnp.mean(jnp.square(xf - mu), -1, keepdims=True)
    return ((xf - mu) * lax.rsqrt(var + eps) * g.astype(jnp.float32) + b.astype(jnp.float32)).astype(x.dtype)

def rms_norm(x, g, eps=1e-6):
    xf = x.astype(jnp.float32)
    ms = jnp.mean(jnp.square(xf), -1, keepdims=True)
    return (xf * lax.rsqrt(ms + eps) * g.astype(jnp.float32)).astype(x.dtype)

def rope(x, pos):
    half = x.shape[-1] // 2
    inv = ROPE_THETA ** (-jnp.arange(half, dtype=jnp.float32) / half)
    ang = pos.astype(jnp.float32)[..., None] * inv
    cos = jnp.cos(ang)[:, :, None, :]
    sin = jnp.sin(ang)[:, :, None, :]
    xf = x.astype(jnp.float32)
    x1, x2 = xf[..., :half], xf[..., half:]
    return jnp.concatenate([x1 * cos - x2 * sin, x2 * cos + x1 * sin], -1).astype(x.dtype)

def swa_with_sinks(q, k, v, sinks):
    B, S, H, D = q.shape
    KVH = k.shape[2]
    G = H // KVH
    nb = S // BLOCK
    qb = q.reshape(B, nb, BLOCK, KVH, G, D)
    kb = k.reshape(B, nb, BLOCK, KVH, D)
    vb = v.reshape(B, nb, BLOCK, KVH, D)
    pad = jnp.zeros_like(kb[:, :1])
    kk = jnp.concatenate([jnp.concatenate([pad, kb[:, :-1]], 1), kb], axis=2)
    vv = jnp.concatenate([jnp.concatenate([pad, vb[:, :-1]], 1), vb], axis=2)
    s = jnp.einsum('bnqhgd,bnkhd->bnhgqk', qb, kk).astype(jnp.float32) * (D ** -0.5)
    qi = jnp.arange(BLOCK)[:, None]
    kj = jnp.arange(2 * BLOCK)[None, :]
    delta = BLOCK + qi - kj
    band = (delta >= 0) & (delta < WINDOW)
    has_prev = (jnp.arange(nb) > 0)[:, None, None] | (kj >= BLOCK)[None]
    mask = band[None] & has_prev
    s = jnp.where(mask[None, :, None, None], s, -jnp.inf)
    sink = jnp.broadcast_to(sinks.astype(jnp.float32).reshape(1, 1, KVH, G, 1, 1), s.shape[:-1] + (1,))
    p = jax.nn.softmax(jnp.concatenate([s, sink], -1), axis=-1)[..., :-1].astype(v.dtype)
    o = jnp.einsum('bnhgqk,bnkhd->bnqhgd', p, vv)
    return o.reshape(B, S, H * D)

def dsa_sparse_attention(q, k, v, qi, ki, wi):
    B, S, H, D = q.shape
    KVH = k.shape[2]
    G = H // KVH
    nb = S // BLOCK
    topk = min(TOPK_MAX, S // 4)
    w_scaled = wi.astype(jnp.float32) * (IDX_HEADS ** -0.5 * IDX_DIM ** -0.5)
    bidx = jnp.arange(B)[:, None, None]
    key_pos = jnp.arange(S)

    def to_blocks(a):
        return a.reshape((B, nb, BLOCK) + a.shape[2:]).swapaxes(0, 1)

    def one_block(args):
        qb, qib, wb, n = args
        t = n * BLOCK + jnp.arange(BLOCK)
        rel = jax.nn.relu(jnp.einsum('bqhd,bsd->bqhs', qib, ki).astype(jnp.float32))
        score = jnp.einsum('bqhs,bqh->bqs', rel, wb)
        causal = key_pos[None, :] <= t[:, None]
        score = jnp.where(causal[None], score, -jnp.inf)
        _, sel = lax.top_k(score, topk)
        ks = k[bidx, sel]
        vs = v[bidx, sel]
        qg = qb.reshape(B, BLOCK, KVH, G, D)
        s = jnp.einsum('bqhgd,bqnhd->bqhgn', qg, ks).astype(jnp.float32) * (D ** -0.5)
        valid = (sel <= t[None, :, None])[:, :, None, None, :]
        s = jnp.where(valid, s, -jnp.inf)
        p = jax.nn.softmax(s, axis=-1).astype(v.dtype)
        o = jnp.einsum('bqhgn,bqnhd->bqhgd', p, vs)
        return o.reshape(B, BLOCK, H * D)

    out = lax.map(one_block, (to_blocks(q), to_blocks(qi), to_blocks(w_scaled), jnp.arange(nb)))
    return out.swapaxes(0, 1).reshape(B, S, H * D)

def hybrid_mixer(h, pos, w_in, sinks, g_a, g_b, w_o):
    B, S, _ = h.shape
    proj = h @ w_in
    qa, ka, va, qb, kb, vb, qi, ki, wi = jnp.split(proj, SPLITS, axis=-1)

    def heads(a, n):
        return a.reshape(B, S, n, -1)

    qa = rope(heads(qa, A_HEADS), pos)
    ka = rope(heads(ka, A_KV_HEADS), pos)
    va = heads(va, A_KV_HEADS)
    qb = rope(heads(qb, B_HEADS), pos)
    kb = rope(heads(kb, B_KV_HEADS), pos)
    vb = heads(vb, B_KV_HEADS)
    qi = rope(heads(qi, IDX_HEADS), pos)
    ki = rope(ki[:, :, None, :], pos)[:, :, 0, :]
    ya = swa_with_sinks(qa, ka, va, sinks)
    yb = dsa_sparse_attention(qb, kb, vb, qi, ki, wi)
    y = jnp.concatenate([rms_norm(ya, g_a), rms_norm(yb, g_b)], -1)
    return y @ w_o

def swiglu(h, w_gate, w_up, w_down):
    return (jax.nn.silu(h @ w_gate) * (h @ w_up)) @ w_down

def setup_inputs(seed: int = 0) -> dict:
    key = jax.random.key(seed)
    ks = jax.random.split(key, 20)
    f32 = jnp.float32
    nrm = lambda k, shape, s: jax.random.normal(k, shape, f32) * s
    x = nrm(ks[0], (BATCH, SEQ, D_MODEL), 1.0)
    c = nrm(ks[1], (BATCH, D_MODEL), 1.0)
    offset = jax.random.randint(ks[2], (BATCH, 1), 0, 1024, dtype=jnp.int32)
    positions = offset + jnp.arange(SEQ, dtype=jnp.int32)[None, :]
    w_ada = nrm(ks[3], (DEPTH, D_MODEL, 6 * D_MODEL), 0.5 * D_MODEL ** -0.5)
    b_ada = nrm(ks[4], (DEPTH, 6 * D_MODEL), 0.01)
    col_scale = np.ones((D_IN,), np.float32)
    col_scale[SPLITS[1]:SPLITS[2]] = BETA
    col_scale[SPLITS[4]:SPLITS[5]] = BETA
    w_in = nrm(ks[5], (DEPTH, D_MODEL, D_IN), D_MODEL ** -0.5) * jnp.asarray(col_scale)
    attn_sinks = nrm(ks[6], (DEPTH, A_HEADS), 1.0)
    g_a = 1.0 + nrm(ks[7], (DEPTH, A_Q), 0.02)
    g_b = 1.0 + nrm(ks[8], (DEPTH, B_Q), 0.02)
    w_o = nrm(ks[9], (DEPTH, A_Q + B_Q, D_MODEL), BETA * (A_Q + B_Q) ** -0.5)
    ln1_g = 1.0 + nrm(ks[10], (DEPTH, D_MODEL), 0.02)
    ln1_b = nrm(ks[11], (DEPTH, D_MODEL), 0.02)
    w_gate = nrm(ks[12], (DEPTH, D_MODEL, D_FF), D_MODEL ** -0.5)
    w_up = nrm(ks[13], (DEPTH, D_MODEL, D_FF), D_MODEL ** -0.5)
    w_down = nrm(ks[14], (DEPTH, D_FF, D_MODEL), BETA * D_FF ** -0.5)
    ln2_g = 1.0 + nrm(ks[15], (DEPTH, D_MODEL), 0.02)
    ln2_b = nrm(ks[16], (DEPTH, D_MODEL), 0.02)
    return {"x": x, "c": c, "positions": positions, "w_ada": w_ada, "b_ada": b_ada,
            "w_in": w_in, "attn_sinks": attn_sinks, "g_a": g_a, "g_b": g_b, "w_o": w_o,
            "ln1_g": ln1_g, "ln1_b": ln1_b, "w_gate": w_gate, "w_up": w_up, "w_down": w_down,
            "ln2_g": ln2_g, "ln2_b": ln2_b}

def reference(x, c, positions, w_ada, b_ada, w_in, attn_sinks, g_a, g_b, w_o,
              ln1_g, ln1_b, w_gate, w_up, w_down, ln2_g, ln2_b):
    c_act = jax.nn.silu(c)
    for l in range(DEPTH):
        mod = (c_act @ w_ada[l] + b_ada[l])[:, None, :]
        sh1, sc1, gt1, sh2, sc2, gt2 = jnp.split(mod, 6, axis=-1)
        h = x * (1.0 + sc1) + sh1
        y = hybrid_mixer(h, positions, w_in[l], attn_sinks[l], g_a[l], g_b[l], w_o[l])
        x = layer_norm(ALPHA * x + (1.0 + gt1) * y, ln1_g[l], ln1_b[l])
        h = x * (1.0 + sc2) + sh2
        y = swiglu(h, w_gate[l], w_up[l], w_down[l])
        x = layer_norm(ALPHA * x + (1.0 + gt2) * y, ln2_g[l], ln2_b[l])
    return x


_drawn_inputs = setup_inputs


def setup_inputs(seed=0):
    import zlib

    import numpy as np

    out = dict(_drawn_inputs(seed))
    spreads = {}
    factors = {'attn_sinks': 4.013, 'g_a': 6.032, 'g_b': 5.72}
    for name, (base, spread) in spreads.items():
        noise = np.random.default_rng([zlib.crc32(name.encode()), seed]).standard_normal(out[name].shape)
        drawn = base * np.exp(spread * noise) if base else spread * noise
        out[name] = __import__('jax').numpy.asarray(drawn.astype(out[name].dtype))
    for name, factor in factors.items():
        out[name] = (out[name] * factor).astype(out[name].dtype)
    return out
```

```python
from contextlib import ExitStack

import numpy as np

import concourse.bass as bass
from concourse import mybir

F32 = mybir.dt.float32
F32R = mybir.dt.float32r
I32 = mybir.dt.int32
ALU = mybir.AluOpType
ACT = mybir.ActivationFunctionType

P = 128
D_MODEL, SEQ, DEPTH = 1024, 512, 2
HD = 64
HEADS = 8
KV_HEADS = 2
PAIRS = HEADS // KV_HEADS
TOPK = min(256, SEQ // 4)
D_FF = ((-(-8 * D_MODEL // 3)) + 255) // 256 * 256
ALPHA = (2.0 * DEPTH) ** 0.25
LN_EPS, RMS_EPS = 1e-5, 1e-6
ROPE_THETA = 10000.0

T = SEQ // P
KD = D_MODEL // P
HALF = D_MODEL // 2
FC = D_FF // P
FG = (12, FC - 12)
PW = 1024

CW = (512, 328, 512, 256, 512)
CK = (2, 2, 2, 4, 2)
CP = tuple(KD // k for k in CK)
C0P = tuple(sum(CP[:c]) for c in range(5))
WO_P = sum(CP)
GU_P = (WO_P + 8, WO_P + 8 + 2 * FG[0] + FG[0])
DN_P = (GU_P[0] + 2 * FG[0], GU_P[1] + 2 * FG[1])
NP = DN_P[1] + FG[1]
RING = 4
assert NP % RING == 0 and NP == 92 and D_MODEL == 1024 and SEQ == 512

PHASES = [(C0P[c], CP[c]) for c in range(5)] + [(WO_P, 4), (WO_P + 4, 4)]
for _g in range(2):
    PHASES += [(DN_P[_g], FG[_g] // 2), (DN_P[_g] + FG[_g] // 2, FG[_g] // 2)]
WO0, WO1, DN00, DN01, DN10, DN11 = range(5, 11)
BANKS = {0: 0, 1: 4, 2: 0, 3: 0, 4: 0, WO0: 0, WO1: 4, DN00: 0, DN01: 4, DN10: 4, DN11: 0}
GU_BANK = (4, 0)

UNITS = [("A", t) for t in range(T)] + [("B", 0), ("B", 3), ("B", 2), ("B", 1)]
IDX_TILES = (3, 2, 1)
SC_AT = (0, 128, 384, 768)
SC_W = 1280
P_RING = 4
S_BANKS = (3, 4, 5)
PT_RING = 4
DVE_HEADS = (3, 7)
LAG_T, LAG_V = 3, 5
ROPE_AT, QB_AT = (1, 3, 5, 7), (5, 7, 9, 11)
LAG_NORM, LAG_SCALE, LAG_Y, LAG_GAIN, LAG_HI, LAG_LO = 6, 7, 9, 10, 11, 12

SH1, SC1, GT1, SH2, SC2, GT2 = range(6)

TAKEN = -3.3e38
CUT = -3.1e38
NEG = -1.0e38


def keys_of(unit):
    kind, t = unit
    lo = max(t - 1, 0) * P if kind == "A" else 0
    return lo, (t + 1) * P


def build_trunk(nc, x, c_col, positions, inv_freq, weights, w_ada, b_ada, ln_col, ln_row, sinks, g_col, out):
    with ExitStack() as ctx:
        def sb(name, shape, dt=F32, on=ctx):
            return on.enter_context(nc.sbuf_tensor(name, shape, dt))

        def sem(name):
            return ctx.enter_context(nc.semaphore(name))

        bank = [ctx.enter_context(nc.psum_tensor(f"bank{i}", [P, 512], F32)) for i in range(8)]

        w_raw = sb("w_raw", [P, RING, PW])
        w_hi = sb("w_hi", [P, RING, PW], F32R)
        w_lo = sb("w_lo", [P, RING, PW], F32R)
        xs = sb("xs", [P, T, D_MODEL])
        hT_hi = sb("hT_hi", [P, KD, SEQ], F32R)
        hT_lo = sb("hT_lo", [P, KD, SEQ], F32R)
        scratch = sb("scratch", [P, PW])
        ada_w = sb("ada_w", [P, RING, PW])
        ada_acc = sb("ada_acc", [P, 2, PW])
        gt_row = sb("gt_row", [P, D_MODEL])
        g_row = sb("g_row", [P, D_MODEL])
        b_row = sb("b_row", [P, D_MODEL])
        ident = sb("ident", [P, P])
        ones = sb("ones", [P, P])
        band = sb("band", [P, 2 * P])
        cos_t = sb("cos_t", [P, T, HD])
        sin_t = sb("sin_t", [P, T, HD])
        cc = sb("cc", [P, 2, KD])
        modb = sb("modb", [P, 6 * DEPTH, KD])
        mod = sb("mod", [P, 6 * DEPTH, KD])
        lnc = sb("lnc", [P, 2 * DEPTH, 2, KD])
        hcoef = sb("hcoef", [P, 2 * DEPTH, 2, KD])
        gcol = sb("gcol", [P, DEPTH, 2, 4])
        nsink = sb("nsink", [P, DEPTH, HEADS])
        stats = sb("stats", [P, T, 2, 6])
        mean_var = sb("mean_var", [P, T, 2])
        rs_in = sb("rs_in", [P, 32])
        rs_out = sb("rs_out", [P, 32])
        minus_half = sb("minus_half", [P, 1])
        rowsum = sb("rowsum", [P, 2, HEADS])
        nmax = sb("nmax", [P, 2, HEADS])
        es = sb("es", [P, 2, HEADS])
        recip = sb("recip", [P, 2, HEADS])
        top8 = sb("top8", [P, T, 8])

        with ExitStack() as att:
            pq = sb("pq", [P, 2, T, 512], on=att)
            pk = sb("pk", [P, T, 256], on=att)
            v_b = sb("v_b", [P, T, P + HEADS], on=att)
            v_a = sb("v_a", [P, T, P], on=att)
            qT = sb("qT", [P, 2, PAIRS, SEQ], on=att)
            kT = sb("kT", [P, 3, SEQ], on=att)
            scores = sb("scores", [P, SC_W], on=att)
            pT = sb("pT", [P, PT_RING, 512], on=att)
            y = sb("y", [P, 2, 512], on=att)
        rel = pq[:, 0]
        prob = pq[:, 1]
        with ExitStack() as ffn:
            gu_hi = sb("gu_hi", [P, FG[0], SEQ], F32R, on=ffn)
            gu_lo = sb("gu_lo", [P, FG[0], SEQ], F32R, on=ffn)
            silu_g = sb("silu_g", [P, 2, SEQ], on=ffn)
            gu = sb("gu", [P, 2, SEQ], on=ffn)
            ztmp = sb("ztmp", [P, HALF], on=ffn)

        raw_in = [sem(f"raw_in{i}") for i in range(RING)]
        ada_in = [sem(f"ada_in{i}") for i in range(RING)]
        x_in = [sem(f"x_in{i}") for i in range(T)]
        small_in = sem("small_in")
        row_in = sem("row_in")
        out_done = sem("out_done")
        consts = sem("consts")
        pool_step = sem("pool_step")
        hi_ready = sem("hi_ready")
        lo_ready = sem("lo_ready")
        piece_used = sem("piece_used")
        tile_done = sem("tile_done")
        x_transposed = sem("x_transposed")
        coef_ready = sem("coef_ready")
        h_scaled_dve = sem("h_scaled_dve")
        h_scaled_act = sem("h_scaled_act")
        h_hi = sem("h_hi")
        h_lo = sem("h_lo")
        proj_evac = sem("proj_evac")
        roped = sem("roped")
        qk_transposed = sem("qk_transposed")
        qk_ready = sem("qk_ready")
        idx_scored = sem("idx_scored")
        relu_done = sem("relu_done")
        idx_acc = sem("idx_acc")
        scored = sem("scored")
        masked = sem("masked")
        probs = sem("probs")
        sink_diff = sem("sink_diff")
        sink_exp = sem("sink_exp")
        p_transposed = sem("p_transposed")
        pT_act = sem("pT_act")
        pT_dve = sem("pT_dve")
        av_done = sem("av_done")
        rs_asked = sem("rs_asked")
        rs_done = sem("rs_done")
        y_ready = sem("y_ready")
        y_transposed = sem("y_transposed")
        y_scaled = sem("y_scaled")
        yT_hi = sem("yT_hi")
        yT_lo = sem("yT_lo")
        z_done = sem("z_done")
        xhat_ready = sem("xhat_ready")
        affine_done = sem("affine_done")
        gate_read = sem("gate_read")
        gu_ready = sem("gu_ready")
        gu_hi_ready = sem("gu_hi_ready")
        gu_lo_ready = sem("gu_lo_ready")
        ada_used = sem("ada_used")
        mod_taken = sem("mod_taken")
        mod_reduced = sem("mod_reduced")
        gt_diag = sem("gt_diag")
        gt_spread = sem("gt_spread")
        gt_taken = sem("gt_taken")
        dve_step = sem("dve_step")
        rope_angle = sem("rope_angle")
        rope_table = sem("rope_table")

        def converted(l, p):
            return l * NP + p + 1

        def used(l, p):
            return RING + l * NP + p + 1

        def slot(l, p):
            return (l * NP + p) % RING

        def wait_phase(eng, l, q, t):
            if t < T - 1:
                eng.wait_ge(tile_done, l * 33 + 3 * q + t + 1)
            else:
                eng.wait_ge(piece_used, used(l, PHASES[q][0] + PHASES[q][1] - 1))

        def at_tile(stage, t):
            return T * stage + t + 1

        def at_chunk(l, c, t):
            return 20 * l + 4 * c + t + 1

        def at_head(l, u, h):
            return 64 * l + 8 * u + h + 1

        def at_unit(l, u):
            return 8 * l + u + 1

        def at_z(l, q, t):
            return 24 * l + 4 * (q - WO0) + t + 1

        def rs_index(l, r):
            return 16 * l + r

        def qk_bank(c, t):
            return 2 if c == 4 else 4 + t

        def gu_before(l, g):
            return l * FC + g * FG[0]

        def on_dve(u, h):
            return u >= 4 and h in DVE_HEADS

        dve_heads = 4 * len(DVE_HEADS)

        def wait_pT(eng, l, u, h):
            flat = [(a, b) for a in range(8) for b in range(HEADS) if (a, b) <= (u, h)]
            n_dve = sum(on_dve(a, b) for a, b in flat)
            if on_dve(u, h):
                eng.wait_ge(pT_dve, l * dve_heads + n_dve)
            else:
                eng.wait_ge(pT_act, l * (64 - dve_heads) + len(flat) - n_dve)

        def back(u, h, n):
            i = 8 * u + h - n
            return None if i < 0 else (i // 8, i % 8)

        NSMALL = 8
        block = ctx.enter_context(nc.Block())

        @block.sync
        def _(sp):
            sp.wait_ge(ada_used, 3)
            for t in range(T):
                sp.dma_start(xs[:, t, :], x[t]).then_inc(x_in[t], 16)
            sp.wait_ge(ada_used, 9)
            for s in range(RING):
                sp.dma_start(w_raw[:, s, :], weights[s]).then_inc(raw_in[s], 16)
            with sp.Fori(1, DEPTH * NP // RING) as i:
                for s in range(RING):
                    sp.wait_ge(lo_ready, i * RING + (s - RING + 1))
                    sp.dma_start(w_raw[:, s, :], weights[i * RING + s]).then_inc(raw_in[s], 16)
            for t in range(T):
                sp.wait_ge(affine_done, at_tile(2 * DEPTH - 1, t))
                sp.dma_start(out[t], xs[:, t, :]).then_inc(out_done, 16)
            sp.wait_ge(out_done, 16 * T)

        @block.gpsimd
        def _(pool):
            fetched = [0]

            def ada_fetch(upto):
                while fetched[0] < upto:
                    n = fetched[0]
                    if n >= RING:
                        pool.wait_ge(ada_used, n - RING + 1)
                    pool.dma_start(ada_w[:, n % RING, :], w_ada[n // KD, n % KD]).then_inc(ada_in[n % RING], 16)
                    fetched[0] += 1

            def rsqrt(l, r):
                n = rs_index(l, r)
                pool.wait_ge(rs_asked, n + 1)
                nc.gpsimd.tensor_tensor(rs_out[:, n:n + 1], rs_in[:, n:n + 1], minus_half[:], ALU.pow)\
                    .then_inc(rs_done, 1)

            def ln_rows(stage):
                if stage > 1:
                    pool.wait_ge(affine_done, at_tile(stage - 2, T - 1))
                pool.dma_start(g_row[:], ln_row[stage - 1, 0:1, :].to_broadcast([P, D_MODEL])).then_inc(row_in, 16)
                pool.dma_start(b_row[:], ln_row[stage - 1, 1:2, :].to_broadcast([P, D_MODEL])).then_inc(row_in, 16)

            ada_fetch(RING)
            nc.gpsimd.memset(minus_half[:], -0.5).then_inc(pool_step, 1)
            nc.gpsimd.memset(ident[:], 0.0).then_inc(pool_step, 1)
            nc.gpsimd.memset(band[:], 0.0).then_inc(pool_step, 1)
            nc.gpsimd.memset(ones[:], 1.0).then_inc(consts, 1)
            pool.wait_ge(pool_step, 3)
            nc.gpsimd.affine_select(out=ident[:], in_=ident[:], compare_op=ALU.not_equal, fill=1.0, base=0,
                                    pattern=[[-1, P]], channel_multiplier=1).then_inc(consts, 1)
            nc.gpsimd.affine_select(out=band[:, 0:P], in_=band[:, 0:P], compare_op=ALU.is_ge, fill=NEG, base=-1,
                                    pattern=[[1, P]], channel_multiplier=-1).then_inc(consts, 1)
            nc.gpsimd.affine_select(out=band[:, P:2 * P], in_=band[:, P:2 * P], compare_op=ALU.is_ge, fill=NEG,
                                    base=0, pattern=[[-1, P]], channel_multiplier=1).then_inc(consts, 1)
            for l in range(DEPTH):
                if l == 0:
                    ada_fetch(4 * KD + RING)
                for u in range(8):
                    rsqrt(l, u)
                if l == 0:
                    ada_fetch(5 * KD + RING)
                ln_rows(2 * l + 1)
                for t in range(T):
                    rsqrt(l, 8 + t)
                if l == 0:
                    base = 5 * KD + RING
                    with pool.Fori(0, FG[0] // 2) as i:
                        for j in range(KD):
                            pool.wait_ge(ada_used, i * KD + (base + j - RING + 1))
                            pool.dma_start(ada_w[:, j % RING, :], w_ada[i + (base + j) // KD, (base + j) % KD])\
                                .then_inc(ada_in[j % RING], 16)
                    fetched[0] = base + KD * FG[0] // 2
                    ada_fetch(6 * DEPTH * KD)
                ln_rows(2 * l + 2)
                for t in range(T):
                    rsqrt(l, 12 + t)

        @block.tensor
        def _(pe):
            nc.tensor.sem_inc(piece_used, RING)

            def wait_piece(l, p):
                pe.wait_ge(hi_ready, converted(l, p))
                pe.wait_ge(lo_ready, converted(l, p))

            def split_product(dst, a_hi, a_lo, b_hi, b_lo, first, last):
                pe.matmul(dst, a_hi, b_hi, start=first, stop=False)
                pe.matmul(dst, a_hi, b_lo, start=False, stop=False)
                return pe.matmul(dst, a_lo, b_hi, start=False, stop=last)

            def transpose_x(stage, t, b0):
                if stage == 0:
                    pe.wait_ge(x_in[t], 16)
                    pe.wait_ge(consts, 4)
                else:
                    pe.wait_ge(xhat_ready, at_tile(stage - 1, t))
                if t >= 2:
                    pe.wait_ge(h_scaled_dve, at_tile(stage, t - 2))
                    pe.wait_ge(h_scaled_act, at_tile(stage, t - 2))
                for k in range(KD):
                    m = pe.transpose(bank[b0 + 2 * (t % 2) + k // 4][:, (k % 4) * P:(k % 4 + 1) * P],
                                     xs[:, t, k * P:(k + 1) * P], ident[:])
                m.then_inc(x_transposed, 1)

            def reduce_mod(g, b):
                pe.wait_ge(ada_used, (g + 1) * KD)
                for k in range(KD):
                    m = pe.matmul(bank[b][:, k:k + 1], ada_acc[:, g % 2, k * P:(k + 1) * P], ones[:, 0:1],
                                  start=True, stop=True)
                m.then_inc(mod_reduced, 1)

            def spread_gate(l, which, b):
                pe.wait_ge(gt_diag, 2 * l + which + 1)
                for half in range(2):
                    m = pe.matmul(bank[b + half][:], ones[:], scratch[:, half * 512:(half + 1) * 512],
                                  start=True, stop=True)
                m.then_inc(gt_spread, 1)

            def accumulate(l, q, j0, j1, a_hi, a_lo, nk, width, wait_tile):
                p0, n = PHASES[q]
                for j in range(j0, j1):
                    wait_piece(l, p0 + j)
                    s = slot(l, p0 + j)
                    for t in range(T):
                        if j == 0:
                            wait_tile(t)
                        rows = slice(t * P, (t + 1) * P)
                        for kk in range(nk):
                            k = j * nk + kk
                            cols = slice(kk * width, (kk + 1) * width)
                            m = split_product(bank[BANKS[q] + t][:, 0:width], a_hi[:, k, rows], a_lo[:, k, rows],
                                              w_hi[:, s, cols], w_lo[:, s, cols],
                                              j == 0 and kk == 0, j == n - 1 and kk == nk - 1)
                        if t == T - 1:
                            m.then_inc(piece_used, 1)
                        elif j == n - 1:
                            m.then_inc(tile_done, 1)

            def finish_tile(l, q, t, a_hi, a_lo, wait_tile):
                p0, n = PHASES[q]
                rows = slice(t * P, (t + 1) * P)
                if n == 4:
                    wait_tile(t)
                for j in range(n - 4, n):
                    if t == 0:
                        wait_piece(l, p0 + j)
                    s = slot(l, p0 + j)
                    for kk in range(2):
                        k = 2 * j + kk
                        cols = slice(kk * 512, (kk + 1) * 512)
                        m = split_product(bank[BANKS[q] + t][:], a_hi[:, k, rows], a_lo[:, k, rows],
                                          w_hi[:, s, cols], w_lo[:, s, cols], k == 0, k == 2 * n - 1)
                    if t == T - 1:
                        m.then_inc(piece_used, 1)
                if t < T - 1:
                    m.then_inc(tile_done, 1)

            def project(l, c, j0, j1):
                def wait_tile(t):
                    if c == 0:
                        pe.wait_ge(h_lo, at_tile(2 * l, t))
                        if l > 0:
                            pe.wait_ge(z_done, at_z(l - 1, DN11, t))
                    elif c == 1:
                        pe.wait_ge(h_scaled_dve, at_tile(2 * l, T - 1))
                        pe.wait_ge(h_scaled_act, at_tile(2 * l, T - 1))
                    else:
                        pe.wait_ge(proj_evac, at_chunk(l, (0, 1, 0, 2, 3)[c], t))
                accumulate(l, c, j0, j1, hT_hi, hT_lo, CK[c], CW[c], wait_tile)

            def transpose_qk(l, c, t):
                pe.wait_ge(roped, at_chunk(l, c, t))
                if c == 0:
                    pe.wait_ge(proj_evac, at_chunk(l, 1, t))
                elif c == 2:
                    pe.wait_ge(relu_done, 24 * (l + 1))
                elif c < 4:
                    pe.wait_ge(qk_ready, at_chunk(l, c - 1, t))
                elif t == 0:
                    pe.wait_ge(proj_evac, at_chunk(l, 4, 2))
                else:
                    pe.wait_ge(qk_ready, at_chunk(l, 4, t - 1))
                for j in range((4, 2, 4, 1, 4)[c]):
                    src = pk[:, t, j * P:(j + 1) * P] if c in (1, 3) else pq[:, (c // 2) % 2, t, j * P:(j + 1) * P]
                    m = pe.transpose(bank[qk_bank(c, t)][:, j * P:(j + 1) * P], src, ident[:])
                m.then_inc(qk_transposed, 1)

            def index_scores(l):
                for i, t in enumerate(IDX_TILES):
                    for h in range(HEADS):
                        n = 24 * l + 8 * i + h
                        if i == 0 and h < 4:
                            pe.wait_ge(qk_ready, at_chunk(l, 1, T - 1))
                        else:
                            pe.wait_ge(relu_done, n - 3)
                        g = 64 * (h % 2)
                        pe.matmul(bank[4 + h % 4][:, 0:(t + 1) * P], qT[g:g + HD, 0, h // 2, t * P:(t + 1) * P],
                                  kT[g:g + HD, 0, 0:(t + 1) * P], start=True, stop=True).then_inc(idx_scored, 1)

            def head_scores(l, u, h):
                kind, t = UNITS[u]
                lo, hi = keys_of(UNITS[u])
                n = 8 * u + h
                if n < len(S_BANKS):
                    pe.wait_ge(qk_ready, at_chunk(l, 3, T - 1))
                    pe.wait_ge(proj_evac, at_chunk(l, 4, T - 1))
                else:
                    pe.wait_ge(masked, at_head(l, u, h) - len(S_BANKS))
                if (u, h) == (4, 0):
                    pe.wait_ge(qk_ready, at_chunk(l, 4, T - 1))
                g = 64 * (h % 2)
                q, k = (1, 2) if kind == "A" else (0, 1)
                pe.matmul(bank[S_BANKS[n % 3]][:, 0:hi - lo], qT[g:g + HD, q, h // 2, t * P:(t + 1) * P],
                          kT[g:g + HD, k, lo:hi], start=True, stop=True).then_inc(scored, 1)

            def transpose_p(l, u, h):
                lo, hi = keys_of(UNITS[u])
                pe.wait_ge(probs, at_head(l, u, h))
                if before := back(u, h, 2):
                    wait_pT(pe, l, *before)
                n = 8 * u + h
                for b in range((hi - lo) // P):
                    m = pe.transpose(bank[6 + h % 2][:, b * P:(b + 1) * P],
                                     prob[:, n % P_RING, b * P:(b + 1) * P], ident[:])
                m.then_inc(p_transposed, 1)

            def head_values(l, u, h):
                kind, t = UNITS[u]
                lo, hi = keys_of(UNITS[u])
                wait_pT(pe, l, u, h)
                if h == 0:
                    if u >= 2:
                        pe.wait_ge(y_ready, at_unit(l, u - 2))
                    else:
                        pe.wait_ge(proj_evac, at_chunk(l, 4, T - 1))
                v = v_a if kind == "A" else v_b
                g = 64 * (h % 2)
                nb = (hi - lo) // P
                for b in range(nb):
                    m = pe.matmul(bank[u % 2][:, h * HD:(h + 1) * HD], pT[:, h % PT_RING, b * P:(b + 1) * P],
                                  v[:, lo // P + b, g:g + HD], start=b == 0, stop=b == nb - 1)
                m.then_inc(av_done, 1)

            def transpose_y(l, u):
                pe.wait_ge(y_ready, at_unit(l, u))
                if u == 0:
                    pe.wait_ge(qk_ready, at_chunk(l, 4, T - 1))
                else:
                    pe.wait_ge(y_scaled, at_unit(l, u - 1))
                for j in range(4):
                    m = pe.transpose(bank[2][:, j * P:(j + 1) * P], y[:, u % 2, j * P:(j + 1) * P], ident[:])
                m.then_inc(y_transposed, 1)

            def attention(l):
                for i in range(64 + LAG_Y):
                    if i < 64:
                        head_scores(l, i // 8, i % 8)
                    if 0 <= i - LAG_T < 64:
                        transpose_p(l, (i - LAG_T) // 8, (i - LAG_T) % 8)
                    if 0 <= i - LAG_V < 64:
                        head_values(l, (i - LAG_V) // 8, (i - LAG_V) % 8)
                    if i in QB_AT:
                        transpose_qk(l, 4, QB_AT.index(i))
                    if (i - LAG_Y) % 8 == 7 and i > LAG_Y:
                        transpose_y(l, (i - LAG_Y) // 8)

            def gate_up(l, g):
                s0 = slot(l, GU_P[g])
                b0 = GU_BANK[g]
                pe.wait_ge(h_lo, at_tile(2 * l + 1, T - 1))
                if g == 0:
                    pe.wait_ge(z_done, at_z(l, WO1, T - 1))
                else:
                    pe.wait_ge(z_done, at_z(l, DN00, T - 1))
                with pe.Fori(0, FG[g] // 2) as i:
                    for j in range(4):
                        pe.wait_ge(hi_ready, i * 4 + converted(l, GU_P[g] + j))
                        pe.wait_ge(lo_ready, i * 4 + converted(l, GU_P[g] + j))
                        pe.wait_ge(gate_read if j % 2 == 0 else gu_ready, i * 2 + (gu_before(l, g) + j // 2 + 1))
                        s = (s0 + j) % RING
                        for k in range(KD):
                            w = slice(k * P, (k + 1) * P)
                            pe.matmul(bank[b0 + j][:], w_hi[:, s, w], hT_hi[:, k, :], start=k == 0, stop=False)
                            pe.matmul(bank[b0 + j][:], w_hi[:, s, w], hT_lo[:, k, :], start=False, stop=False)
                            m = pe.matmul(bank[b0 + j][:], w_lo[:, s, w], hT_hi[:, k, :], start=False,
                                          stop=k == KD - 1)
                        m.then_inc(piece_used, 1)
                    if (l, g) == (0, 0):
                        pe.wait_ge(ada_used, i * KD + 6 * KD)
                        for k in range(KD):
                            m = pe.matmul(bank[0][:, k:k + 1], ada_acc[:, 1, k * P:(k + 1) * P], ones[:, 0:1],
                                          start=True, stop=True)
                        m.then_inc(mod_reduced, 1)

            def down(l, g, half):
                q = DN00 + 2 * g + half
                last = (g, half) == (1, 1)

                def wait_tile(t):
                    if half == 0 and t == 0:
                        pe.wait_ge(gu_lo_ready, gu_before(l, g) + FG[g])
                    if q == DN00 and t == 0:
                        pe.wait_ge(h_scaled_dve, at_tile(2 * l + 1, T - 1))
                        pe.wait_ge(h_scaled_act, at_tile(2 * l + 1, T - 1))
                        pe.wait_ge(z_done, at_z(l, WO0, T - 1))
                        pe.wait_ge(gt_taken, 2 * l + 2)
                    elif q in (DN01, DN11) and t == 0:
                        pe.wait_ge(gu_ready, gu_before(l, g) + FG[g] + 2)
                        pe.wait_ge(gate_read, gu_before(l, g) + FG[g] + 2)
                    elif q == DN10:
                        pe.wait_ge(z_done, at_z(l, DN01, t))
                        if t == T - 1:
                            pe.wait_ge(mod_taken, 6 * DEPTH)

                if not last:
                    accumulate(l, q, 0, PHASES[q][1], gu_hi, gu_lo, 2, 512, wait_tile)
                    return
                accumulate(l, q, 0, PHASES[q][1] - 4, gu_hi, gu_lo, 2, 512, wait_tile)
                for t in range(T):
                    finish_tile(l, q, t, gu_hi, gu_lo, wait_tile)
                    if l + 1 < DEPTH:
                        if t >= 2:
                            transpose_x(2 * l + 2, t - 2, 4)
                if l + 1 < DEPTH:
                    transpose_x(2 * l + 2, 2, 4)
                    transpose_x(2 * l + 2, 3, 4)

            transpose_x(0, 0, 4)
            transpose_x(0, 1, 4)
            reduce_mod(0, 0)
            reduce_mod(1, 1)
            transpose_x(0, 2, 4)
            transpose_x(0, 3, 4)
            for l in range(DEPTH):
                project(l, 0, 0, 4)
                project(l, 1, 0, 4)
                project(l, 2, 0, 2)
                for t in range(T):
                    transpose_qk(l, 0, t)
                for t in range(T):
                    transpose_qk(l, 1, t)
                index_scores(l)
                project(l, 2, 2, 4)
                project(l, 3, 0, 2)
                for t in range(T):
                    transpose_qk(l, 2, t)
                for t in range(T):
                    transpose_qk(l, 3, t)
                project(l, 4, 0, 4)
                attention(l)
                if l == 0:
                    pe.wait_ge(masked, at_head(l, 7, 7))
                    wait_pT(pe, l, 7, 6)
                    wait_pT(pe, l, 7, 7)
                    reduce_mod(2, 7)
                    reduce_mod(3, 4)
                spread_gate(l, 0, 5)

                def wait_wo0(t):
                    pe.wait_ge(yT_lo, at_unit(l, 7))
                    pe.wait_ge(masked, at_head(l, 7, 7))

                def wait_wo1(t):
                    if t == 0:
                        pe.wait_ge(gt_taken, 2 * l + 1)
                        pe.wait_ge(mod_taken, 4)
                        pe.wait_ge(masked, at_head(l, 7, 7))
                        wait_pT(pe, l, 7, 6)
                        wait_pT(pe, l, 7, 7)
                    if l == 0 and t == 3:
                        pe.wait_ge(mod_taken, 5)

                accumulate(l, WO0, 0, 4, hT_hi, hT_lo, 2, 512, wait_wo0)
                if l == 0:
                    reduce_mod(4, 7)
                for t in range(T):
                    finish_tile(l, WO1, t, hT_hi, hT_lo, wait_wo1)
                    if t == 0:
                        pe.wait_ge(z_done, at_z(l, WO0, T - 1))
                    if t >= 2:
                        transpose_x(2 * l + 1, t - 2, 0)
                transpose_x(2 * l + 1, 2, 0)
                transpose_x(2 * l + 1, 3, 0)
                for g in range(2):
                    gate_up(l, g)
                    if (l, g) == (0, 1):
                        reduce_mod(6 * DEPTH - 1, 7)
                    if g == 0:
                        spread_gate(l, 1, 2)
                    down(l, g, 0)
                    down(l, g, 1)

        @block.scalar
        def _(act):
            conv = [0]

            def convert(l, upto):
                while conv[0] < min(l * NP + upto, DEPTH * NP):
                    p = conv[0]
                    act.wait_ge(raw_in[p % RING], 16 * (p // RING + 1))
                    act.wait_ge(piece_used, p + 1)
                    nc.scalar.activation(w_hi[:, p % RING, :], w_raw[:, p % RING, :], ACT.Copy).then_inc(hi_ready, 1)
                    conv[0] += 1

            def build_h(stage, t, b0):
                act.wait_ge(coef_ready, stage + 1)
                act.wait_ge(x_transposed, at_tile(stage, t))
                if stage > 0 or t > 0:
                    act.wait_ge(h_lo, at_tile(stage, t) - 1)
                    act.wait_ge(h_hi, at_tile(stage, t) - 1)
                if t == 0 and stage % 2 == 1:
                    act.wait_ge(yT_lo, at_unit(stage // 2, 7))
                    act.wait_ge(gt_spread, 2 * (stage // 2) + 1)
                elif t == 0 and stage > 0:
                    act.wait_ge(gt_spread, stage)
                for k in range(4, KD):
                    m = nc.scalar.activation(scratch[:, k * P:(k + 1) * P],
                                             bank[b0 + 2 * (t % 2) + 1][:, (k - 4) * P:(k - 3) * P],
                                             ACT.Identity, scale=hcoef[:, stage, 0, k:k + 1],
                                             bias=hcoef[:, stage, 1, k:k + 1])
                m.then_inc(h_scaled_act, 1)
                act.wait_ge(h_scaled_act, at_tile(stage, t))
                act.wait_ge(h_scaled_dve, at_tile(stage, t))
                nc.scalar.activation(hT_hi[:, :, t * P:(t + 1) * P],
                                     scratch[:].rearrange("p (k s) -> p k s", k=KD), ACT.Copy).then_inc(h_hi, 1)

            def evacuate(l, c, t):
                wait_phase(act, l, c, t)
                src = bank[BANKS[c] + t]
                if c in (0, 2, 4):
                    if c == 4:
                        act.wait_ge(idx_acc, 24 * (l + 1))
                    elif l > 0 and c == 0:
                        act.wait_ge(qk_transposed, at_chunk(l - 1, 4, t))
                    elif l > 0:
                        act.wait_ge(p_transposed, 64 * l)
                    nc.scalar.activation(pq[:, (c // 2) % 2, t, :], src[:], ACT.Copy).then_inc(proj_evac, 1)
                elif c == 1:
                    if l > 0:
                        act.wait_ge(qk_transposed, at_chunk(l - 1, 3, t))
                    for d in range(2):
                        nc.scalar.activation(pk[:, t, d * HD:(d + 1) * HD], src[:, 0:HD], ACT.Copy)
                    nc.scalar.activation(pk[:, t, P:2 * P], src[:, HD:HD + P], ACT.Copy)
                    nc.scalar.activation(v_b[:, t, 0:P], src[:, HD + P:HD + 2 * P], ACT.Copy)
                    nc.scalar.activation(v_b[:, t, P:P + HEADS], src[:, HD + 2 * P:HD + 2 * P + HEADS], ACT.Copy,
                                         scale=HEADS ** -0.5 * HD ** -0.5).then_inc(proj_evac, 1)
                else:
                    act.wait_ge(qk_transposed, at_chunk(l, 1, t))
                    nc.scalar.activation(pk[:, t, 0:P], src[:, 0:P], ACT.Copy)
                    nc.scalar.activation(v_a[:, t, :], src[:, P:2 * P], ACT.Copy).then_inc(proj_evac, 1)

            def copy_qk(l, c, t):
                act.wait_ge(qk_transposed, at_chunk(l, c, t))
                if c == 4 and t == 0:
                    act.wait_ge(idx_scored, 24 * (l + 1))
                n = (4, 2, 4, 1, 4)[c]
                cols = slice(t * P, (t + 1) * P)
                if c in (1, 3):
                    dst = kT[:, 0:2, cols] if c == 1 else kT[:, 2:3, cols]
                else:
                    dst = qT[:, (c // 2) % 2, :, cols]
                nc.scalar.activation(dst, bank[qk_bank(c, t)][:, 0:n * P].rearrange("p (j s) -> p j s", j=n), ACT.Copy)\
                    .then_inc(qk_ready, 1)

            def relu(l, i, h):
                n = 24 * l + 8 * i + h
                act.wait_ge(idx_scored, n + 1)
                if 8 * i + h >= P_RING:
                    act.wait_ge(idx_acc, n - P_RING + 1)
                else:
                    act.wait_ge(qk_transposed, at_chunk(l, 0, T - 1))
                w = (IDX_TILES[i] + 1) * P
                nc.scalar.activation(rel[:, (8 * i + h) % P_RING, 0:w], bank[4 + h % 4][:, 0:w], ACT.Relu)\
                    .then_inc(relu_done, 1)

            def exponential(l, u, h):
                lo, hi = keys_of(UNITS[u])
                n = 8 * u + h
                act.wait_ge(masked, at_head(l, u, h))
                p = prob[:, n % P_RING, 0:hi - lo]
                nc.scalar.activation(p, p, ACT.Exp, scale=-1.0, bias=nmax[:, u % 2, h:h + 1],
                                     accum_out=rowsum[:, u % 2, h:h + 1]).then_inc(probs, 1)

            def copy_p(l, u, h):
                lo, hi = keys_of(UNITS[u])
                act.wait_ge(p_transposed, at_head(l, u, h))
                if before := back(u, h, PT_RING):
                    act.wait_ge(av_done, at_head(l, *before))
                nc.scalar.activation(pT[:, h % PT_RING, 0:hi - lo], bank[6 + h % 2][:, 0:hi - lo], ACT.Copy)\
                    .then_inc(pT_act, 1)

            def sink_weight(l, u):
                act.wait_ge(sink_diff, 4 * l + u + 1)
                nc.scalar.activation(es[:, u % 2, :], es[:, u % 2, :], ACT.Exp).then_inc(sink_exp, 1)

            def split_y(l, u):
                kind, t = UNITS[u]
                act.wait_ge(y_scaled, at_unit(l, u))
                k0 = 0 if kind == "A" else 4
                nc.scalar.activation(hT_hi[:, k0:k0 + 4, t * P:(t + 1) * P],
                                     scratch[:, (u % 2) * 512:(u % 2 + 1) * 512].rearrange("p (k s) -> p k s", k=4),
                                     ACT.Copy).then_inc(yT_hi, 1)

            def attention(l):
                for i in range(64 + LAG_HI):
                    if i < 64:
                        exponential(l, i // 8, i % 8)
                        u, h = i // 8, i % 8
                        if h == 7 and UNITS[u][0] == "A":
                            sink_weight(l, u)
                    if 0 <= i - LAG_T < 64:
                        u, h = (i - LAG_T) // 8, (i - LAG_T) % 8
                        if not on_dve(u, h):
                            copy_p(l, u, h)
                    if i in QB_AT:
                        copy_qk(l, 4, QB_AT.index(i))
                    if (i - LAG_HI) % 8 == 7 and i > LAG_HI:
                        split_y(l, (i - LAG_HI) // 8)
                    if i == 40:
                        convert(l, WO_P + 2)
                    if i == 56:
                        convert(l, WO_P + 4)

            def feed(l, g):
                p0 = GU_P[g]
                f0 = gu_before(l, g)
                s0 = slot(l, p0)
                with act.Fori(0, FG[g] // 2) as i:
                    for f in range(2):
                        for j in (2 * f + 2, 2 * f + 3):
                            s = (s0 + j) % RING
                            act.wait_ge(raw_in[s], i * 16 + 16 * ((l * NP + p0 + j) // RING + 1))
                            act.wait_ge(piece_used, i * 4 + (l * NP + p0 + j + 1))
                            nc.scalar.activation(w_hi[:, s, :], w_raw[:, s, :], ACT.Copy).then_inc(hi_ready, 1)
                        act.wait_ge(piece_used, i * 4 + used(l, p0 + 2 * f))
                        nc.scalar.activation(silu_g[:, f, :], bank[GU_BANK[g] + 2 * f][:], ACT.Silu)\
                            .then_inc(gate_read, 1)
                        act.wait_ge(gu_ready, i * 2 + (f0 + f + 1 + 2))
                        nc.scalar.activation(gu_hi[:, bass.ds(i * 2 + f, 1), :], gu[:, f:f + 1, :], ACT.Copy)\
                            .then_inc(gu_hi_ready, 1)
                conv[0] += 4 * (FG[g] // 2)

            for dst, src in ((cc[:, 0, :], c_col), (modb[:], b_ada), (lnc[:], ln_col), (gcol[:], g_col)):
                act.dma_start(dst, src).then_inc(small_in, 16)
            act.dma_start(nsink[:], sinks.to_broadcast([P, DEPTH, HEADS])).then_inc(small_in, 16)
            act.dma_start(ada_acc[:, 1, 0:32], inv_freq.to_broadcast([P, 32])).then_inc(small_in, 16)
            act.dma_start(ada_acc[:, 1, 32:36].bitcast(I32), positions).then_inc(small_in, 16)
            act.wait_ge(small_in, 16 * 7)
            nc.scalar.activation(cc[:, 1, :], cc[:, 0, :], ACT.Silu).then_inc(rope_table, 1)
            nc.scalar.sem_inc(gate_read, 2)
            act.wait_ge(rope_angle, 1)
            nc.scalar.activation(scratch[:, 0:256], scratch[:, 0:256], ACT.Sin).then_inc(rope_table, 1)
            convert(0, RING)
            for t in range(T):
                build_h(0, t, 4)
            for l in range(DEPTH):
                for c in range(2):
                    convert(l, C0P[c + 1] + 2)
                    for t in range(T):
                        evacuate(l, c, t)
                    convert(l, C0P[c + 1] + 3)
                for t in range(T):
                    copy_qk(l, 0, t)
                for t in range(T):
                    copy_qk(l, 1, t)
                for i in range(len(IDX_TILES)):
                    for h in range(HEADS):
                        relu(l, i, h)
                convert(l, C0P[4] + 1)
                for t in range(T):
                    evacuate(l, 2, t)
                convert(l, C0P[4] + 2)
                for t in range(T):
                    evacuate(l, 3, t)
                convert(l, C0P[4] + 3)
                for t in range(T):
                    copy_qk(l, 2, t)
                for t in range(T):
                    copy_qk(l, 3, t)
                convert(l, C0P[4] + 4)
                for t in range(T):
                    evacuate(l, 4, t)
                attention(l)
                for t in range(T):
                    convert(l, WO_P + 4 + t + 1)
                for t in range(T):
                    if t == T - 1:
                        convert(l, GU_P[0] + 2)
                    build_h(2 * l + 1, t, 0)
                feed(l, 0)
                convert(l, DN_P[0] + 2)
                convert(l, GU_P[1] + 2)
                feed(l, 1)
                convert(l, NP)
                if l + 1 < DEPTH:
                    for t in range(T):
                        if t == T - 1:
                            convert(l + 1, 2)
                        build_h(2 * l + 2, t, 4)

        @block.vector
        def _(dve):
            steps = [0]
            conv = [0]
            ada = [0]

            def step(ins):
                steps[0] += 1
                ins.then_inc(dve_step, 1)
                dve.wait_ge(dve_step, steps[0])

            def convert(l, upto):
                while conv[0] < min(l * NP + upto, DEPTH * NP):
                    p = conv[0]
                    dve.wait_ge(hi_ready, p + 1)
                    nc.vector.tensor_tensor(w_lo[:, p % RING, :], w_raw[:, p % RING, :],
                                            w_hi[:, p % RING, :].bitcast(F32), ALU.subtract).then_inc(lo_ready, 1)
                    conv[0] += 1

            def ada_group(g, k0=0, k1=KD):
                for k in range(k0, k1):
                    n = g * KD + k
                    if k > 0:
                        dve.wait_ge(ada_used, n)
                    ada_piece(n, k, g)

            def ada_piece(n, k, g):
                dve.wait_ge(ada_in[n % RING], 16 * (n // RING + 1))
                if k == 0:
                    if g >= 2:
                        dve.wait_ge(mod_reduced, g - 1)
                    nc.vector.tensor_scalar(ada_acc[:, g % 2, :], ada_w[:, n % RING, :], cc[:, 1, 0:1], None,
                                            ALU.mult).then_inc(ada_used, 1)
                else:
                    nc.vector.scalar_tensor_tensor(out=ada_acc[:, g % 2, :], in0=ada_w[:, n % RING, :],
                                                   scalar=cc[:, 1, k:k + 1], in1=ada_acc[:, g % 2, :],
                                                   op0=ALU.mult, op1=ALU.add).then_inc(ada_used, 1)

            def take_mod(g, b):
                dve.wait_ge(mod_reduced, g + 1)
                nc.vector.tensor_tensor(mod[:, g, :], bank[b][:, 0:KD], modb[:, g, :], ALU.add)\
                    .then_inc(mod_taken, 1)
                dve.wait_ge(mod_taken, g + 1)

            def h_coefficients(stage):
                l, second = stage // 2, stage % 2
                sh, sc = mod[:, 6 * l + 3 * second, :], mod[:, 6 * l + 3 * second + 1, :]
                nc.vector.scalar_tensor_tensor(out=hcoef[:, stage, 0, :], in0=sc, scalar=1.0,
                                               in1=lnc[:, stage, 0, :], op0=ALU.add, op1=ALU.mult)
                step(nc.vector.scalar_tensor_tensor(out=hcoef[:, stage, 1, :], in0=sc, scalar=1.0,
                                                    in1=lnc[:, stage, 1, :], op0=ALU.add, op1=ALU.mult))
                nc.vector.tensor_tensor(hcoef[:, stage, 1, :], hcoef[:, stage, 1, :], sh, ALU.add)\
                    .then_inc(coef_ready, 1)
                dve.wait_ge(coef_ready, stage + 1)

            def gate_diagonal(l, which):
                g = 6 * l + (GT1, GT2)[which]
                if which == 0:
                    dve.wait_ge(yT_lo, at_unit(l, 7))
                else:
                    dve.wait_ge(h_lo, at_tile(2 * l + 1, T - 1))
                step(nc.vector.tensor_scalar(mod[:, g, :], mod[:, g, :], 1.0, None, ALU.add))
                nc.vector.tensor_tensor(scratch[:].rearrange("p (k s) -> p k s", k=KD),
                                        ident[:].unsqueeze(1).to_broadcast([P, KD, P]),
                                        mod[:, g, :].unsqueeze(2).to_broadcast([P, KD, P]), ALU.mult)\
                    .then_inc(gt_diag, 1)

            def take_gate(l, which, b):
                dve.wait_ge(gt_spread, 2 * l + which + 1)
                for half in range(2):
                    m = nc.vector.tensor_copy(gt_row[:, half * 512:(half + 1) * 512], bank[b + half][:])
                m.then_inc(gt_taken, 1)
                dve.wait_ge(gt_taken, 2 * l + which + 1)

            def build_h(stage, t, b0):
                dve.wait_ge(x_transposed, at_tile(stage, t))
                if stage > 0 or t > 0:
                    dve.wait_ge(h_hi, at_tile(stage, t) - 1)
                    dve.wait_ge(h_lo, at_tile(stage, t) - 1)
                for k in range(4):
                    m = nc.vector.tensor_scalar(scratch[:, k * P:(k + 1) * P],
                                                bank[b0 + 2 * (t % 2)][:, k * P:(k + 1) * P],
                                                hcoef[:, stage, 0, k:k + 1], hcoef[:, stage, 1, k:k + 1],
                                                ALU.mult, ALU.add)
                m.then_inc(h_scaled_dve, 1)
                dve.wait_ge(h_hi, at_tile(stage, t))
                cols = slice(t * P, (t + 1) * P)
                nc.vector.tensor_tensor(hT_lo[:, :, cols], scratch[:].rearrange("p (k s) -> p k s", k=KD),
                                        hT_hi[:, :, cols].bitcast(F32), ALU.subtract).then_inc(h_lo, 1)

            def rope(l, c, t):
                dve.wait_ge(proj_evac, at_chunk(l, c, t))
                if at_chunk(l, c, t) > 1:
                    dve.wait_ge(roped, at_chunk(l, c, t) - 1)
                heads = (8, 4, 8, 2, 8)[c]
                v = pk[:, t, 0:heads * HD] if c in (1, 3) else pq[:, (c // 2) % 2, t, :]
                v = v.rearrange("p (h d) -> p h d", h=heads)
                a = scratch[:, 0:heads * HD].rearrange("p (h d) -> p h d", h=heads)
                b = scratch[:, 512:512 + heads * HD].rearrange("p (h d) -> p h d", h=heads)
                n = HD // 2

                def over_heads(table, d0, d1):
                    return table[:, t, d0:d1].unsqueeze(1).to_broadcast([P, heads, d1 - d0])

                nc.vector.tensor_tensor(b[:, :, 0:n], v[:, :, n:HD], over_heads(sin_t, 0, n), ALU.mult)
                nc.vector.tensor_tensor(b[:, :, n:HD], v[:, :, 0:n], over_heads(sin_t, n, HD), ALU.mult)
                step(nc.vector.tensor_tensor(a, v, over_heads(cos_t, 0, HD), ALU.mult))
                nc.vector.tensor_tensor(v, a, b, ALU.add).then_inc(roped, 1)

            def add_index_head(l, i, h):
                t = IDX_TILES[i]
                w = (t + 1) * P
                n = 24 * l + 8 * i + h
                dve.wait_ge(relu_done, n + 1)
                part = rel[:, (8 * i + h) % P_RING, 0:w]
                sc = scores[:, SC_AT[t]:SC_AT[t] + w]
                wi = v_b[:, t, P + h:P + h + 1]
                if h == 0:
                    nc.vector.tensor_scalar(sc, part, wi, None, ALU.mult).then_inc(idx_acc, 1)
                else:
                    nc.vector.scalar_tensor_tensor(out=sc, in0=part, scalar=wi, in1=sc, op0=ALU.mult, op1=ALU.add)\
                        .then_inc(idx_acc, 1)
                dve.wait_ge(idx_acc, n + 1)
                if h == HEADS - 1:
                    own = scores[:, SC_AT[t] + t * P:SC_AT[t] + w]
                    step(nc.vector.tensor_tensor(own, own, band[:, P:2 * P], ALU.add))

            def top_rounds(r0, r1):
                for r in range(r0, r1):
                    for t in IDX_TILES:
                        sc = scores[:, SC_AT[t]:SC_AT[t] + (t + 1) * P]
                        steps[0] += 1
                        if r > 0:
                            dve.wait_ge(dve_step, steps[0] - 3)
                        nc.vector.max(top8[:, t, :], sc).then_inc(dve_step, 1)
                    for t in IDX_TILES:
                        sc = scores[:, SC_AT[t]:SC_AT[t] + (t + 1) * P]
                        steps[0] += 1
                        dve.wait_ge(dve_step, steps[0] - 3)
                        nc.vector.match_replace(out=sc, in_to_replace=top8[:, t, :], in_values=sc, imm_value=TAKEN)\
                            .then_inc(dve_step, 1)

            def top_masks():
                dve.wait_ge(dve_step, steps[0])
                nc.vector.tensor_copy(scores[:, 0:P], band[:, P:2 * P])
                step(nc.vector.tensor_scalar(scores[:, P:SC_W], scores[:, P:SC_W], CUT, NEG, ALU.is_gt, ALU.mult))

            def mask_scores(l, u, h):
                kind, t = UNITS[u]
                lo, hi = keys_of(UNITS[u])
                n = 8 * u + h
                dve.wait_ge(scored, at_head(l, u, h))
                if n >= P_RING:
                    dve.wait_ge(p_transposed, at_head(l, u, h) - P_RING)
                else:
                    dve.wait_ge(qk_transposed, at_chunk(l, 2, T - 1))
                if h == 0 and u >= 2:
                    dve.wait_ge(probs, at_head(l, u - 2, 7))
                if kind == "A":
                    mask = band[:] if t > 0 else band[:, P:2 * P]
                    start = nsink[:, l, h:h + 1]
                else:
                    mask = scores[:, SC_AT[t]:SC_AT[t] + hi - lo]
                    start = 3.0e38
                nc.vector.tensor_tensor_reduce(out=prob[:, n % P_RING, 0:hi - lo], in0=bank[S_BANKS[n % 3]][:, 0:hi - lo],
                                               in1=mask, scale=-(HD ** -0.5), scalar=start, op0=ALU.add,
                                               op1=ALU.min, accum_out=nmax[:, u % 2, h:h + 1]).then_inc(masked, 1)

            def copy_p(l, u, h):
                lo, hi = keys_of(UNITS[u])
                dve.wait_ge(p_transposed, at_head(l, u, h))
                if before := back(u, h, PT_RING):
                    dve.wait_ge(av_done, at_head(l, *before))
                nc.vector.tensor_copy(pT[:, h % PT_RING, 0:hi - lo], bank[6 + h % 2][:, 0:hi - lo]).then_inc(pT_dve, 1)

            def sink_difference(l, u):
                dve.wait_ge(masked, at_head(l, u, 7))
                nc.vector.tensor_tensor(es[:, u % 2, :], nmax[:, u % 2, :], nsink[:, l, :], ALU.subtract)\
                    .then_inc(sink_diff, 1)

            def norm_y(l, u):
                kind, t = UNITS[u]
                b = u % 2
                dve.wait_ge(probs, at_head(l, u, 7))
                total = rowsum[:, b, :]
                if kind == "A":
                    dve.wait_ge(sink_exp, 4 * l + u + 1)
                    step(nc.vector.tensor_tensor(es[:, b, :], rowsum[:, b, :], es[:, b, :], ALU.add))
                    total = es[:, b, :]
                step(nc.vector.reciprocal(recip[:, b, :], total))
                dve.wait_ge(av_done, at_head(l, u, 7))
                if u >= 2:
                    dve.wait_ge(y_transposed, at_unit(l, u - 2))
                step(nc.vector.tensor_tensor(y[:, b, :].rearrange("p (h d) -> p h d", h=HEADS),
                                             bank[b][:].rearrange("p (h d) -> p h d", h=HEADS),
                                             recip[:, b, :].unsqueeze(2).to_broadcast([P, HEADS, HD]), ALU.mult))
                if u >= 2:
                    dve.wait_ge(yT_hi, at_unit(l, u - 2))
                    dve.wait_ge(yT_lo, at_unit(l, u - 2))
                else:
                    dve.wait_ge(roped, at_chunk(l, 4, T - 1))
                n = rs_index(l, u)
                step(nc.vector.tensor_tensor_reduce(out=scratch[:, b * 512:(b + 1) * 512], in0=y[:, b, :],
                                                    in1=y[:, b, :], scale=1.0, scalar=0.0, op0=ALU.mult,
                                                    op1=ALU.add, accum_out=mean_var[:, 0, 0:1]))
                nc.vector.tensor_scalar(rs_in[:, n:n + 1], mean_var[:, 0, 0:1], 1.0 / 512, RMS_EPS, ALU.mult,
                                        ALU.add).then_inc(rs_asked, 1)

            def scale_y(l, u):
                n = rs_index(l, u)
                dve.wait_ge(rs_done, n + 1)
                nc.vector.tensor_scalar(y[:, u % 2, :], y[:, u % 2, :], rs_out[:, n:n + 1], None, ALU.mult)\
                    .then_inc(y_ready, 1)

            def gain_y(l, u):
                kind, _ = UNITS[u]
                g = gcol[:, l, 0 if kind == "A" else 1, :]
                dve.wait_ge(y_transposed, at_unit(l, u))
                dst = scratch[:, (u % 2) * 512:(u % 2 + 1) * 512].rearrange("p (k s) -> p k s", k=4)
                nc.vector.tensor_tensor(dst, bank[2][:].rearrange("p (k s) -> p k s", k=4),
                                        g.unsqueeze(2).to_broadcast([P, 4, P]), ALU.mult).then_inc(y_scaled, 1)

            def split_y(l, u):
                kind, t = UNITS[u]
                k0 = 0 if kind == "A" else 4
                dve.wait_ge(yT_hi, at_unit(l, u))
                cols = slice(t * P, (t + 1) * P)
                nc.vector.tensor_tensor(hT_lo[:, k0:k0 + 4, cols],
                                        scratch[:, (u % 2) * 512:(u % 2 + 1) * 512]
                                        .rearrange("p (k s) -> p k s", k=4),
                                        hT_hi[:, k0:k0 + 4, cols].bitcast(F32), ALU.subtract).then_inc(yT_lo, 1)

            def residual(l, q, t, first):
                half = (q - WO0) % 2
                cols = slice(half * HALF, (half + 1) * HALF)
                wait_phase(dve, l, q, t)
                nc.vector.tensor_tensor(ztmp[:], bank[BANKS[q] + t][:], gt_row[:, cols], ALU.mult)\
                    .then_inc(z_done, 1)
                dve.wait_ge(z_done, at_z(l, q, t))
                step(nc.vector.scalar_tensor_tensor(out=xs[:, t, cols], in0=xs[:, t, cols],
                                                    scalar=ALPHA if first else 1.0, in1=ztmp[:],
                                                    op0=ALU.mult, op1=ALU.add))
                if q in (WO0, WO1, DN10, DN11):
                    steps[0] += 1
                    nc.vector.bn_stats(stats[:, t, half, :], xs[:, t, cols]).then_inc(dve_step, 1)

            def layer_norm(l, second, t):
                r = rs_index(l, 8 + 4 * second + t)
                stage = 2 * l + 1 + second
                dve.wait_ge(dve_step, steps[0])
                step(nc.vector.bn_aggr(mean_var[:, t, :], stats[:, t, :, :]))
                nc.vector.tensor_scalar(rs_in[:, r:r + 1], mean_var[:, t, 1:2], LN_EPS, None, ALU.add)\
                    .then_inc(rs_asked, 1)
                dve.wait_ge(rs_done, r + 1)
                nc.vector.tensor_scalar(xs[:, t, :], xs[:, t, :], mean_var[:, t, 0:1], rs_out[:, r:r + 1],
                                        ALU.subtract, ALU.mult).then_inc(xhat_ready, 1)

            def affine(stage, t):
                dve.wait_ge(row_in, 32 * stage)
                if stage < 2 * DEPTH:
                    dve.wait_ge(x_transposed, at_tile(stage, t))
                else:
                    dve.wait_ge(xhat_ready, at_tile(stage - 1, t))
                step(nc.vector.tensor_tensor(xs[:, t, :], xs[:, t, :], g_row[:], ALU.mult))
                nc.vector.tensor_tensor(xs[:, t, :], xs[:, t, :], b_row[:], ALU.add).then_inc(affine_done, 1)
                dve.wait_ge(affine_done, at_tile(stage - 1, t))

            def rope_tables():
                two_pi = 2.0 * np.pi
                c1 = np.float32(np.round(two_pi * 2 ** 8) / 2 ** 8)
                c2 = np.float32(np.round((two_pi - float(c1)) * 2 ** 20) / 2 ** 20)
                c3 = np.float32(two_pi - float(c1) - float(c2))
                magic = 1.5 * 2 ** 23
                pos_f = top8[:, 0, 0:T]
                step(nc.vector.tensor_copy(pos_f, ada_acc[:, 1, 32:36].bitcast(I32)))
                ang = ada_acc[:, 1, 64:192]
                for t in range(T):
                    m = nc.vector.tensor_scalar(ang[:, t * 32:(t + 1) * 32], ada_acc[:, 1, 0:32],
                                                pos_f[:, t:t + 1], None, ALU.mult)
                step(m)
                turns = ada_acc[:, 1, 192:448]
                nc.vector.tensor_scalar(turns[:, 0:128], ang, 1.0 / two_pi, None, ALU.mult)
                step(nc.vector.tensor_scalar(turns[:, 128:256], ang, 1.0 / two_pi, 0.25, ALU.mult, ALU.add))
                step(nc.vector.tensor_scalar(turns, turns, magic, None, ALU.add))
                step(nc.vector.tensor_scalar(turns, turns, -magic, None, ALU.add))
                r = scratch[:, 0:256]
                for i in range(2):
                    m = nc.vector.scalar_tensor_tensor(out=r[:, i * 128:(i + 1) * 128],
                                                       in0=turns[:, i * 128:(i + 1) * 128], scalar=-float(c1),
                                                       in1=ang, op0=ALU.mult, op1=ALU.add)
                step(m)
                for c in (c2, c3):
                    step(nc.vector.scalar_tensor_tensor(out=r, in0=turns, scalar=-float(c), in1=r,
                                                        op0=ALU.mult, op1=ALU.add))
                step(nc.vector.tensor_scalar(r[:, 128:256], r[:, 128:256], float(np.float32(np.pi / 2)), None,
                                             ALU.add))
                pi = float(np.nextafter(np.float32(np.pi), np.float32(0)))
                nc.vector.tensor_scalar(r, r, pi, -pi, ALU.min, ALU.max).then_inc(rope_angle, 1)

            def rope_signs():
                dve.wait_ge(rope_table, 2)
                s = scratch[:, 0:128].rearrange("p (t d) -> p t d", t=T)
                c = scratch[:, 128:256].rearrange("p (t d) -> p t d", t=T)
                nc.vector.tensor_scalar(sin_t[:, :, 0:32], s, -1.0, None, ALU.mult)
                nc.vector.tensor_copy(sin_t[:, :, 32:64], s)
                nc.vector.tensor_copy(cos_t[:, :, 0:32], c)
                step(nc.vector.tensor_copy(cos_t[:, :, 32:64], c))

            def attention(l):
                rounds = TOPK // 8
                done = [9]

                def rounds_to(n):
                    top_rounds(done[0], n)
                    done[0] = n

                for i in range(64 + LAG_LO):
                    if i < 64:
                        u, h = i // 8, i % 8
                        if i == 32:
                            rounds_to(rounds)
                            top_masks()
                        mask_scores(l, u, h)
                        if h == 7 and UNITS[u][0] == "A":
                            sink_difference(l, u)
                        if i % 4 == 3 and 8 <= i < 32:
                            rounds_to(9 + (i - 3) // 4)
                    if 0 <= i - LAG_T < 64:
                        u, h = (i - LAG_T) // 8, (i - LAG_T) % 8
                        if on_dve(u, h):
                            copy_p(l, u, h)
                    if i in ROPE_AT:
                        rope(l, 4, ROPE_AT.index(i))
                    for lag, part in ((LAG_NORM, norm_y), (LAG_SCALE, scale_y), (LAG_GAIN, gain_y),
                                      (LAG_LO, split_y)):
                        if (i - lag) % 8 == 7 and i > lag:
                            part(l, (i - lag) // 8)
                    if i == 40:
                        convert(l, WO_P + 2)
                    if i == 56:
                        convert(l, WO_P + 4)

            def feed(l, g):
                p0 = GU_P[g]
                f0 = gu_before(l, g)
                s0 = slot(l, p0)
                with_ada = (l, g) == (0, 0)
                with dve.Fori(0, FG[g] // 2) as i:
                    for f in range(2):
                        for j in (2 * f + 2, 2 * f + 3):
                            s = (s0 + j) % RING
                            dve.wait_ge(hi_ready, i * 4 + converted(l, p0 + j))
                            nc.vector.tensor_tensor(w_lo[:, s, :], w_raw[:, s, :], w_hi[:, s, :].bitcast(F32),
                                                    ALU.subtract).then_inc(lo_ready, 1)
                        if with_ada:
                            for k in range(4 * f, 4 * f + 4):
                                n = 5 * KD + k
                                dve.wait_ge(ada_in[n % RING], i * (16 * KD // RING) + 16 * (n // RING + 1))
                                if k == 0:
                                    m = nc.vector.tensor_scalar(ada_acc[:, 1, :], ada_w[:, n % RING, :],
                                                                cc[:, 1, 0:1], None, ALU.mult)
                                else:
                                    dve.wait_ge(ada_used, i * KD + n)
                                    m = nc.vector.scalar_tensor_tensor(
                                        out=ada_acc[:, 1, :], in0=ada_w[:, n % RING, :], scalar=cc[:, 1, k:k + 1],
                                        in1=ada_acc[:, 1, :], op0=ALU.mult, op1=ALU.add)
                                m.then_inc(ada_used, 1)
                        dve.wait_ge(piece_used, i * 4 + used(l, p0 + 2 * f + 1))
                        dve.wait_ge(gate_read, i * 2 + (f0 + f + 1 + 2))
                        nc.vector.tensor_tensor(gu[:, f, :], bank[GU_BANK[g] + 2 * f + 1][:], silu_g[:, f, :],
                                                ALU.mult).then_inc(gu_ready, 1)
                        dve.wait_ge(gu_hi_ready, i * 2 + (f0 + f + 1))
                        at = bass.ds(i * 2 + f, 1)
                        nc.vector.tensor_tensor(gu_lo[:, at, :], gu[:, f:f + 1, :],
                                                gu_hi[:, at, :].bitcast(F32), ALU.subtract).then_inc(gu_lo_ready, 1)
                        dve.wait_ge(gu_lo_ready, i * 2 + (f0 + f + 1))
                    if with_ada:
                        dve.wait_ge(mod_reduced, i + 6)
                        nc.vector.tensor_tensor(mod[:, bass.ds(i + 5, 1), :],
                                                bank[0][:, 0:KD].unsqueeze(1),
                                                modb[:, bass.ds(i + 5, 1), :], ALU.add).then_inc(mod_taken, 1)
                if with_ada:
                    dve.wait_ge(mod_taken, 5 + FG[0] // 2)
                conv[0] += 4 * (FG[g] // 2)

            nc.vector.sem_inc(gu_ready, 2)
            dve.wait_ge(consts, 4)
            dve.wait_ge(rope_table, 1)
            dve.wait_ge(small_in, 16 * 7)
            rope_tables()
            step(nc.vector.tensor_scalar(nsink[:], nsink[:], -1.0, None, ALU.mult))
            ada_group(0)
            rope_signs()
            ada_group(1)
            take_mod(0, 0)
            take_mod(1, 1)
            h_coefficients(0)
            convert(0, 1)
            for t in range(T):
                build_h(0, t, 4)
                convert(0, min(2 + t, RING))
            for l in range(DEPTH):
                convert(l, 4)
                if l == 0:
                    ada_group(2, 0, 4)
                    convert(l, 5)
                    ada_group(2, 4, KD)
                else:
                    for t in range(T):
                        affine(2 * l, t)
                        convert(l, 4 + min(t, 1))
                convert(l, C0P[1] + 2)
                for t in range(T):
                    rope(l, 0, t)
                    convert(l, C0P[1] + 3)
                convert(l, C0P[2])
                if l == 0:
                    ada_group(3, 0, 4)
                convert(l, C0P[2] + 2)
                for t in range(T):
                    rope(l, 1, t)
                convert(l, C0P[2] + 3)
                for i in range(len(IDX_TILES)):
                    for h in range(HEADS):
                        add_index_head(l, i, h)
                if l == 0:
                    ada_group(3, 4, KD)
                convert(l, C0P[3])
                top_rounds(0, 1)
                convert(l, C0P[3] + 1)
                top_rounds(1, 2)
                convert(l, C0P[4] + 1)
                for t in range(T):
                    rope(l, 2, t)
                convert(l, C0P[4] + 2)
                for t in range(T):
                    rope(l, 3, t)
                convert(l, C0P[4] + 3)
                top_rounds(2, 4)
                convert(l, C0P[4] + 4)
                top_rounds(4, 9)
                attention(l)
                if l == 0:
                    take_mod(2, 7)
                    take_mod(3, 4)
                gate_diagonal(l, 0)
                take_gate(l, 0, 5)
                convert(l, WO_P + 5)
                if l == 0:
                    ada_group(4, 0, 4)
                    convert(l, WO_P + 6)
                    ada_group(4, 4, KD)
                convert(l, WO_P + 7)
                for t in range(T):
                    residual(l, WO0, t, True)
                convert(l, WO_P + 8)
                if l == 0:
                    take_mod(4, 7)
                if l == 0:
                    h_coefficients(1)
                else:
                    h_coefficients(3)
                for t in range(T):
                    residual(l, WO1, t, True)
                    layer_norm(l, 0, t)
                    if t >= 2:
                        build_h(2 * l + 1, t - 2, 0)
                build_h(2 * l + 1, 2, 0)
                convert(l, GU_P[0] + 1)
                build_h(2 * l + 1, 3, 0)
                convert(l, GU_P[0] + 2)
                feed(l, 0)
                if l == 0:
                    h_coefficients(2)
                gate_diagonal(l, 1)
                take_gate(l, 1, 2)
                for t in range(T):
                    affine(2 * l + 1, t)
                    convert(l, DN_P[0] + 3 + t)
                for half in range(2):
                    q = DN00 + half
                    convert(l, PHASES[q][0] + PHASES[q][1] + (3, 2)[half])
                    for t in range(T):
                        residual(l, q, t, True)
                    if (l, half) == (0, 0):
                        ada_group(6 * DEPTH - 1)
                convert(l, GU_P[1] + 2)
                feed(l, 1)
                if l == 0:
                    take_mod(6 * DEPTH - 1, 7)
                convert(l, DN_P[1] + 5)
                for t in range(T):
                    convert(l, DN_P[1] + 5 + t)
                    residual(l, DN10, t, False)
                convert(l, NP)
                for t in range(T):
                    residual(l, DN11, t, False)
                    layer_norm(l, 1, t)
                    if l + 1 < DEPTH:
                        if t >= 2:
                            build_h(2 * l + 2, t - 2, 4)
                    else:
                        affine(2 * DEPTH, t)
                if l + 1 < DEPTH:
                    build_h(2 * l + 2, 2, 4)
                    convert(l + 1, 1)
                    build_h(2 * l + 2, 3, 4)
                    convert(l + 1, 2)


def weight_pieces(w_in, w_o, w_gate, w_up, w_down):
    a_q, a_k, a_v, b_q, b_k, b_v, i_q, i_k, i_w = np.split(
        w_in, np.cumsum([512, 128, 128, 512, 128, 128, 512, 64]), axis=-1)
    chunks = [i_q, np.concatenate([i_k, b_k, b_v, i_w], -1), paired(a_q, -1),
              np.concatenate([a_k, a_v], -1), paired(b_q, -1)]
    out = np.zeros((DEPTH, NP, P, PW), np.float32)
    w_o = np.concatenate([paired(w_o[:, :512], 1), paired(w_o[:, 512:], 1)], 1)
    for c, w in enumerate(chunks):
        for j in range(CP[c]):
            for kk in range(CK[c]):
                k = j * CK[c] + kk
                out[:, C0P[c] + j, :, kk * CW[c]:(kk + 1) * CW[c]] = w[:, k * P:(k + 1) * P]
    for half in range(2):
        cols = slice(half * HALF, (half + 1) * HALF)
        for k in range(KD):
            out[:, WO_P + 4 * half + k // 2, :, (k % 2) * 512:(k % 2 + 1) * 512] = w_o[:, k * P:(k + 1) * P, cols]
    f0 = 0
    for g in range(2):
        for f in range(FG[g]):
            cols = slice((f0 + f) * P, (f0 + f + 1) * P)
            for i, w in enumerate((w_gate, w_up)):
                out[:, GU_P[g] + 2 * f + i] = w[:, :, cols].reshape(DEPTH, KD, P, P).transpose(0, 2, 1, 3)\
                    .reshape(DEPTH, P, PW)
            for half in range(2):
                out[:, DN_P[g] + half * FG[g] // 2 + f // 2, :, (f % 2) * 512:(f % 2 + 1) * 512] = \
                    w_down[:, cols, half * HALF:(half + 1) * HALF]
        f0 += FG[g]
    return out.reshape(DEPTH * NP, P, PW)


def paired(a, axis):
    axis = axis % a.ndim
    n = a.shape[axis] // HEADS
    s = a.shape
    b = a.reshape(s[:axis] + (KV_HEADS, PAIRS, n) + s[axis + 1:])
    return np.swapaxes(b, axis, axis + 1).reshape(s)


def kernel(x, c, positions, w_ada, b_ada, w_in, attn_sinks, g_a, g_b, w_o,
           ln1_g, ln1_b, w_gate, w_up, w_down, ln2_g, ln2_b):
    import concourse.bacc as bacc
    from concourse.bass_utils import run_bass_kernel_spmd

    def columns(a):
        a = np.asarray(a)
        return np.ascontiguousarray(np.moveaxis(a.reshape(a.shape[:-1] + (-1, P)), -1, 0))

    (x, c, positions, w_ada, b_ada, w_in, attn_sinks, g_a, g_b, w_o, ln1_g, ln1_b, w_gate, w_up, w_down,
     ln2_g, ln2_b) = map(np.asarray, (x, c, positions, w_ada, b_ada, w_in, attn_sinks, g_a, g_b, w_o, ln1_g,
                                      ln1_b, w_gate, w_up, w_down, ln2_g, ln2_b))
    one, zero = np.ones((D_MODEL,), np.float32), np.zeros((D_MODEL,), np.float32)
    rows = np.stack([np.stack([g, b]) for l in range(DEPTH)
                     for g, b in ((ln1_g[l], ln1_b[l]), (ln2_g[l], ln2_b[l]))])
    before = np.concatenate([np.stack([one, zero])[None], rows[:-1]])
    arrays = {
        "x": x.reshape(T, P, D_MODEL),
        "c_col": columns(c[0]),
        "positions": positions.reshape(T, P).T,
        "inv_freq": (ROPE_THETA ** (-np.arange(HD // 2) / (HD // 2))).astype(np.float32)[None],
        "weights": weight_pieces(w_in, w_o, w_gate, w_up, w_down),
        "w_ada": w_ada.reshape(DEPTH, KD, P, 6, PW).transpose(0, 3, 1, 2, 4).reshape(6 * DEPTH, KD, P, PW),
        "b_ada": columns(b_ada.reshape(6 * DEPTH, D_MODEL)),
        "ln_col": columns(before),
        "ln_row": rows,
        "sinks": paired(attn_sinks, 1)[None],
        "g_col": columns(np.stack([paired(g_a, 1), paired(g_b, 1)], 1)),
    }
    nc = bacc.Bacc("TRN2", target_bir_lowering=False, num_devices=1)
    ins, aps = {}, {}
    for name, a in arrays.items():
        a = np.ascontiguousarray(a)
        ins[f"in_{name}"] = a
        aps[name] = nc.dram_tensor(f"in_{name}", a.shape, mybir.dt.from_np(a.dtype), kind="ExternalInput").ap()
    out = nc.dram_tensor("trunk_out", (T, P, D_MODEL), F32, kind="ExternalOutput").ap()
    build_trunk(nc, out=out, **aps)
    r = run_bass_kernel_spmd(nc, [ins], core_ids=[0])
    return r.results[0]["trunk_out"].reshape(1, SEQ, D_MODEL)
```

```python
from contextlib import ExitStack

import numpy as np

import concourse.bass as bass
from concourse import mybir

F32 = mybir.dt.float32
F32R = mybir.dt.float32r
I32 = mybir.dt.int32
ALU = mybir.AluOpType
ACT = mybir.ActivationFunctionType

P = 128
D_MODEL, SEQ, DEPTH = 1024, 512, 2
HD = 64
HEADS = 8
KV_HEADS = 2
PAIRS = HEADS // KV_HEADS
TOPK = min(256, SEQ // 4)
D_FF = ((-(-8 * D_MODEL // 3)) + 255) // 256 * 256
ALPHA = (2.0 * DEPTH) ** 0.25
LN_EPS, RMS_EPS = 1e-5, 1e-6
ROPE_THETA = 10000.0

T = SEQ // P
KD = D_MODEL // P
HALF = D_MODEL // 2
FC = D_FF // P
FG = (12, FC - 12)
PW = 1024

CW = (512, 328, 512, 256, 512)
CK = (2, 2, 2, 4, 2)
CP = tuple(KD // k for k in CK)
C0P = tuple(sum(CP[:c]) for c in range(5))
WO_P = sum(CP)
GU_P = (WO_P + 8, WO_P + 8 + 2 * FG[0] + FG[0])
DN_P = (GU_P[0] + 2 * FG[0], GU_P[1] + 2 * FG[1])
NP = DN_P[1] + FG[1]
RING = 4
assert NP % RING == 0 and NP == 92 and D_MODEL == 1024 and SEQ == 512

PHASES = [(C0P[c], CP[c]) for c in range(5)] + [(WO_P, 4), (WO_P + 4, 4)]
for _g in range(2):
    PHASES += [(DN_P[_g], FG[_g] // 2), (DN_P[_g] + FG[_g] // 2, FG[_g] // 2)]
WO0, WO1, DN00, DN01, DN10, DN11 = range(5, 11)
BANKS = {0: 0, 1: 4, 2: 0, 3: 0, 4: 0, WO0: 0, WO1: 4, DN00: 0, DN01: 4, DN10: 4, DN11: 0}
GU_BANK = (4, 0)

UNITS = [("A", t) for t in range(T)] + [("B", 0), ("B", 3), ("B", 2), ("B", 1)]
IDX_TILES = (3, 2, 1)
SC_AT = (0, 128, 384, 768)
SC_W = 1280
P_RING = 4
S_BANKS = (3, 4, 5)
PT_RING = 4
DVE_HEADS = (3, 7)
LAG_T, LAG_V = 3, 5
ROPE_AT, QB_AT = (1, 3, 5, 7), (5, 7, 9, 11)
LAG_NORM, LAG_SCALE, LAG_Y, LAG_GAIN, LAG_HI, LAG_LO = 6, 7, 9, 10, 11, 12

SH1, SC1, GT1, SH2, SC2, GT2 = range(6)

TAKEN = -3.3e38
CUT = -3.1e38
NEG = -1.0e38


def keys_of(unit):
    kind, t = unit
    lo = max(t - 1, 0) * P if kind == "A" else 0
    return lo, (t + 1) * P


def build_trunk(nc, x, c_col, positions, inv_freq, weights, w_ada, b_ada, ln_col, ln_row, sinks, g_col, out):
    with ExitStack() as ctx:
        def sb(name, shape, dt=F32, on=ctx):
            return on.enter_context(nc.sbuf_tensor(name, shape, dt))

        def sem(name):
            return ctx.enter_context(nc.semaphore(name))

        bank = [ctx.enter_context(nc.psum_tensor(f"bank{i}", [P, 512], F32)) for i in range(8)]

        w_raw = sb("w_raw", [P, RING, PW])
        w_hi = sb("w_hi", [P, RING, PW], F32R)
        w_lo = sb("w_lo", [P, RING, PW], F32R)
        xs = sb("xs", [P, T, D_MODEL])
        hT_hi = sb("hT_hi", [P, KD, SEQ], F32R)
        hT_lo = sb("hT_lo", [P, KD, SEQ], F32R)
        scratch = sb("scratch", [P, PW])
        ada_w = sb("ada_w", [P, RING, PW])
        ada_acc = sb("ada_acc", [P, 2, PW])
        gt_row = sb("gt_row", [P, D_MODEL])
        g_row = sb("g_row", [P, D_MODEL])
        b_row = sb("b_row", [P, D_MODEL])
        ident = sb("ident", [P, P])
        ones = sb("ones", [P, P])
        band = sb("band", [P, 2 * P])
        cos_t = sb("cos_t", [P, T, HD])
        sin_t = sb("sin_t", [P, T, HD])
        cc = sb("cc", [P, 2, KD])
        modb = sb("modb", [P, 6 * DEPTH, KD])
        mod = sb("mod", [P, 6 * DEPTH, KD])
        lnc = sb("lnc", [P, 2 * DEPTH, 2, KD])
        hcoef = sb("hcoef", [P, 2 * DEPTH, 2, KD])
        gcol = sb("gcol", [P, DEPTH, 2, 4])
        nsink = sb("nsink", [P, DEPTH, HEADS])
        stats = sb("stats", [P, T, 2, 6])
        mean_var = sb("mean_var", [P, T, 2])
        rs_in = sb("rs_in", [P, 32])
        rs_out = sb("rs_out", [P, 32])
        minus_half = sb("minus_half", [P, 1])
        rowsum = sb("rowsum", [P, 2, HEADS])
        nmax = sb("nmax", [P, 2, HEADS])
        es = sb("es", [P, 2, HEADS])
        recip = sb("recip", [P, 2, HEADS])
        top8 = sb("top8", [P, T, 8])

        with ExitStack() as att:
            pq = sb("pq", [P, 2, T, 512], on=att)
            pk = sb("pk", [P, T, 256], on=att)
            v_b = sb("v_b", [P, T, P + HEADS], on=att)
            v_a = sb("v_a", [P, T, P], on=att)
            qT = sb("qT", [P, 2, PAIRS, SEQ], on=att)
            kT = sb("kT", [P, 3, SEQ], on=att)
            scores = sb("scores", [P, SC_W], on=att)
            pT = sb("pT", [P, PT_RING, 512], on=att)
            y = sb("y", [P, 2, 512], on=att)
        rel = pq[:, 0]
        prob = pq[:, 1]
        angles = pq[:, 1, 0:2]
        with ExitStack() as ffn:
            gu_hi = sb("gu_hi", [P, FG[0], SEQ], F32R, on=ffn)
            gu_lo = sb("gu_lo", [P, FG[0], SEQ], F32R, on=ffn)
            silu_g = sb("silu_g", [P, 2, SEQ], on=ffn)
            gu = sb("gu", [P, 2, SEQ], on=ffn)
            ztmp = sb("ztmp", [P, HALF], on=ffn)

        raw_in = [sem(f"raw_in{i}") for i in range(RING)]
        ada_first_in = [sem(f"ada_first_in{i}") for i in range(RING)]
        ada_in = [sem(f"ada_in{i}") for i in range(RING)]
        x_in = [sem(f"x_in{i}") for i in range(T)]
        small_in = sem("small_in")
        row_in = sem("row_in")
        c_in = sem("c_in")
        out_ready = sem("out_ready")
        out_done = sem("out_done")
        consts = sem("consts")
        pool_step = sem("pool_step")
        hi_ready = sem("hi_ready")
        lo_ready = sem("lo_ready")
        piece_used = sem("piece_used")
        tile_done = sem("tile_done")
        x_transposed = sem("x_transposed")
        coef_ready = sem("coef_ready")
        h_scaled_dve = sem("h_scaled_dve")
        h_scaled_act = sem("h_scaled_act")
        h_hi = sem("h_hi")
        h_lo = sem("h_lo")
        proj_evac = sem("proj_evac")
        roped = sem("roped")
        qk_transposed = sem("qk_transposed")
        qk_ready = sem("qk_ready")
        idx_scored = sem("idx_scored")
        relu_done = sem("relu_done")
        idx_acc = sem("idx_acc")
        scored = sem("scored")
        masked = sem("masked")
        probs = sem("probs")
        sink_diff = sem("sink_diff")
        sink_exp = sem("sink_exp")
        p_transposed = sem("p_transposed")
        pT_act = sem("pT_act")
        pT_dve = sem("pT_dve")
        av_done = sem("av_done")
        rs_asked = sem("rs_asked")
        rs_done = sem("rs_done")
        y_ready = sem("y_ready")
        y_transposed = sem("y_transposed")
        y_scaled = sem("y_scaled")
        yT_hi = sem("yT_hi")
        yT_lo = sem("yT_lo")
        z_done = sem("z_done")
        xhat_ready = sem("xhat_ready")
        affine_done = sem("affine_done")
        gate_read = sem("gate_read")
        gu_ready = sem("gu_ready")
        gu_hi_ready = sem("gu_hi_ready")
        gu_lo_ready = sem("gu_lo_ready")
        ada_used = sem("ada_used")
        mod_taken = sem("mod_taken")
        mod_reduced = sem("mod_reduced")
        gt_diag = sem("gt_diag")
        gt_spread = sem("gt_spread")
        gt_taken = sem("gt_taken")
        dve_step = sem("dve_step")
        rope_angle = sem("rope_angle")
        rope_table = sem("rope_table")

        def converted(l, p):
            return l * NP + p + 1

        def used(l, p):
            return RING + l * NP + p + 1

        def slot(l, p):
            return (l * NP + p) % RING

        def wait_phase(eng, l, q, t):
            if t < T - 1:
                eng.wait_ge(tile_done, l * 33 + 3 * q + t + 1)
            else:
                eng.wait_ge(piece_used, used(l, PHASES[q][0] + PHASES[q][1] - 1))

        def dve_chunks(stage, t):
            return 0 if stage > 0 and t < 2 else 4

        def scaled_dve(stage, t):
            return t + 1 if stage == 0 else T + 2 * (stage - 1) + max(t - 1, 0)

        def at_tile(stage, t):
            return T * stage + t + 1

        def at_chunk(l, c, t):
            return 20 * l + 4 * c + t + 1

        def at_head(l, u, h):
            return 64 * l + 8 * u + h + 1

        def at_unit(l, u):
            return 8 * l + u + 1

        def at_z(l, q, t):
            return 24 * l + 4 * (q - WO0) + t + 1

        def rs_index(l, r):
            return 16 * l + r

        def qk_bank(c, t):
            return 2 if c == 4 else 4 + t

        def gu_before(l, g):
            return l * FC + g * FG[0]

        def on_dve(u, h):
            return u >= 4 and h in DVE_HEADS

        dve_heads = 4 * len(DVE_HEADS)

        def wait_pT(eng, l, u, h):
            flat = [(a, b) for a in range(8) for b in range(HEADS) if (a, b) <= (u, h)]
            n_dve = sum(on_dve(a, b) for a, b in flat)
            if on_dve(u, h):
                eng.wait_ge(pT_dve, l * dve_heads + n_dve)
            else:
                eng.wait_ge(pT_act, l * (64 - dve_heads) + len(flat) - n_dve)

        def back(u, h, n):
            i = 8 * u + h - n
            return None if i < 0 else (i // 8, i % 8)

        NSMALL = 8
        block = ctx.enter_context(nc.Block())

        @block.sync
        def _(sp):
            for n in range(2 * KD):
                if n >= RING:
                    sp.wait_ge(ada_used, n - RING + 1)
                sp.dma_start(ada_w[:, n % RING, :], w_ada[n // KD, n % KD]).then_inc(ada_first_in[n % RING], 16)
            for t in range(T):
                sp.dma_start(xs[:, t, :], x[t]).then_inc(x_in[t], 16)
            for s in range(RING):
                sp.dma_start(w_raw[:, s, :], weights[s]).then_inc(raw_in[s], 16)
            with sp.Fori(1, DEPTH * NP // RING) as i:
                for s in range(RING):
                    sp.wait_ge(lo_ready, i * RING + (s - RING + 1))
                    sp.dma_start(w_raw[:, s, :], weights[i * RING + s]).then_inc(raw_in[s], 16)
            for t in range(T):
                for half in range(2):
                    sp.wait_ge(out_ready, 2 * t + half + 1)
                    cols = slice(half * HALF, (half + 1) * HALF)
                    sp.dma_start(out[t][:, cols], xs[:, t, cols]).then_inc(out_done, 16)
            sp.wait_ge(out_done, 16 * 2 * T)

        @block.gpsimd
        def _(pool):
            fetched = [2 * KD]

            def ada_fetch(upto):
                while fetched[0] < upto:
                    n = fetched[0]
                    if n >= RING:
                        pool.wait_ge(ada_used, n - RING + 1)
                    pool.dma_start(ada_w[:, n % RING, :], w_ada[n // KD, n % KD]).then_inc(ada_in[n % RING], 16)
                    fetched[0] += 1

            def rsqrt(l, r):
                n = rs_index(l, r)
                pool.wait_ge(rs_asked, n + 1)
                nc.gpsimd.tensor_tensor(rs_out[:, n:n + 1], rs_in[:, n:n + 1], minus_half[:], ALU.pow)\
                    .then_inc(rs_done, 1)

            def ln_rows(stage):
                if stage > 1:
                    pool.wait_ge(affine_done, at_tile(stage - 2, T - 1))
                pool.dma_start(g_row[:], ln_row[stage - 1, 0:1, :].to_broadcast([P, D_MODEL])).then_inc(row_in, 16)
                pool.dma_start(b_row[:], ln_row[stage - 1, 1:2, :].to_broadcast([P, D_MODEL])).then_inc(row_in, 16)

            nc.gpsimd.memset(minus_half[:], -0.5).then_inc(pool_step, 1)
            nc.gpsimd.memset(ident[:], 0.0).then_inc(pool_step, 1)
            nc.gpsimd.memset(band[:], 0.0).then_inc(pool_step, 1)
            nc.gpsimd.memset(ones[:], 1.0).then_inc(consts, 1)
            pool.wait_ge(pool_step, 3)
            nc.gpsimd.affine_select(out=ident[:], in_=ident[:], compare_op=ALU.not_equal, fill=1.0, base=0,
                                    pattern=[[-1, P]], channel_multiplier=1).then_inc(consts, 1)
            nc.gpsimd.affine_select(out=band[:, 0:P], in_=band[:, 0:P], compare_op=ALU.is_ge, fill=NEG, base=-1,
                                    pattern=[[1, P]], channel_multiplier=-1).then_inc(consts, 1)
            nc.gpsimd.affine_select(out=band[:, P:2 * P], in_=band[:, P:2 * P], compare_op=ALU.is_ge, fill=NEG,
                                    base=0, pattern=[[-1, P]], channel_multiplier=1).then_inc(consts, 1)
            for l in range(DEPTH):
                if l == 0:
                    ada_fetch(4 * KD + RING)
                for u in range(8):
                    rsqrt(l, u)
                if l == 0:
                    ada_fetch(5 * KD + RING)
                ln_rows(2 * l + 1)
                for t in range(T):
                    rsqrt(l, 8 + t)
                if l == 0:
                    base = 5 * KD + RING
                    with pool.Fori(0, FG[0] // 2) as i:
                        for j in range(KD):
                            pool.wait_ge(ada_used, i * KD + (base + j - RING + 1))
                            pool.dma_start(ada_w[:, j % RING, :], w_ada[i + (base + j) // KD, (base + j) % KD])\
                                .then_inc(ada_in[j % RING], 16)
                    fetched[0] = base + KD * FG[0] // 2
                    ada_fetch(6 * DEPTH * KD)
                ln_rows(2 * l + 2)
                for t in range(T):
                    rsqrt(l, 12 + t)

        @block.tensor
        def _(pe):
            nc.tensor.sem_inc(piece_used, RING)

            def wait_piece(l, p):
                pe.wait_ge(hi_ready, converted(l, p))
                pe.wait_ge(lo_ready, converted(l, p))

            def split_product(dst, a_hi, a_lo, b_hi, b_lo, first, last):
                pe.matmul(dst, a_hi, b_hi, start=first, stop=False)
                pe.matmul(dst, a_hi, b_lo, start=False, stop=False)
                return pe.matmul(dst, a_lo, b_hi, start=False, stop=last)

            def transpose_x(stage, t, b0):
                if stage == 0:
                    pe.wait_ge(x_in[t], 16)
                    pe.wait_ge(consts, 4)
                else:
                    pe.wait_ge(xhat_ready, at_tile(stage - 1, t))
                if t >= 2:
                    pe.wait_ge(h_scaled_dve, scaled_dve(stage, t - 2))
                    pe.wait_ge(h_scaled_act, at_tile(stage, t - 2))
                for k in range(KD):
                    m = pe.transpose(bank[b0 + 2 * (t % 2) + k // 4][:, (k % 4) * P:(k % 4 + 1) * P],
                                     xs[:, t, k * P:(k + 1) * P], ident[:])
                m.then_inc(x_transposed, 1)

            def reduce_mod(g, b):
                if g == 0:
                    pe.wait_ge(consts, 4)
                pe.wait_ge(ada_used, (g + 1) * KD)
                for k in range(KD):
                    m = pe.matmul(bank[b][:, k:k + 1], ada_acc[:, g % 2, k * P:(k + 1) * P], ones[:, 0:1],
                                  start=True, stop=True)
                m.then_inc(mod_reduced, 1)

            def spread_gate(l, which, b):
                pe.wait_ge(gt_diag, 2 * l + which + 1)
                for half in range(2):
                    m = pe.matmul(bank[b + half][:], ones[:], scratch[:, half * 512:(half + 1) * 512],
                                  start=True, stop=True)
                m.then_inc(gt_spread, 1)

            def accumulate(l, q, j0, j1, a_hi, a_lo, nk, width, wait_tile):
                p0, n = PHASES[q]
                for j in range(j0, j1):
                    wait_piece(l, p0 + j)
                    s = slot(l, p0 + j)
                    for t in range(T):
                        if j == 0:
                            wait_tile(t)
                        rows = slice(t * P, (t + 1) * P)
                        for kk in range(nk):
                            k = j * nk + kk
                            cols = slice(kk * width, (kk + 1) * width)
                            m = split_product(bank[BANKS[q] + t][:, 0:width], a_hi[:, k, rows], a_lo[:, k, rows],
                                              w_hi[:, s, cols], w_lo[:, s, cols],
                                              j == 0 and kk == 0, j == n - 1 and kk == nk - 1)
                        if t == T - 1:
                            m.then_inc(piece_used, 1)
                        elif j == n - 1:
                            m.then_inc(tile_done, 1)

            def finish_tile(l, q, t, a_hi, a_lo, wait_tile):
                p0, n = PHASES[q]
                rows = slice(t * P, (t + 1) * P)
                if n == 4:
                    wait_tile(t)
                for j in range(n - 4, n):
                    if t == 0:
                        wait_piece(l, p0 + j)
                    s = slot(l, p0 + j)
                    for kk in range(2):
                        k = 2 * j + kk
                        cols = slice(kk * 512, (kk + 1) * 512)
                        m = split_product(bank[BANKS[q] + t][:], a_hi[:, k, rows], a_lo[:, k, rows],
                                          w_hi[:, s, cols], w_lo[:, s, cols], k == 0, k == 2 * n - 1)
                    if t == T - 1:
                        m.then_inc(piece_used, 1)
                if t < T - 1:
                    m.then_inc(tile_done, 1)

            def project_first(l):
                p0, n = PHASES[0]
                for pair in range(2):
                    for j in range(n):
                        s = slot(l, p0 + j)
                        if pair == 0:
                            wait_piece(l, p0 + j)
                        for t in (2 * pair, 2 * pair + 1):
                            if j == 0:
                                pe.wait_ge(h_lo, at_tile(2 * l, t))
                                if l > 0:
                                    pe.wait_ge(z_done, at_z(l - 1, DN11, t))
                            rows = slice(t * P, (t + 1) * P)
                            for kk in range(CK[0]):
                                k = j * CK[0] + kk
                                cols = slice(kk * CW[0], (kk + 1) * CW[0])
                                m = split_product(bank[BANKS[0] + t][:], hT_hi[:, k, rows], hT_lo[:, k, rows],
                                                  w_hi[:, s, cols], w_lo[:, s, cols], k == 0, k == KD - 1)
                            if t == T - 1:
                                m.then_inc(piece_used, 1)
                            elif j == n - 1:
                                m.then_inc(tile_done, 1)
                        if pair == 0 and j == 1:
                            transpose_x(2 * l, T - 1, 4)

            def project(l, c, j0, j1):
                def wait_tile(t):
                    if c == 1:
                        pe.wait_ge(h_scaled_dve, scaled_dve(2 * l, T - 1))
                        pe.wait_ge(h_scaled_act, at_tile(2 * l, T - 1))
                    else:
                        pe.wait_ge(proj_evac, at_chunk(l, (None, None, 0, 2, 3)[c], t))
                accumulate(l, c, j0, j1, hT_hi, hT_lo, CK[c], CW[c], wait_tile)

            def transpose_qk(l, c, t):
                pe.wait_ge(roped, at_chunk(l, c, t))
                if c == 0:
                    pe.wait_ge(proj_evac, at_chunk(l, 1, t))
                elif c == 2:
                    pe.wait_ge(relu_done, 24 * (l + 1))
                elif c < 4:
                    pe.wait_ge(qk_ready, at_chunk(l, c - 1, t))
                elif t == 0:
                    pe.wait_ge(proj_evac, at_chunk(l, 4, 2))
                else:
                    pe.wait_ge(qk_ready, at_chunk(l, 4, t - 1))
                for j in range((4, 2, 4, 1, 4)[c]):
                    src = pk[:, t, j * P:(j + 1) * P] if c in (1, 3) else pq[:, (c // 2) % 2, t, j * P:(j + 1) * P]
                    m = pe.transpose(bank[qk_bank(c, t)][:, j * P:(j + 1) * P], src, ident[:])
                m.then_inc(qk_transposed, 1)

            def index_scores(l):
                for i, t in enumerate(IDX_TILES):
                    for h in range(HEADS):
                        n = 24 * l + 8 * i + h
                        if i == 0 and h < 4:
                            pe.wait_ge(qk_ready, at_chunk(l, 1, T - 1))
                        else:
                            pe.wait_ge(relu_done, n - 3)
                        g = 64 * (h % 2)
                        pe.matmul(bank[4 + h % 4][:, 0:(t + 1) * P], qT[g:g + HD, 0, h // 2, t * P:(t + 1) * P],
                                  kT[g:g + HD, 0, 0:(t + 1) * P], start=True, stop=True).then_inc(idx_scored, 1)

            def head_scores(l, u, h):
                kind, t = UNITS[u]
                lo, hi = keys_of(UNITS[u])
                n = 8 * u + h
                if n < len(S_BANKS):
                    pe.wait_ge(qk_ready, at_chunk(l, 3, T - 1))
                    pe.wait_ge(proj_evac, at_chunk(l, 4, T - 1))
                else:
                    pe.wait_ge(masked, at_head(l, u, h) - len(S_BANKS))
                if (u, h) == (4, 0):
                    pe.wait_ge(qk_ready, at_chunk(l, 4, T - 1))
                g = 64 * (h % 2)
                q, k = (1, 2) if kind == "A" else (0, 1)
                pe.matmul(bank[S_BANKS[n % 3]][:, 0:hi - lo], qT[g:g + HD, q, h // 2, t * P:(t + 1) * P],
                          kT[g:g + HD, k, lo:hi], start=True, stop=True).then_inc(scored, 1)

            def transpose_p(l, u, h):
                lo, hi = keys_of(UNITS[u])
                pe.wait_ge(probs, at_head(l, u, h))
                if before := back(u, h, 2):
                    wait_pT(pe, l, *before)
                n = 8 * u + h
                for b in range((hi - lo) // P):
                    m = pe.transpose(bank[6 + h % 2][:, b * P:(b + 1) * P],
                                     prob[:, n % P_RING, b * P:(b + 1) * P], ident[:])
                m.then_inc(p_transposed, 1)

            def head_values(l, u, h):
                kind, t = UNITS[u]
                lo, hi = keys_of(UNITS[u])
                wait_pT(pe, l, u, h)
                if h == 0:
                    if u >= 2:
                        pe.wait_ge(y_ready, at_unit(l, u - 2))
                    else:
                        pe.wait_ge(proj_evac, at_chunk(l, 4, T - 1))
                v = v_a if kind == "A" else v_b
                g = 64 * (h % 2)
                nb = (hi - lo) // P
                for b in range(nb):
                    m = pe.matmul(bank[u % 2][:, h * HD:(h + 1) * HD], pT[:, h % PT_RING, b * P:(b + 1) * P],
                                  v[:, lo // P + b, g:g + HD], start=b == 0, stop=b == nb - 1)
                m.then_inc(av_done, 1)

            def transpose_y(l, u):
                pe.wait_ge(y_ready, at_unit(l, u))
                if u == 0:
                    pe.wait_ge(qk_ready, at_chunk(l, 4, T - 1))
                else:
                    pe.wait_ge(y_scaled, at_unit(l, u - 1))
                for j in range(4):
                    m = pe.transpose(bank[2][:, j * P:(j + 1) * P], y[:, u % 2, j * P:(j + 1) * P], ident[:])
                m.then_inc(y_transposed, 1)

            def attention(l):
                for i in range(64 + LAG_Y):
                    if i < 64:
                        head_scores(l, i // 8, i % 8)
                    if 0 <= i - LAG_T < 64:
                        transpose_p(l, (i - LAG_T) // 8, (i - LAG_T) % 8)
                    if 0 <= i - LAG_V < 64:
                        head_values(l, (i - LAG_V) // 8, (i - LAG_V) % 8)
                    if i in QB_AT:
                        transpose_qk(l, 4, QB_AT.index(i))
                    if (i - LAG_Y) % 8 == 7 and i > LAG_Y:
                        transpose_y(l, (i - LAG_Y) // 8)

            def gate_up(l, g):
                s0 = slot(l, GU_P[g])
                b0 = GU_BANK[g]

                def wait_turn(j, i):
                    pe.wait_ge(hi_ready, i * 4 + converted(l, GU_P[g] + j))
                    pe.wait_ge(lo_ready, i * 4 + converted(l, GU_P[g] + j))
                    pe.wait_ge(gate_read if j % 2 == 0 else gu_ready, i * 2 + (gu_before(l, g) + j // 2 + 1))

                def product(j, cols):
                    s = (s0 + j) % RING
                    for k in range(KD):
                        w = slice(k * P, (k + 1) * P)
                        m = split_product(bank[b0 + j][:, cols], w_hi[:, s, w], w_lo[:, s, w],
                                          hT_hi[:, k, cols], hT_lo[:, k, cols], k == 0, k == KD - 1)
                    return m

                def reduce_ada(i):
                    pe.wait_ge(ada_used, i * KD + 6 * KD)
                    for k in range(KD):
                        m = pe.matmul(bank[0][:, k:k + 1], ada_acc[:, 1, k * P:(k + 1) * P], ones[:, 0:1],
                                      start=True, stop=True)
                    m.then_inc(mod_reduced, 1)

                if g == 0:
                    for half in range(2):
                        pe.wait_ge(h_lo, at_tile(2 * l + 1, 2 * half + 1))
                        for j in range(4):
                            if half == 0:
                                wait_turn(j, 0)
                                pe.wait_ge(z_done, at_z(l, WO1, j))
                            m = product(j, slice(half * 256, (half + 1) * 256))
                            if half == 1:
                                m.then_inc(piece_used, 1)
                            elif j == 1:
                                transpose_x(2 * l + 1, T - 1, 0)
                    if l == 0:
                        reduce_ada(0)
                else:
                    pe.wait_ge(z_done, at_z(l, DN00, T - 1))
                with pe.Fori(1 - g, FG[g] // 2) as i:
                    for j in range(4):
                        wait_turn(j, i)
                        product(j, slice(0, SEQ)).then_inc(piece_used, 1)
                    if (l, g) == (0, 0):
                        reduce_ada(i)

            def down(l, g, half):
                q = DN00 + 2 * g + half
                last = (g, half) == (1, 1)

                def wait_tile(t):
                    if half == 0 and t == 0:
                        pe.wait_ge(gu_lo_ready, gu_before(l, g) + FG[g])
                    if q == DN00 and t == 0:
                        pe.wait_ge(h_scaled_dve, scaled_dve(2 * l + 1, T - 1))
                        pe.wait_ge(h_scaled_act, at_tile(2 * l + 1, T - 1))
                        pe.wait_ge(z_done, at_z(l, WO0, T - 1))
                        pe.wait_ge(mod_taken, 5 + FG[0] // 2)
                    elif q in (DN01, DN11) and t == 0:
                        pe.wait_ge(gt_taken, 2 * l + 2)
                        pe.wait_ge(gu_ready, gu_before(l, g) + FG[g] + 2)
                        pe.wait_ge(gate_read, gu_before(l, g) + FG[g] + 2)
                    elif q == DN10:
                        pe.wait_ge(z_done, at_z(l, DN01, t))
                        if t == T - 1:
                            pe.wait_ge(mod_taken, 6 * DEPTH)

                if q == DN00:
                    accumulate(l, q, 0, 2, gu_hi, gu_lo, 2, 512, wait_tile)
                    pe.wait_ge(gu_ready, gu_before(l, g) + FG[g] + 2)
                    pe.wait_ge(gate_read, gu_before(l, g) + FG[g] + 2)
                    spread_gate(l, 1, 4)
                if not last:
                    accumulate(l, q, 2 if q == DN00 else 0, PHASES[q][1], gu_hi, gu_lo, 2, 512, wait_tile)
                    return
                accumulate(l, q, 0, PHASES[q][1] - 4, gu_hi, gu_lo, 2, 512, wait_tile)
                for t in range(T):
                    finish_tile(l, q, t, gu_hi, gu_lo, wait_tile)
                    if l + 1 < DEPTH and t > 0:
                        transpose_x(2 * l + 2, t - 1, 4)

            reduce_mod(0, 0)
            reduce_mod(1, 1)
            for t in range(T - 1):
                transpose_x(0, t, 4)
            for l in range(DEPTH):
                project_first(l)
                project(l, 1, 0, 4)
                project(l, 2, 0, 2)
                for t in range(T):
                    transpose_qk(l, 0, t)
                for t in range(T):
                    transpose_qk(l, 1, t)
                index_scores(l)
                project(l, 2, 2, 4)
                project(l, 3, 0, 2)
                for t in range(T):
                    transpose_qk(l, 2, t)
                for t in range(T):
                    transpose_qk(l, 3, t)
                project(l, 4, 0, 4)
                attention(l)
                if l == 0:
                    pe.wait_ge(masked, at_head(l, 7, 7))
                    wait_pT(pe, l, 7, 6)
                    wait_pT(pe, l, 7, 7)
                    reduce_mod(2, 7)
                    reduce_mod(3, 4)

                def wait_wo0(t):
                    pe.wait_ge(yT_lo, at_unit(l, 7))
                    pe.wait_ge(masked, at_head(l, 7, 7))

                def wait_wo1(t):
                    if t == 0:
                        pe.wait_ge(gt_taken, 2 * l + 1)
                        pe.wait_ge(mod_taken, 4)
                        pe.wait_ge(masked, at_head(l, 7, 7))
                        wait_pT(pe, l, 7, 6)
                        wait_pT(pe, l, 7, 7)
                    if l == 0 and t == 3:
                        pe.wait_ge(mod_taken, 5)

                accumulate(l, WO0, 0, 2, hT_hi, hT_lo, 2, 512, wait_wo0)
                spread_gate(l, 0, 5)
                accumulate(l, WO0, 2, 4, hT_hi, hT_lo, 2, 512, wait_wo0)
                if l == 0:
                    reduce_mod(4, 7)
                for t in range(T):
                    finish_tile(l, WO1, t, hT_hi, hT_lo, wait_wo1)
                    if t == 0:
                        pe.wait_ge(z_done, at_z(l, WO0, T - 1))
                    else:
                        transpose_x(2 * l + 1, t - 1, 0)
                for g in range(2):
                    gate_up(l, g)
                    if (l, g) == (0, 1):
                        reduce_mod(6 * DEPTH - 1, 7)
                    down(l, g, 0)
                    down(l, g, 1)

        @block.scalar
        def _(act):
            conv = [0]

            def convert(l, upto):
                while conv[0] < min(l * NP + upto, DEPTH * NP):
                    p = conv[0]
                    act.wait_ge(raw_in[p % RING], 16 * (p // RING + 1))
                    act.wait_ge(piece_used, p + 1)
                    nc.scalar.activation(w_hi[:, p % RING, :], w_raw[:, p % RING, :], ACT.Copy).then_inc(hi_ready, 1)
                    conv[0] += 1

            def build_h(stage, t, b0, upto):
                act.wait_ge(coef_ready, stage + 1)
                act.wait_ge(x_transposed, at_tile(stage, t))
                if stage > 0 or t > 0:
                    act.wait_ge(h_lo, at_tile(stage, t) - 1)
                    act.wait_ge(h_hi, at_tile(stage, t) - 1)
                if t == 0 and stage % 2 == 1:
                    act.wait_ge(yT_lo, at_unit(stage // 2, 7))
                    act.wait_ge(gt_spread, 2 * (stage // 2) + 1)
                elif t == 0 and stage > 0:
                    act.wait_ge(gt_spread, stage)
                for k in range(dve_chunks(stage, t), KD):
                    m = nc.scalar.activation(scratch[:, k * P:(k + 1) * P],
                                             bank[b0 + 2 * (t % 2) + k // 4][:, (k % 4) * P:(k % 4 + 1) * P],
                                             ACT.Identity, scale=hcoef[:, stage, 0, k:k + 1],
                                             bias=hcoef[:, stage, 1, k:k + 1])
                m.then_inc(h_scaled_act, 1)
                convert(stage // 2, upto)
                act.wait_ge(h_scaled_act, at_tile(stage, t))
                act.wait_ge(h_scaled_dve, scaled_dve(stage, t))
                nc.scalar.activation(hT_hi[:, :, t * P:(t + 1) * P],
                                     scratch[:].rearrange("p (k s) -> p k s", k=KD), ACT.Copy).then_inc(h_hi, 1)

            def evacuate(l, c, t):
                wait_phase(act, l, c, t)
                src = bank[BANKS[c] + t]
                if c in (0, 2, 4):
                    if c == 4:
                        act.wait_ge(idx_acc, 24 * (l + 1))
                    elif l > 0 and c == 0:
                        act.wait_ge(qk_transposed, at_chunk(l - 1, 4, t))
                    elif l > 0:
                        act.wait_ge(p_transposed, 64 * l)
                    nc.scalar.activation(pq[:, (c // 2) % 2, t, :], src[:], ACT.Copy).then_inc(proj_evac, 1)
                elif c == 1:
                    if l > 0:
                        act.wait_ge(qk_transposed, at_chunk(l - 1, 3, t))
                    for d in range(2):
                        nc.scalar.activation(pk[:, t, d * HD:(d + 1) * HD], src[:, 0:HD], ACT.Copy)
                    nc.scalar.activation(pk[:, t, P:2 * P], src[:, HD:HD + P], ACT.Copy)
                    nc.scalar.activation(v_b[:, t, 0:P], src[:, HD + P:HD + 2 * P], ACT.Copy)
                    nc.scalar.activation(v_b[:, t, P:P + HEADS], src[:, HD + 2 * P:HD + 2 * P + HEADS], ACT.Copy,
                                         scale=HEADS ** -0.5 * HD ** -0.5).then_inc(proj_evac, 1)
                else:
                    act.wait_ge(qk_transposed, at_chunk(l, 1, t))
                    nc.scalar.activation(pk[:, t, 0:P], src[:, 0:P], ACT.Copy)
                    nc.scalar.activation(v_a[:, t, :], src[:, P:2 * P], ACT.Copy).then_inc(proj_evac, 1)

            def copy_qk(l, c, t):
                act.wait_ge(qk_transposed, at_chunk(l, c, t))
                if c == 4 and t == 0:
                    act.wait_ge(idx_scored, 24 * (l + 1))
                n = (4, 2, 4, 1, 4)[c]
                cols = slice(t * P, (t + 1) * P)
                if c in (1, 3):
                    dst = kT[:, 0:2, cols] if c == 1 else kT[:, 2:3, cols]
                else:
                    dst = qT[:, (c // 2) % 2, :, cols]
                nc.scalar.activation(dst, bank[qk_bank(c, t)][:, 0:n * P].rearrange("p (j s) -> p j s", j=n), ACT.Copy)\
                    .then_inc(qk_ready, 1)

            def relu(l, i, h):
                n = 24 * l + 8 * i + h
                act.wait_ge(idx_scored, n + 1)
                if 8 * i + h >= P_RING:
                    act.wait_ge(idx_acc, n - P_RING + 1)
                else:
                    act.wait_ge(qk_transposed, at_chunk(l, 0, T - 1))
                w = (IDX_TILES[i] + 1) * P
                nc.scalar.activation(rel[:, (8 * i + h) % P_RING, 0:w], bank[4 + h % 4][:, 0:w], ACT.Relu)\
                    .then_inc(relu_done, 1)

            def exponential(l, u, h):
                lo, hi = keys_of(UNITS[u])
                n = 8 * u + h
                act.wait_ge(masked, at_head(l, u, h))
                p = prob[:, n % P_RING, 0:hi - lo]
                nc.scalar.activation(p, p, ACT.Exp, scale=-1.0, bias=nmax[:, u % 2, h:h + 1],
                                     accum_out=rowsum[:, u % 2, h:h + 1]).then_inc(probs, 1)

            def copy_p(l, u, h):
                lo, hi = keys_of(UNITS[u])
                act.wait_ge(p_transposed, at_head(l, u, h))
                if before := back(u, h, PT_RING):
                    act.wait_ge(av_done, at_head(l, *before))
                nc.scalar.activation(pT[:, h % PT_RING, 0:hi - lo], bank[6 + h % 2][:, 0:hi - lo], ACT.Copy)\
                    .then_inc(pT_act, 1)

            def sink_weight(l, u):
                act.wait_ge(sink_diff, 4 * l + u + 1)
                nc.scalar.activation(es[:, u % 2, :], es[:, u % 2, :], ACT.Exp).then_inc(sink_exp, 1)

            def split_y(l, u):
                kind, t = UNITS[u]
                act.wait_ge(y_scaled, at_unit(l, u))
                k0 = 0 if kind == "A" else 4
                nc.scalar.activation(hT_hi[:, k0:k0 + 4, t * P:(t + 1) * P],
                                     scratch[:, (u % 2) * 512:(u % 2 + 1) * 512].rearrange("p (k s) -> p k s", k=4),
                                     ACT.Copy).then_inc(yT_hi, 1)

            def attention(l):
                for i in range(64 + LAG_HI):
                    if i < 64:
                        exponential(l, i // 8, i % 8)
                        u, h = i // 8, i % 8
                        if h == 7 and UNITS[u][0] == "A":
                            sink_weight(l, u)
                    if 0 <= i - LAG_T < 64:
                        u, h = (i - LAG_T) // 8, (i - LAG_T) % 8
                        if not on_dve(u, h):
                            copy_p(l, u, h)
                    if i in QB_AT:
                        copy_qk(l, 4, QB_AT.index(i))
                    if (i - LAG_HI) % 8 == 7 and i > LAG_HI:
                        split_y(l, (i - LAG_HI) // 8)
                    if i == 40:
                        convert(l, WO_P + 2)
                    if i == 56:
                        convert(l, WO_P + 4)

            def feed(l, g):
                p0 = GU_P[g]
                f0 = gu_before(l, g)
                s0 = slot(l, p0)
                with act.Fori(0, FG[g] // 2) as i:
                    for f in range(2):
                        act.wait_ge(piece_used, i * 4 + used(l, p0 + 2 * f))
                        nc.scalar.activation(silu_g[:, f, :], bank[GU_BANK[g] + 2 * f][:], ACT.Silu)\
                            .then_inc(gate_read, 1)
                        for j in (2 * f + 4, 2 * f + 5):
                            s = (s0 + j) % RING
                            act.wait_ge(raw_in[s], i * 16 + 16 * ((l * NP + p0 + j) // RING + 1))
                            act.wait_ge(piece_used, i * 4 + (l * NP + p0 + j + 1))
                            nc.scalar.activation(w_hi[:, s, :], w_raw[:, s, :], ACT.Copy).then_inc(hi_ready, 1)
                        act.wait_ge(gu_ready, i * 2 + (f0 + f + 1 + 2))
                        nc.scalar.activation(gu_hi[:, bass.ds(i * 2 + f, 1), :], gu[:, f:f + 1, :], ACT.Copy)\
                            .then_inc(gu_hi_ready, 1)
                conv[0] += 4 * (FG[g] // 2)

            act.dma_start(cc[:, 0, :], c_col).then_inc(c_in, 16)
            act.wait_ge(c_in, 16)
            nc.scalar.activation(cc[:, 1, :], cc[:, 0, :], ACT.Silu).then_inc(rope_table, 1)
            for dst, src in ((modb[:], b_ada), (lnc[:], ln_col), (gcol[:], g_col)):
                act.dma_start(dst, src).then_inc(small_in, 16)
            act.dma_start(nsink[:], sinks.to_broadcast([P, DEPTH, HEADS])).then_inc(small_in, 16)
            act.dma_start(angles[:, 0, 0:32], inv_freq.to_broadcast([P, 32])).then_inc(small_in, 16)
            act.dma_start(angles[:, 0, 32:36].bitcast(I32), positions).then_inc(small_in, 16)
            nc.scalar.sem_inc(gate_read, 2)
            act.wait_ge(rope_angle, 1)
            nc.scalar.activation(angles[:, 1, 0:256], angles[:, 1, 0:256], ACT.Sin).then_inc(rope_table, 1)
            for t in range(T):
                build_h(0, t, 4, t + 1)
            for l in range(DEPTH):
                for c in range(2):
                    convert(l, C0P[c + 1] + 2)
                    for t in range(T):
                        evacuate(l, c, t)
                    convert(l, C0P[c + 1] + 3)
                for t in range(T):
                    copy_qk(l, 0, t)
                for t in range(T):
                    copy_qk(l, 1, t)
                for i in range(len(IDX_TILES)):
                    for h in range(HEADS):
                        relu(l, i, h)
                convert(l, C0P[4] + 1)
                for t in range(T):
                    evacuate(l, 2, t)
                convert(l, C0P[4] + 2)
                for t in range(T):
                    evacuate(l, 3, t)
                convert(l, C0P[4] + 3)
                for t in range(T):
                    copy_qk(l, 2, t)
                for t in range(T):
                    copy_qk(l, 3, t)
                convert(l, C0P[4] + 4)
                for t in range(T):
                    evacuate(l, 4, t)
                attention(l)
                for t in range(T):
                    convert(l, WO_P + 4 + t + 1)
                for t in range(2):
                    build_h(2 * l + 1, t, 0, 0)
                convert(l, GU_P[0] + 3)
                for t in range(2, T):
                    build_h(2 * l + 1, t, 0, GU_P[0] + 4)
                feed(l, 0)
                convert(l, GU_P[1] + 4)
                feed(l, 1)
                convert(l, NP)
                if l + 1 < DEPTH:
                    for t in range(2):
                        build_h(2 * l + 2, t, 4, 0)
                    convert(l + 1, 3)
                    for t in range(2, T):
                        build_h(2 * l + 2, t, 4, 4)

        @block.vector
        def _(dve):
            steps = [0]
            conv = [0]
            ada = [0]

            def step(ins):
                steps[0] += 1
                ins.then_inc(dve_step, 1)
                dve.wait_ge(dve_step, steps[0])

            def convert(l, upto):
                while conv[0] < min(l * NP + upto, DEPTH * NP):
                    p = conv[0]
                    dve.wait_ge(hi_ready, p + 1)
                    nc.vector.tensor_tensor(w_lo[:, p % RING, :], w_raw[:, p % RING, :],
                                            w_hi[:, p % RING, :].bitcast(F32), ALU.subtract).then_inc(lo_ready, 1)
                    conv[0] += 1

            def ada_group(g, k0=0, k1=KD):
                for k in range(k0, k1):
                    n = g * KD + k
                    if k > 0:
                        dve.wait_ge(ada_used, n)
                    ada_piece(n, k, g)

            def ada_piece(n, k, g):
                if n < 2 * KD:
                    dve.wait_ge(ada_first_in[n % RING], 16 * (n // RING + 1))
                else:
                    dve.wait_ge(ada_in[n % RING], 16 * ((n - 2 * KD) // RING + 1))
                if k == 0:
                    if g >= 2:
                        dve.wait_ge(mod_reduced, g - 1)
                    nc.vector.tensor_scalar(ada_acc[:, g % 2, :], ada_w[:, n % RING, :], cc[:, 1, 0:1], None,
                                            ALU.mult).then_inc(ada_used, 1)
                else:
                    nc.vector.scalar_tensor_tensor(out=ada_acc[:, g % 2, :], in0=ada_w[:, n % RING, :],
                                                   scalar=cc[:, 1, k:k + 1], in1=ada_acc[:, g % 2, :],
                                                   op0=ALU.mult, op1=ALU.add).then_inc(ada_used, 1)

            def take_mod(g, b):
                dve.wait_ge(mod_reduced, g + 1)
                nc.vector.tensor_tensor(mod[:, g, :], bank[b][:, 0:KD], modb[:, g, :], ALU.add)\
                    .then_inc(mod_taken, 1)
                dve.wait_ge(mod_taken, g + 1)

            def h_coefficients(stage):
                l, second = stage // 2, stage % 2
                sh, sc = mod[:, 6 * l + 3 * second, :], mod[:, 6 * l + 3 * second + 1, :]
                nc.vector.scalar_tensor_tensor(out=hcoef[:, stage, 0, :], in0=sc, scalar=1.0,
                                               in1=lnc[:, stage, 0, :], op0=ALU.add, op1=ALU.mult)
                step(nc.vector.scalar_tensor_tensor(out=hcoef[:, stage, 1, :], in0=sc, scalar=1.0,
                                                    in1=lnc[:, stage, 1, :], op0=ALU.add, op1=ALU.mult))
                nc.vector.tensor_tensor(hcoef[:, stage, 1, :], hcoef[:, stage, 1, :], sh, ALU.add)\
                    .then_inc(coef_ready, 1)
                dve.wait_ge(coef_ready, stage + 1)

            def gate_diagonal(l, which):
                g = 6 * l + (GT1, GT2)[which]
                if which == 0:
                    dve.wait_ge(yT_lo, at_unit(l, 7))
                else:
                    dve.wait_ge(h_lo, at_tile(2 * l + 1, T - 1))
                step(nc.vector.tensor_scalar(mod[:, g, :], mod[:, g, :], 1.0, None, ALU.add))
                nc.vector.tensor_tensor(scratch[:].rearrange("p (k s) -> p k s", k=KD),
                                        ident[:].unsqueeze(1).to_broadcast([P, KD, P]),
                                        mod[:, g, :].unsqueeze(2).to_broadcast([P, KD, P]), ALU.mult)\
                    .then_inc(gt_diag, 1)

            def take_gate(l, which, b):
                dve.wait_ge(gt_spread, 2 * l + which + 1)
                for half in range(2):
                    m = nc.vector.tensor_copy(gt_row[:, half * 512:(half + 1) * 512], bank[b + half][:])
                m.then_inc(gt_taken, 1)
                dve.wait_ge(gt_taken, 2 * l + which + 1)

            def scale_h(stage, t, b0):
                dve.wait_ge(x_transposed, at_tile(stage, t))
                if stage > 0 or t > 0:
                    dve.wait_ge(h_hi, at_tile(stage, t) - 1)
                    dve.wait_ge(h_lo, at_tile(stage, t) - 1)
                for k in range(dve_chunks(stage, t)):
                    m = nc.vector.tensor_scalar(scratch[:, k * P:(k + 1) * P],
                                                bank[b0 + 2 * (t % 2)][:, k * P:(k + 1) * P],
                                                hcoef[:, stage, 0, k:k + 1], hcoef[:, stage, 1, k:k + 1],
                                                ALU.mult, ALU.add)
                m.then_inc(h_scaled_dve, 1)

            def split_h(stage, t):
                dve.wait_ge(h_hi, at_tile(stage, t))
                cols = slice(t * P, (t + 1) * P)
                nc.vector.tensor_tensor(hT_lo[:, :, cols], scratch[:].rearrange("p (k s) -> p k s", k=KD),
                                        hT_hi[:, :, cols].bitcast(F32), ALU.subtract).then_inc(h_lo, 1)

            def rope(l, c, t):
                dve.wait_ge(proj_evac, at_chunk(l, c, t))
                if at_chunk(l, c, t) > 1:
                    dve.wait_ge(roped, at_chunk(l, c, t) - 1)
                heads = (8, 4, 8, 2, 8)[c]
                v = pk[:, t, 0:heads * HD] if c in (1, 3) else pq[:, (c // 2) % 2, t, :]
                v = v.rearrange("p (h d) -> p h d", h=heads)
                a = scratch[:, 0:heads * HD].rearrange("p (h d) -> p h d", h=heads)
                b = scratch[:, 512:512 + heads * HD].rearrange("p (h d) -> p h d", h=heads)
                n = HD // 2

                def over_heads(table, d0, d1):
                    return table[:, t, d0:d1].unsqueeze(1).to_broadcast([P, heads, d1 - d0])

                nc.vector.tensor_tensor(b[:, :, 0:n], v[:, :, n:HD], over_heads(sin_t, 0, n), ALU.mult)
                nc.vector.tensor_tensor(b[:, :, n:HD], v[:, :, 0:n], over_heads(sin_t, n, HD), ALU.mult)
                step(nc.vector.tensor_tensor(a, v, over_heads(cos_t, 0, HD), ALU.mult))
                nc.vector.tensor_tensor(v, a, b, ALU.add).then_inc(roped, 1)

            def add_index_head(l, i, h):
                t = IDX_TILES[i]
                w = (t + 1) * P
                n = 24 * l + 8 * i + h
                dve.wait_ge(relu_done, n + 1)
                part = rel[:, (8 * i + h) % P_RING, 0:w]
                sc = scores[:, SC_AT[t]:SC_AT[t] + w]
                wi = v_b[:, t, P + h:P + h + 1]
                if h == 0:
                    nc.vector.tensor_scalar(sc, part, wi, None, ALU.mult).then_inc(idx_acc, 1)
                else:
                    nc.vector.scalar_tensor_tensor(out=sc, in0=part, scalar=wi, in1=sc, op0=ALU.mult, op1=ALU.add)\
                        .then_inc(idx_acc, 1)
                dve.wait_ge(idx_acc, n + 1)
                if h == HEADS - 1:
                    own = scores[:, SC_AT[t] + t * P:SC_AT[t] + w]
                    step(nc.vector.tensor_tensor(own, own, band[:, P:2 * P], ALU.add))

            def top_rounds(r0, r1):
                for r in range(r0, r1):
                    for t in IDX_TILES:
                        sc = scores[:, SC_AT[t]:SC_AT[t] + (t + 1) * P]
                        steps[0] += 1
                        if r > 0:
                            dve.wait_ge(dve_step, steps[0] - 3)
                        nc.vector.max(top8[:, t, :], sc).then_inc(dve_step, 1)
                    for t in IDX_TILES:
                        sc = scores[:, SC_AT[t]:SC_AT[t] + (t + 1) * P]
                        steps[0] += 1
                        dve.wait_ge(dve_step, steps[0] - 3)
                        nc.vector.match_replace(out=sc, in_to_replace=top8[:, t, :], in_values=sc, imm_value=TAKEN)\
                            .then_inc(dve_step, 1)

            def top_masks():
                dve.wait_ge(dve_step, steps[0])
                nc.vector.tensor_copy(scores[:, 0:P], band[:, P:2 * P])
                step(nc.vector.tensor_scalar(scores[:, P:SC_W], scores[:, P:SC_W], CUT, NEG, ALU.is_gt, ALU.mult))

            def mask_scores(l, u, h):
                kind, t = UNITS[u]
                lo, hi = keys_of(UNITS[u])
                n = 8 * u + h
                dve.wait_ge(scored, at_head(l, u, h))
                if n >= P_RING:
                    dve.wait_ge(p_transposed, at_head(l, u, h) - P_RING)
                else:
                    dve.wait_ge(qk_transposed, at_chunk(l, 2, T - 1))
                if h == 0 and u >= 2:
                    dve.wait_ge(probs, at_head(l, u - 2, 7))
                if kind == "A":
                    mask = band[:] if t > 0 else band[:, P:2 * P]
                    start = nsink[:, l, h:h + 1]
                else:
                    mask = scores[:, SC_AT[t]:SC_AT[t] + hi - lo]
                    start = 3.0e38
                nc.vector.tensor_tensor_reduce(out=prob[:, n % P_RING, 0:hi - lo], in0=bank[S_BANKS[n % 3]][:, 0:hi - lo],
                                               in1=mask, scale=-(HD ** -0.5), scalar=start, op0=ALU.add,
                                               op1=ALU.min, accum_out=nmax[:, u % 2, h:h + 1]).then_inc(masked, 1)

            def copy_p(l, u, h):
                lo, hi = keys_of(UNITS[u])
                dve.wait_ge(p_transposed, at_head(l, u, h))
                if before := back(u, h, PT_RING):
                    dve.wait_ge(av_done, at_head(l, *before))
                nc.vector.tensor_copy(pT[:, h % PT_RING, 0:hi - lo], bank[6 + h % 2][:, 0:hi - lo]).then_inc(pT_dve, 1)

            def sink_difference(l, u):
                dve.wait_ge(masked, at_head(l, u, 7))
                nc.vector.tensor_tensor(es[:, u % 2, :], nmax[:, u % 2, :], nsink[:, l, :], ALU.subtract)\
                    .then_inc(sink_diff, 1)

            def norm_y(l, u):
                kind, t = UNITS[u]
                b = u % 2
                dve.wait_ge(probs, at_head(l, u, 7))
                total = rowsum[:, b, :]
                if kind == "A":
                    dve.wait_ge(sink_exp, 4 * l + u + 1)
                    step(nc.vector.tensor_tensor(es[:, b, :], rowsum[:, b, :], es[:, b, :], ALU.add))
                    total = es[:, b, :]
                step(nc.vector.reciprocal(recip[:, b, :], total))
                dve.wait_ge(av_done, at_head(l, u, 7))
                if u >= 2:
                    dve.wait_ge(y_transposed, at_unit(l, u - 2))
                step(nc.vector.tensor_tensor(y[:, b, :].rearrange("p (h d) -> p h d", h=HEADS),
                                             bank[b][:].rearrange("p (h d) -> p h d", h=HEADS),
                                             recip[:, b, :].unsqueeze(2).to_broadcast([P, HEADS, HD]), ALU.mult))
                if u >= 2:
                    dve.wait_ge(yT_hi, at_unit(l, u - 2))
                    dve.wait_ge(yT_lo, at_unit(l, u - 2))
                else:
                    dve.wait_ge(roped, at_chunk(l, 4, T - 1))
                n = rs_index(l, u)
                step(nc.vector.tensor_tensor_reduce(out=scratch[:, b * 512:(b + 1) * 512], in0=y[:, b, :],
                                                    in1=y[:, b, :], scale=1.0, scalar=0.0, op0=ALU.mult,
                                                    op1=ALU.add, accum_out=mean_var[:, 0, 0:1]))
                nc.vector.tensor_scalar(rs_in[:, n:n + 1], mean_var[:, 0, 0:1], 1.0 / 512, RMS_EPS, ALU.mult,
                                        ALU.add).then_inc(rs_asked, 1)

            def scale_y(l, u):
                n = rs_index(l, u)
                dve.wait_ge(rs_done, n + 1)
                nc.vector.tensor_scalar(y[:, u % 2, :], y[:, u % 2, :], rs_out[:, n:n + 1], None, ALU.mult)\
                    .then_inc(y_ready, 1)

            def gain_y(l, u):
                kind, _ = UNITS[u]
                g = gcol[:, l, 0 if kind == "A" else 1, :]
                dve.wait_ge(y_transposed, at_unit(l, u))
                dst = scratch[:, (u % 2) * 512:(u % 2 + 1) * 512].rearrange("p (k s) -> p k s", k=4)
                nc.vector.tensor_tensor(dst, bank[2][:].rearrange("p (k s) -> p k s", k=4),
                                        g.unsqueeze(2).to_broadcast([P, 4, P]), ALU.mult).then_inc(y_scaled, 1)

            def split_y(l, u):
                kind, t = UNITS[u]
                k0 = 0 if kind == "A" else 4
                dve.wait_ge(yT_hi, at_unit(l, u))
                cols = slice(t * P, (t + 1) * P)
                nc.vector.tensor_tensor(hT_lo[:, k0:k0 + 4, cols],
                                        scratch[:, (u % 2) * 512:(u % 2 + 1) * 512]
                                        .rearrange("p (k s) -> p k s", k=4),
                                        hT_hi[:, k0:k0 + 4, cols].bitcast(F32), ALU.subtract).then_inc(yT_lo, 1)

            def residual(l, q, t, first):
                half = (q - WO0) % 2
                cols = slice(half * HALF, (half + 1) * HALF)
                wait_phase(dve, l, q, t)
                nc.vector.tensor_tensor(ztmp[:], bank[BANKS[q] + t][:], gt_row[:, cols], ALU.mult)\
                    .then_inc(z_done, 1)
                dve.wait_ge(z_done, at_z(l, q, t))
                step(nc.vector.scalar_tensor_tensor(out=xs[:, t, cols], in0=xs[:, t, cols],
                                                    scalar=ALPHA if first else 1.0, in1=ztmp[:],
                                                    op0=ALU.mult, op1=ALU.add))
                if q in (WO0, WO1, DN10, DN11):
                    steps[0] += 1
                    nc.vector.bn_stats(stats[:, t, half, :], xs[:, t, cols]).then_inc(dve_step, 1)

            def moments(l, second, t):
                r = rs_index(l, 8 + 4 * second + t)
                dve.wait_ge(dve_step, steps[0])
                step(nc.vector.bn_aggr(mean_var[:, t, :], stats[:, t, :, :]))
                nc.vector.tensor_scalar(rs_in[:, r:r + 1], mean_var[:, t, 1:2], LN_EPS, None, ALU.add)\
                    .then_inc(rs_asked, 1)

            def normalise(l, second, t):
                r = rs_index(l, 8 + 4 * second + t)
                dve.wait_ge(rs_done, r + 1)
                nc.vector.tensor_scalar(xs[:, t, :], xs[:, t, :], mean_var[:, t, 0:1], rs_out[:, r:r + 1],
                                        ALU.subtract, ALU.mult).then_inc(xhat_ready, 1)

            def output_tile(t):
                r = rs_index(DEPTH - 1, 12 + t)
                dve.wait_ge(row_in, 32 * 2 * DEPTH)
                for half in range(2):
                    cols = slice(half * HALF, (half + 1) * HALF)
                    m = nc.vector.scalar_tensor_tensor(out=xs[:, t, cols], in0=xs[:, t, cols],
                                                       scalar=mean_var[:, t, 0:1], in1=g_row[:, cols],
                                                       op0=ALU.subtract, op1=ALU.mult)
                step(m)
                dve.wait_ge(rs_done, r + 1)
                for half in range(2):
                    cols = slice(half * HALF, (half + 1) * HALF)
                    nc.vector.scalar_tensor_tensor(out=xs[:, t, cols], in0=xs[:, t, cols],
                                                   scalar=rs_out[:, r:r + 1], in1=b_row[:, cols],
                                                   op0=ALU.mult, op1=ALU.add).then_inc(out_ready, 1)

            def last_tiles(l, q, b0):
                second = int(q == DN11)
                stage = 2 * l + 1 + second
                pieces = (l, GU_P[0]) if q == WO1 else (l + 1, 0)

                def convert_next(n):
                    convert(pieces[0], pieces[1] + n)

                for t in range(T):
                    residual(l, q, t, not second)
                    moments(l, second, t)
                    if t == T - 1:
                        convert_next(2)
                    normalise(l, second, t)
                    if 0 < t < T - 1:
                        split_h(stage, t - 1)
                    if t == T - 2:
                        convert_next(1)
                for t in range(2, T):
                    convert_next(t + 1)
                    scale_h(stage, t, b0)
                    if t == 2:
                        convert_next(4)
                    split_h(stage, t)

            def affine(stage, t):
                dve.wait_ge(row_in, 32 * stage)
                dve.wait_ge(x_transposed, at_tile(stage, t))
                step(nc.vector.tensor_tensor(xs[:, t, :], xs[:, t, :], g_row[:], ALU.mult))
                nc.vector.tensor_tensor(xs[:, t, :], xs[:, t, :], b_row[:], ALU.add).then_inc(affine_done, 1)
                dve.wait_ge(affine_done, at_tile(stage - 1, t))

            def rope_tables():
                two_pi = 2.0 * np.pi
                c1 = np.float32(np.round(two_pi * 2 ** 8) / 2 ** 8)
                c2 = np.float32(np.round((two_pi - float(c1)) * 2 ** 20) / 2 ** 20)
                c3 = np.float32(two_pi - float(c1) - float(c2))
                magic = 1.5 * 2 ** 23
                pos_f = top8[:, 0, 0:T]
                step(nc.vector.tensor_copy(pos_f, angles[:, 0, 32:36].bitcast(I32)))
                ang = angles[:, 0, 64:192]
                for t in range(T):
                    m = nc.vector.tensor_scalar(ang[:, t * 32:(t + 1) * 32], angles[:, 0, 0:32],
                                                pos_f[:, t:t + 1], None, ALU.mult)
                step(m)
                turns = angles[:, 0, 192:448]
                nc.vector.tensor_scalar(turns[:, 0:128], ang, 1.0 / two_pi, None, ALU.mult)
                step(nc.vector.tensor_scalar(turns[:, 128:256], ang, 1.0 / two_pi, 0.25, ALU.mult, ALU.add))
                step(nc.vector.tensor_scalar(turns, turns, magic, None, ALU.add))
                step(nc.vector.tensor_scalar(turns, turns, -magic, None, ALU.add))
                r = angles[:, 1, 0:256]
                for i in range(2):
                    m = nc.vector.scalar_tensor_tensor(out=r[:, i * 128:(i + 1) * 128],
                                                       in0=turns[:, i * 128:(i + 1) * 128], scalar=-float(c1),
                                                       in1=ang, op0=ALU.mult, op1=ALU.add)
                step(m)
                for c in (c2, c3):
                    step(nc.vector.scalar_tensor_tensor(out=r, in0=turns, scalar=-float(c), in1=r,
                                                        op0=ALU.mult, op1=ALU.add))
                step(nc.vector.tensor_scalar(r[:, 128:256], r[:, 128:256], float(np.float32(np.pi / 2)), None,
                                             ALU.add))
                pi = float(np.nextafter(np.float32(np.pi), np.float32(0)))
                nc.vector.tensor_scalar(r, r, pi, -pi, ALU.min, ALU.max).then_inc(rope_angle, 1)

            def rope_signs():
                dve.wait_ge(rope_table, 2)
                s = angles[:, 1, 0:128].rearrange("p (t d) -> p t d", t=T)
                c = angles[:, 1, 128:256].rearrange("p (t d) -> p t d", t=T)
                nc.vector.tensor_scalar(sin_t[:, :, 0:32], s, -1.0, None, ALU.mult)
                nc.vector.tensor_copy(sin_t[:, :, 32:64], s)
                nc.vector.tensor_copy(cos_t[:, :, 0:32], c)
                step(nc.vector.tensor_copy(cos_t[:, :, 32:64], c))

            def attention(l):
                rounds = TOPK // 8
                done = [9]

                def rounds_to(n):
                    top_rounds(done[0], n)
                    done[0] = n

                for i in range(64 + LAG_LO):
                    if i < 64:
                        u, h = i // 8, i % 8
                        if i == 32:
                            rounds_to(rounds)
                            top_masks()
                        mask_scores(l, u, h)
                        if h == 7 and UNITS[u][0] == "A":
                            sink_difference(l, u)
                        if i % 4 == 3 and 8 <= i < 32:
                            rounds_to(9 + (i - 3) // 4)
                    if 0 <= i - LAG_T < 64:
                        u, h = (i - LAG_T) // 8, (i - LAG_T) % 8
                        if on_dve(u, h):
                            copy_p(l, u, h)
                    if i in ROPE_AT:
                        rope(l, 4, ROPE_AT.index(i))
                    for lag, part in ((LAG_NORM, norm_y), (LAG_SCALE, scale_y), (LAG_GAIN, gain_y),
                                      (LAG_LO, split_y)):
                        if (i - lag) % 8 == 7 and i > lag:
                            part(l, (i - lag) // 8)
                    if i == 40:
                        convert(l, WO_P + 2)
                    if i == 56:
                        convert(l, WO_P + 4)

            def feed(l, g):
                p0 = GU_P[g]
                f0 = gu_before(l, g)
                s0 = slot(l, p0)
                with_ada = (l, g) == (0, 0)

                def low_half(i, j):
                    s = (s0 + j) % RING
                    dve.wait_ge(hi_ready, i * 4 + converted(l, p0 + j))
                    nc.vector.tensor_tensor(w_lo[:, s, :], w_raw[:, s, :], w_hi[:, s, :].bitcast(F32),
                                            ALU.subtract).then_inc(lo_ready, 1)

                def ada_pieces(i, k0, k1):
                    for k in range(k0, k1):
                        n = 5 * KD + k
                        dve.wait_ge(ada_in[n % RING], i * (16 * KD // RING) + 16 * ((n - 2 * KD) // RING + 1))
                        if k == 0:
                            m = nc.vector.tensor_scalar(ada_acc[:, 1, :], ada_w[:, n % RING, :], cc[:, 1, 0:1],
                                                        None, ALU.mult)
                        else:
                            dve.wait_ge(ada_used, i * KD + n)
                            m = nc.vector.scalar_tensor_tensor(
                                out=ada_acc[:, 1, :], in0=ada_w[:, n % RING, :], scalar=cc[:, 1, k:k + 1],
                                in1=ada_acc[:, 1, :], op0=ALU.mult, op1=ALU.add)
                        m.then_inc(ada_used, 1)

                with dve.Fori(0, FG[g] // 2) as i:
                    for f in range(2):
                        if with_ada:
                            ada_pieces(i, 4 * f, 4 * f + 4)
                        low_half(i, 2 * f + 4)
                        dve.wait_ge(piece_used, i * 4 + used(l, p0 + 2 * f + 1))
                        dve.wait_ge(gate_read, i * 2 + (f0 + f + 1 + 2))
                        nc.vector.tensor_tensor(gu[:, f, :], bank[GU_BANK[g] + 2 * f + 1][:], silu_g[:, f, :],
                                                ALU.mult).then_inc(gu_ready, 1)
                        low_half(i, 2 * f + 5)
                        dve.wait_ge(gu_hi_ready, i * 2 + (f0 + f + 1))
                        at = bass.ds(i * 2 + f, 1)
                        nc.vector.tensor_tensor(gu_lo[:, at, :], gu[:, f:f + 1, :],
                                                gu_hi[:, at, :].bitcast(F32), ALU.subtract).then_inc(gu_lo_ready, 1)
                        dve.wait_ge(gu_lo_ready, i * 2 + (f0 + f + 1))
                    if with_ada:
                        dve.wait_ge(mod_reduced, i + 6)
                        nc.vector.tensor_tensor(mod[:, bass.ds(i + 5, 1), :],
                                                bank[0][:, 0:KD].unsqueeze(1),
                                                modb[:, bass.ds(i + 5, 1), :], ALU.add).then_inc(mod_taken, 1)
                if with_ada:
                    dve.wait_ge(mod_taken, 5 + FG[0] // 2)
                conv[0] += 4 * (FG[g] // 2)

            nc.vector.sem_inc(gu_ready, 2)
            dve.wait_ge(consts, 4)
            dve.wait_ge(rope_table, 1)
            ada_group(0)
            ada_group(1)
            dve.wait_ge(small_in, 16 * 6)
            rope_tables()
            step(nc.vector.tensor_scalar(nsink[:], nsink[:], -1.0, None, ALU.mult))
            take_mod(0, 0)
            take_mod(1, 1)
            h_coefficients(0)
            for t in range(T):
                scale_h(0, t, 4)
                convert(0, t + 1)
                split_h(0, t)
                if t == 0:
                    rope_signs()
            for l in range(DEPTH):
                convert(l, 4)
                if l == 0:
                    ada_group(2, 0, 4)
                    convert(l, 5)
                    ada_group(2, 4, KD)
                else:
                    for t in range(T):
                        affine(2 * l, t)
                        convert(l, 4 + min(t, 1))
                convert(l, C0P[1] + 2)
                for t in range(T):
                    rope(l, 0, t)
                    convert(l, C0P[1] + 3)
                convert(l, C0P[2])
                if l == 0:
                    ada_group(3, 0, 4)
                convert(l, C0P[2] + 2)
                for t in range(T):
                    rope(l, 1, t)
                convert(l, C0P[2] + 3)
                for i in range(len(IDX_TILES)):
                    for h in range(HEADS):
                        add_index_head(l, i, h)
                if l == 0:
                    ada_group(3, 4, KD)
                convert(l, C0P[3])
                top_rounds(0, 1)
                convert(l, C0P[3] + 1)
                top_rounds(1, 2)
                convert(l, C0P[4] + 1)
                for t in range(T):
                    rope(l, 2, t)
                convert(l, C0P[4] + 2)
                for t in range(T):
                    rope(l, 3, t)
                convert(l, C0P[4] + 3)
                top_rounds(2, 4)
                convert(l, C0P[4] + 4)
                top_rounds(4, 9)
                attention(l)
                if l == 0:
                    take_mod(2, 7)
                    take_mod(3, 4)
                gate_diagonal(l, 0)
                if l == 0:
                    ada_group(4, 0, 4)
                convert(l, WO_P + 5)
                take_gate(l, 0, 5)
                if l == 0:
                    convert(l, WO_P + 6)
                    ada_group(4, 4, KD)
                convert(l, WO_P + 7)
                for t in range(T):
                    residual(l, WO0, t, True)
                convert(l, WO_P + 8)
                if l == 0:
                    take_mod(4, 7)
                if l == 0:
                    h_coefficients(1)
                else:
                    h_coefficients(3)
                last_tiles(l, WO1, 0)
                feed(l, 0)
                if l == 0:
                    h_coefficients(2)
                gate_diagonal(l, 1)
                affine(2 * l + 1, 0)
                affine(2 * l + 1, 1)
                convert(l, DN_P[0] + 5)
                take_gate(l, 1, 4)
                for t in range(2, T):
                    affine(2 * l + 1, t)
                    convert(l, DN_P[0] + 4 + t)
                for half in range(2):
                    q = DN00 + half
                    convert(l, PHASES[q][0] + PHASES[q][1] + (3, 2)[half])
                    for t in range(T):
                        residual(l, q, t, True)
                    if (l, half) == (0, 0):
                        ada_group(6 * DEPTH - 1)
                convert(l, GU_P[1] + 4)
                feed(l, 1)
                if l == 0:
                    take_mod(6 * DEPTH - 1, 7)
                convert(l, DN_P[1] + 5)
                for t in range(T):
                    convert(l, DN_P[1] + 5 + t)
                    residual(l, DN10, t, False)
                convert(l, NP)
                if l + 1 < DEPTH:
                    last_tiles(l, DN11, 4)
                else:
                    for t in range(T):
                        residual(l, DN11, t, False)
                        moments(l, 1, t)
                        output_tile(t)


def weight_pieces(w_in, w_o, w_gate, w_up, w_down):
    a_q, a_k, a_v, b_q, b_k, b_v, i_q, i_k, i_w = np.split(
        w_in, np.cumsum([512, 128, 128, 512, 128, 128, 512, 64]), axis=-1)
    chunks = [i_q, np.concatenate([i_k, b_k, b_v, i_w], -1), paired(a_q, -1),
              np.concatenate([a_k, a_v], -1), paired(b_q, -1)]
    out = np.zeros((DEPTH, NP, P, PW), np.float32)
    w_o = np.concatenate([paired(w_o[:, :512], 1), paired(w_o[:, 512:], 1)], 1)
    for c, w in enumerate(chunks):
        for j in range(CP[c]):
            for kk in range(CK[c]):
                k = j * CK[c] + kk
                out[:, C0P[c] + j, :, kk * CW[c]:(kk + 1) * CW[c]] = w[:, k * P:(k + 1) * P]
    for half in range(2):
        cols = slice(half * HALF, (half + 1) * HALF)
        for k in range(KD):
            out[:, WO_P + 4 * half + k // 2, :, (k % 2) * 512:(k % 2 + 1) * 512] = w_o[:, k * P:(k + 1) * P, cols]
    f0 = 0
    for g in range(2):
        for f in range(FG[g]):
            cols = slice((f0 + f) * P, (f0 + f + 1) * P)
            for i, w in enumerate((w_gate, w_up)):
                out[:, GU_P[g] + 2 * f + i] = w[:, :, cols].reshape(DEPTH, KD, P, P).transpose(0, 2, 1, 3)\
                    .reshape(DEPTH, P, PW)
            for half in range(2):
                out[:, DN_P[g] + half * FG[g] // 2 + f // 2, :, (f % 2) * 512:(f % 2 + 1) * 512] = \
                    w_down[:, cols, half * HALF:(half + 1) * HALF]
        f0 += FG[g]
    return out.reshape(DEPTH * NP, P, PW)


def paired(a, axis):
    axis = axis % a.ndim
    n = a.shape[axis] // HEADS
    s = a.shape
    b = a.reshape(s[:axis] + (KV_HEADS, PAIRS, n) + s[axis + 1:])
    return np.swapaxes(b, axis, axis + 1).reshape(s)


def kernel(x, c, positions, w_ada, b_ada, w_in, attn_sinks, g_a, g_b, w_o,
           ln1_g, ln1_b, w_gate, w_up, w_down, ln2_g, ln2_b):
    import concourse.bacc as bacc
    from concourse.bass_utils import run_bass_kernel_spmd

    def columns(a):
        a = np.asarray(a)
        return np.ascontiguousarray(np.moveaxis(a.reshape(a.shape[:-1] + (-1, P)), -1, 0))

    (x, c, positions, w_ada, b_ada, w_in, attn_sinks, g_a, g_b, w_o, ln1_g, ln1_b, w_gate, w_up, w_down,
     ln2_g, ln2_b) = map(np.asarray, (x, c, positions, w_ada, b_ada, w_in, attn_sinks, g_a, g_b, w_o, ln1_g,
                                      ln1_b, w_gate, w_up, w_down, ln2_g, ln2_b))
    one, zero = np.ones((D_MODEL,), np.float32), np.zeros((D_MODEL,), np.float32)
    rows = np.stack([np.stack([g, b]) for l in range(DEPTH)
                     for g, b in ((ln1_g[l], ln1_b[l]), (ln2_g[l], ln2_b[l]))])
    before = np.concatenate([np.stack([one, zero])[None], rows[:-1]])
    arrays = {
        "x": x.reshape(T, P, D_MODEL),
        "c_col": columns(c[0]),
        "positions": positions.reshape(T, P).T,
        "inv_freq": (ROPE_THETA ** (-np.arange(HD // 2) / (HD // 2))).astype(np.float32)[None],
        "weights": weight_pieces(w_in, w_o, w_gate, w_up, w_down),
        "w_ada": w_ada.reshape(DEPTH, KD, P, 6, PW).transpose(0, 3, 1, 2, 4).reshape(6 * DEPTH, KD, P, PW),
        "b_ada": columns(b_ada.reshape(6 * DEPTH, D_MODEL)),
        "ln_col": columns(before),
        "ln_row": rows,
        "sinks": paired(attn_sinks, 1)[None],
        "g_col": columns(np.stack([paired(g_a, 1), paired(g_b, 1)], 1)),
    }
    nc = bacc.Bacc("TRN2", target_bir_lowering=False, num_devices=1)
    ins, aps = {}, {}
    for name, a in arrays.items():
        a = np.ascontiguousarray(a)
        ins[f"in_{name}"] = a
        aps[name] = nc.dram_tensor(f"in_{name}", a.shape, mybir.dt.from_np(a.dtype), kind="ExternalInput").ap()
    out = nc.dram_tensor("trunk_out", (T, P, D_MODEL), F32, kind="ExternalOutput").ap()
    build_trunk(nc, out=out, **aps)
    r = run_bass_kernel_spmd(nc, [ins], core_ids=[0])
    return r.results[0]["trunk_out"].reshape(1, SEQ, D_MODEL)
```

```python
from contextlib import ExitStack

import numpy as np

import concourse.bass as bass
from concourse import mybir

F32 = mybir.dt.float32
F32R = mybir.dt.float32r
I32 = mybir.dt.int32
ALU = mybir.AluOpType
ACT = mybir.ActivationFunctionType

P = 128
D_MODEL, SEQ, DEPTH = 1024, 512, 2
HD = 64
HEADS = 8
KV_HEADS = 2
PAIRS = HEADS // KV_HEADS
TOPK = min(256, SEQ // 4)
D_FF = ((-(-8 * D_MODEL // 3)) + 255) // 256 * 256
ALPHA = (2.0 * DEPTH) ** 0.25
LN_EPS, RMS_EPS = 1e-5, 1e-6
ROPE_THETA = 10000.0

T = SEQ // P
KD = D_MODEL // P
HALF = D_MODEL // 2
FC = D_FF // P
FG = (12, FC - 12)
PW = 1024

CW = (512, 328, 512, 256, 512)
CK = (2, 2, 2, 4, 2)
CP = tuple(KD // k for k in CK)
C0P = tuple(sum(CP[:c]) for c in range(5))
WO_P = sum(CP)
GU_P = (WO_P + 8, WO_P + 8 + 2 * FG[0] + FG[0])
DN_P = (GU_P[0] + 2 * FG[0], GU_P[1] + 2 * FG[1])
NP = DN_P[1] + FG[1]
RING = 4
assert NP % RING == 0 and NP == 92 and D_MODEL == 1024 and SEQ == 512

PHASES = [(C0P[c], CP[c]) for c in range(5)] + [(WO_P, 4), (WO_P + 4, 4)]
for _g in range(2):
    PHASES += [(DN_P[_g], FG[_g] // 2), (DN_P[_g] + FG[_g] // 2, FG[_g] // 2)]
WO0, WO1, DN00, DN01, DN10, DN11 = range(5, 11)
BANKS = {0: 0, 1: 4, 2: 0, 3: 0, WO0: 0, WO1: 4, DN00: 0, DN01: 4, DN10: 4, DN11: 0}
GU_BANK = (4, 0)

UNITS = [("A", t) for t in range(T)] + [("B", 0), ("B", 1), ("B", 3), ("B", 2)]
IDX_TILES = (3, 2, 1)
WO0_ORDER = (0, 3, 1, 2)
SC_AT = (None, 0, 256, 640)
SC_W = 1152
P_RING = 4
QB_BANK = 5
QB_FREE = 40
PT_RING = 4
DVE_HEADS = (3, 7)
LAG_T, LAG_V = 3, 5
LAG_NORM, LAG_ROOT, LAG_SCALE, LAG_Y, LAG_SPLIT = 6, 7, 8, 11, 12
QB_STEPS = tuple(1 + 7 * n // 3 for n in range(T * CP[4]))
ROPE_AT = tuple(QB_STEPS[CP[4] * t + CP[4] - 1] + 2 for t in range(T))
QB_AT = tuple(r + 3 for r in ROPE_AT)
ASIDE_AT = tuple(range(42, 58, 2))
WO_AT = (42, 47, 52, 57)
MASKS_AT = 40
EARLY_ROUNDS = 3

SH1, SC1, GT1, SH2, SC2, GT2 = range(6)

TAKEN = -3.3e38
CUT = -3.1e38
NEG = -1.0e38


def keys_of(unit):
    kind, t = unit
    lo = max(t - 1, 0) * P if kind == "A" else 0
    return lo, (t + 1) * P


def build_trunk(nc, x, c_col, positions, inv_freq, weights, w_ada, b_ada, ln_col, ln_row, sinks, g_col, out):
    with ExitStack() as ctx:
        def sb(name, shape, dt=F32, on=ctx):
            return on.enter_context(nc.sbuf_tensor(name, shape, dt))

        def sem(name):
            return ctx.enter_context(nc.semaphore(name))

        bank = [ctx.enter_context(nc.psum_tensor(f"bank{i}", [P, 512], F32)) for i in range(8)]

        w_raw = sb("w_raw", [P, RING, PW])
        w_hi = sb("w_hi", [P, RING, PW], F32R)
        w_lo = sb("w_lo", [P, RING, PW], F32R)
        xs = sb("xs", [P, T, D_MODEL])
        hT_hi = sb("hT_hi", [P, KD, SEQ], F32R)
        hT_lo = sb("hT_lo", [P, KD, SEQ], F32R)
        scratch = sb("scratch", [P, PW])
        ada_w = sb("ada_w", [P, RING, PW])
        ada_acc = sb("ada_acc", [P, 2, PW])
        gt_row = sb("gt_row", [P, D_MODEL])
        g_row = sb("g_row", [P, D_MODEL])
        b_row = sb("b_row", [P, D_MODEL])
        ident = sb("ident", [P, P])
        ones = sb("ones", [P, P])
        band = sb("band", [P, 2 * P])
        cos_t = sb("cos_t", [P, T, HD])
        sin_t = sb("sin_t", [P, T, HD])
        cc = sb("cc", [P, 2, KD])
        modb = sb("modb", [P, 6 * DEPTH, KD])
        mod = sb("mod", [P, 6 * DEPTH, KD])
        lnc = sb("lnc", [P, 2 * DEPTH, 2, KD])
        hcoef = sb("hcoef", [P, 2 * DEPTH, 2, KD])
        gcol = sb("gcol", [P, DEPTH, 2, 4])
        nsink = sb("nsink", [P, DEPTH, HEADS])
        stats = sb("stats", [P, T, 2, 6])
        mean_var = sb("mean_var", [P, T, 2])
        rs_in = sb("rs_in", [P, 32])
        rs_out = sb("rs_out", [P, 32])
        minus_half = sb("minus_half", [P, 1])
        mean_sq = sb("mean_sq", [P, 2, 1])
        rowsum = sb("rowsum", [P, 2, HEADS])
        nmax = sb("nmax", [P, 2, HEADS])
        es = sb("es", [P, 2, HEADS])
        recip = sb("recip", [P, 2, HEADS])
        top8 = sb("top8", [P, T, 8])

        with ExitStack() as att:
            pq = sb("pq", [P, 2, T, 512], on=att)
            pk = sb("pk", [P, T, 256], on=att)
            v_b = sb("v_b", [P, T, P + HD], on=att)
            v_a = sb("v_a", [P, T, P + HD], on=att)
            wi = sb("wi", [P, T, HEADS], on=att)
            qT = sb("qT", [P, 2, PAIRS, SEQ], on=att)
            kiT = sb("kiT", [P, SEQ], on=att)
            kT = sb("kT", [P, 2, KV_HEADS, SEQ], on=att)
            scores = sb("scores", [P, SC_W], on=att)
            pT = sb("pT", [P, PT_RING, 512], on=att)
        rel = pq[:, 0]
        prob = pq[:, 1]
        y = gt_row[:].rearrange("p (b n) -> p b n", b=2)
        angles = pq[:, 1, 0:2]
        with ExitStack() as ffn:
            gu_hi = sb("gu_hi", [P, FG[0], SEQ], F32R, on=ffn)
            gu_lo = sb("gu_lo", [P, FG[0], SEQ], F32R, on=ffn)
            silu_g = sb("silu_g", [P, 2, SEQ], on=ffn)
            gu = sb("gu", [P, 2, SEQ], on=ffn)
            ztmp = sb("ztmp", [P, HALF], on=ffn)

        raw_in = [sem(f"raw_in{i}") for i in range(RING)]
        ada_first_in = [sem(f"ada_first_in{i}") for i in range(RING)]
        ada_in = [sem(f"ada_in{i}") for i in range(RING)]
        x_in = [sem(f"x_in{i}") for i in range(T)]
        small_in = sem("small_in")
        row_in = sem("row_in")
        c_in = sem("c_in")
        out_ready = sem("out_ready")
        out_done = sem("out_done")
        consts = sem("consts")
        pool_step = sem("pool_step")
        hi_ready = sem("hi_ready")
        lo_ready = sem("lo_ready")
        piece_used = sem("piece_used")
        tile_done = sem("tile_done")
        x_transposed = sem("x_transposed")
        coef_ready = sem("coef_ready")
        h_scaled_dve = sem("h_scaled_dve")
        h_scaled_act = sem("h_scaled_act")
        h_hi = sem("h_hi")
        h_lo = sem("h_lo")
        proj_evac = sem("proj_evac")
        keys_zeroed = sem("keys_zeroed")
        y_normed = sem("y_normed")
        y_squared = sem("y_squared")
        roped = sem("roped")
        rotated = sem("rotated")
        tables_ready = sem("tables_ready")
        qk_transposed = sem("qk_transposed")
        qk_ready = sem("qk_ready")
        idx_scored = sem("idx_scored")
        relu_done = sem("relu_done")
        idx_acc = sem("idx_acc")
        scored = sem("scored")
        masked = sem("masked")
        probs = sem("probs")
        sink_diff = sem("sink_diff")
        sink_exp = sem("sink_exp")
        p_transposed = sem("p_transposed")
        pT_act = sem("pT_act")
        pT_dve = sem("pT_dve")
        av_done = sem("av_done")
        rs_asked = sem("rs_asked")
        rs_done = sem("rs_done")
        y_ready = sem("y_ready")
        y_transposed = sem("y_transposed")
        yT_hi = sem("yT_hi")
        yT_lo = sem("yT_lo")
        z_done = sem("z_done")
        xhat_ready = sem("xhat_ready")
        affine_done = sem("affine_done")
        gate_read = sem("gate_read")
        gu_ready = sem("gu_ready")
        gu_hi_ready = sem("gu_hi_ready")
        gu_lo_ready = sem("gu_lo_ready")
        ada_used = sem("ada_used")
        mod_taken = sem("mod_taken")
        mod_reduced = sem("mod_reduced")
        gt_diag = sem("gt_diag")
        gt_spread = sem("gt_spread")
        gt_taken = sem("gt_taken")
        dve_step = sem("dve_step")
        rope_angle = sem("rope_angle")
        rope_table = sem("rope_table")

        def converted(l, p):
            return l * NP + p + 1

        def used(l, p):
            return RING + l * NP + p + 1

        def gained(p):
            l, j = p // NP, (p % NP - WO_P) % 4
            return [(slice(kk * 512, (kk + 1) * 512), gcol[:, l, j // 2, (2 * j + kk) % 4:(2 * j + kk) % 4 + 1])
                    for kk in range(2)]

        def slot(l, p):
            return (l * NP + p) % RING

        def place(q, t):
            return WO0_ORDER.index(t) if q == WO0 else t

        def wait_phase(eng, l, q, t):
            if place(q, t) < T - 1:
                eng.wait_ge(tile_done, l * 33 + 3 * q + place(q, t) + 1)
            else:
                eng.wait_ge(piece_used, used(l, PHASES[q][0] + PHASES[q][1] - 1))

        def dve_chunks(stage, t):
            return 0 if stage > 0 and t < 2 else 4

        def scaled_dve(stage, t):
            return t + 1 if stage == 0 else T + 2 * (stage - 1) + max(t - 1, 0)

        def at_tile(stage, t):
            return T * stage + t + 1

        def at_chunk(l, c, t):
            return 20 * l + 4 * c + t + 1

        def at_head(l, u, h):
            return 64 * l + 8 * u + h + 1

        def at_unit(l, u):
            return 8 * l + u + 1

        def at_z(l, q, t):
            return 24 * l + 4 * (q - WO0) + t + 1

        def rs_index(l, r):
            return 16 * l + r

        def qk_bank(c, t):
            return 2 if c == 4 else 4 + t

        def gu_before(l, g):
            return l * FC + g * FG[0]

        def s_bank(n):
            return bank[3 + n % 2] if n < QB_FREE else bank[(QB_BANK, 3, 4)[(n - QB_FREE) % 3]]

        def on_dve(u, h):
            return u >= 4 and h in DVE_HEADS

        dve_heads = 4 * len(DVE_HEADS)

        def wait_pT(eng, l, u, h):
            flat = [(a, b) for a in range(8) for b in range(HEADS) if (a, b) <= (u, h)]
            n_dve = sum(on_dve(a, b) for a, b in flat)
            if on_dve(u, h):
                eng.wait_ge(pT_dve, l * dve_heads + n_dve)
            else:
                eng.wait_ge(pT_act, l * (64 - dve_heads) + len(flat) - n_dve)

        def back(u, h, n):
            i = 8 * u + h - n
            return None if i < 0 else (i // 8, i % 8)

        def rope_views(c, t):
            heads = (8, 4, 8, 2, 8)[c]
            v = pk[:, t, 0:heads * HD] if c in (1, 3) else pq[:, (c // 2) % 2, t, :]
            return heads, [a.rearrange("p (h d) -> p h d", h=heads)
                           for a in (v, scratch[:, 0:heads * HD], scratch[:, 512:512 + heads * HD])]

        def rotate(engine, c, t):
            heads, (v, a, b) = rope_views(c, t)
            n = HD // 2

            def over_heads(table, d0, d1):
                return table[:, t, d0:d1].unsqueeze(1).to_broadcast([P, heads, d1 - d0])

            engine.tensor_tensor(b[:, :, 0:n], v[:, :, n:HD], over_heads(sin_t, 0, n), ALU.mult)
            engine.tensor_tensor(b[:, :, n:HD], v[:, :, 0:n], over_heads(sin_t, n, HD), ALU.mult)
            return engine.tensor_tensor(a, v, over_heads(cos_t, 0, HD), ALU.mult)

        def rotate_sum(engine, c, t):
            _, (v, a, b) = rope_views(c, t)
            return engine.tensor_tensor(v, a, b, ALU.add)

        block = ctx.enter_context(nc.Block())

        @block.sync
        def _(sp):
            for n in range(2 * KD):
                if n >= RING:
                    sp.wait_ge(ada_used, n - RING + 1)
                sp.dma_start(ada_w[:, n % RING, :], w_ada[n // KD, n % KD]).then_inc(ada_first_in[n % RING], 16)
            for t in range(T):
                sp.dma_start(xs[:, t, :], x[t]).then_inc(x_in[t], 16)
            for s in range(RING):
                sp.dma_start(w_raw[:, s, :], weights[s]).then_inc(raw_in[s], 16)
            with sp.Fori(1, DEPTH * NP // RING) as i:
                for s in range(RING):
                    sp.wait_ge(lo_ready, i * RING + (s - RING + 1))
                    sp.dma_start(w_raw[:, s, :], weights[i * RING + s]).then_inc(raw_in[s], 16)
            for t in range(T):
                for half in range(2):
                    sp.wait_ge(out_ready, 2 * t + half + 1)
                    cols = slice(half * HALF, (half + 1) * HALF)
                    sp.dma_start(out[t][:, cols], xs[:, t, cols]).then_inc(out_done, 16)
            sp.wait_ge(out_done, 16 * 2 * T)

        @block.gpsimd
        def _(pool):
            fetched = [2 * KD]

            def ada_fetch(upto):
                while fetched[0] < upto:
                    n = fetched[0]
                    if n >= RING:
                        pool.wait_ge(ada_used, n - RING + 1)
                    pool.dma_start(ada_w[:, n % RING, :], w_ada[n // KD, n % KD]).then_inc(ada_in[n % RING], 16)
                    fetched[0] += 1

            def rsqrt(l, r):
                n = rs_index(l, r)
                pool.wait_ge(rs_asked, n + 1)
                nc.gpsimd.tensor_tensor(rs_out[:, n:n + 1], rs_in[:, n:n + 1], minus_half[:], ALU.pow)\
                    .then_inc(rs_done, 1)

            def rope(l, c, t):
                pool.wait_ge(proj_evac, at_chunk(l, c, t))
                if at_chunk(l, c, t) > 1:
                    pool.wait_ge(roped, at_chunk(l, c, t) - 1)
                rotate(nc.gpsimd, c, t).then_inc(rotated, 1)
                pool.wait_ge(rotated, 2 * T * l + T * (c // 4) + t + 1)
                rotate_sum(nc.gpsimd, c, t).then_inc(roped, 1)

            def ln_rows(stage):
                if stage > 1:
                    pool.wait_ge(affine_done, at_tile(stage - 2, T - 1))
                pool.dma_start(g_row[:], ln_row[stage - 1, 0:1, :].to_broadcast([P, D_MODEL])).then_inc(row_in, 16)
                pool.dma_start(b_row[:], ln_row[stage - 1, 1:2, :].to_broadcast([P, D_MODEL])).then_inc(row_in, 16)

            nc.gpsimd.memset(minus_half[:], -0.5).then_inc(pool_step, 1)
            nc.gpsimd.memset(ident[:], 0.0).then_inc(pool_step, 1)
            nc.gpsimd.memset(band[:], 0.0).then_inc(pool_step, 1)
            nc.gpsimd.memset(ones[:], 1.0).then_inc(consts, 1)
            pool.wait_ge(pool_step, 3)
            nc.gpsimd.affine_select(out=ident[:], in_=ident[:], compare_op=ALU.not_equal, fill=1.0, base=0,
                                    pattern=[[-1, P]], channel_multiplier=1).then_inc(consts, 1)
            nc.gpsimd.affine_select(out=band[:, 0:P], in_=band[:, 0:P], compare_op=ALU.is_ge, fill=NEG, base=-1,
                                    pattern=[[1, P]], channel_multiplier=-1).then_inc(consts, 1)
            nc.gpsimd.affine_select(out=band[:, P:2 * P], in_=band[:, P:2 * P], compare_op=ALU.is_ge, fill=NEG,
                                    base=0, pattern=[[-1, P]], channel_multiplier=1).then_inc(consts, 1)
            for l in range(DEPTH):
                if l == 0:
                    ada_fetch(2 * KD + 4 + RING)
                    pool.wait_ge(tables_ready, 1)
                for t in range(T):
                    rope(l, 0, t)
                    if l == 0:
                        ada_fetch(3 * KD + t + 1)
                pool.wait_ge(roped, at_chunk(l, 0, T - 1))
                for g in range(KV_HEADS):
                    other = slice((1 - g) * HD, (2 - g) * HD)
                    nc.gpsimd.memset(kT[other, :, g, :], 0.0).then_inc(keys_zeroed, 1)
                    pool.wait_ge(keys_zeroed, 2 * l + g + 1)
                if l == 0:
                    ada_fetch(4 * KD + RING)
                for i in range(64 + LAG_ROOT):
                    if i in ASIDE_AT and l == 0:
                        ada_fetch(4 * KD + RING + ASIDE_AT.index(i) + 1)
                    if i in ROPE_AT:
                        rope(l, 4, ROPE_AT.index(i))
                    if (i - LAG_ROOT) % 8 == 7 and i > LAG_ROOT:
                        rsqrt(l, (i - LAG_ROOT) // 8)
                ln_rows(2 * l + 1)
                for t in range(T):
                    rsqrt(l, 8 + t)
                if l == 0:
                    base = 5 * KD + RING
                    with pool.Fori(0, FG[0] // 2) as i:
                        for j in range(KD):
                            pool.wait_ge(ada_used, i * KD + (base + j - RING + 1))
                            pool.dma_start(ada_w[:, j % RING, :], w_ada[i + (base + j) // KD, (base + j) % KD])\
                                .then_inc(ada_in[j % RING], 16)
                    fetched[0] = base + KD * FG[0] // 2
                    ada_fetch(6 * DEPTH * KD)
                ln_rows(2 * l + 2)
                for t in range(T):
                    rsqrt(l, 12 + t)

        @block.tensor
        def _(pe):
            nc.tensor.sem_inc(piece_used, RING)

            def wait_piece(l, p):
                pe.wait_ge(hi_ready, converted(l, p))
                pe.wait_ge(lo_ready, converted(l, p))

            def split_product(dst, a_hi, a_lo, b_hi, b_lo, first, last):
                pe.matmul(dst, a_hi, b_hi, start=first, stop=False)
                pe.matmul(dst, a_hi, b_lo, start=False, stop=False)
                return pe.matmul(dst, a_lo, b_hi, start=False, stop=last)

            def transpose_x(stage, t, b0):
                if stage == 0:
                    pe.wait_ge(x_in[t], 16)
                    pe.wait_ge(consts, 4)
                else:
                    pe.wait_ge(xhat_ready, at_tile(stage - 1, t))
                if t >= 2:
                    pe.wait_ge(h_scaled_dve, scaled_dve(stage, t - 2))
                    pe.wait_ge(h_scaled_act, at_tile(stage, t - 2))
                for k in range(KD):
                    m = pe.transpose(bank[b0 + 2 * (t % 2) + k // 4][:, (k % 4) * P:(k % 4 + 1) * P],
                                     xs[:, t, k * P:(k + 1) * P], ident[:])
                m.then_inc(x_transposed, 1)

            def reduce_mod(g, b):
                if g == 0:
                    pe.wait_ge(consts, 4)
                pe.wait_ge(ada_used, (g + 1) * KD)
                for k in range(KD):
                    m = pe.matmul(bank[b][:, k:k + 1], ada_acc[:, g % 2, k * P:(k + 1) * P], ones[:, 0:1],
                                  start=True, stop=True)
                m.then_inc(mod_reduced, 1)

            def spread_gate(l, which, b):
                pe.wait_ge(gt_diag, 2 * l + which + 1)
                for half in range(2):
                    m = pe.matmul(bank[b + half][:], ones[:], scratch[:, half * 512:(half + 1) * 512],
                                  start=True, stop=True)
                m.then_inc(gt_spread, 1)

            def accumulate(l, q, j0, j1, a_hi, a_lo, nk, width, wait_tile):
                p0, n = PHASES[q]
                for j in range(j0, j1):
                    wait_piece(l, p0 + j)
                    s = slot(l, p0 + j)
                    for t in range(T):
                        if j == 0:
                            wait_tile(t)
                        rows = slice(t * P, (t + 1) * P)
                        for kk in range(nk):
                            k = j * nk + kk
                            cols = slice(kk * width, (kk + 1) * width)
                            m = split_product(bank[BANKS[q] + t][:, 0:width], a_hi[:, k, rows], a_lo[:, k, rows],
                                              w_hi[:, s, cols], w_lo[:, s, cols],
                                              j == 0 and kk == 0, j == n - 1 and kk == nk - 1)
                        if t == T - 1:
                            m.then_inc(piece_used, 1)
                        elif j == n - 1:
                            m.then_inc(tile_done, 1)

            def finish_tile(l, q, t, a_hi, a_lo, wait_tile):
                p0, n = PHASES[q]
                rows = slice(t * P, (t + 1) * P)
                if n == 4:
                    wait_tile(t)
                for j in range(n - 4, n):
                    if t == 0:
                        wait_piece(l, p0 + j)
                    s = slot(l, p0 + j)
                    for kk in range(2):
                        k = 2 * j + kk
                        cols = slice(kk * 512, (kk + 1) * 512)
                        m = split_product(bank[BANKS[q] + t][:], a_hi[:, k, rows], a_lo[:, k, rows],
                                          w_hi[:, s, cols], w_lo[:, s, cols], k == 0, k == 2 * n - 1)
                    if t == T - 1:
                        m.then_inc(piece_used, 1)
                if t < T - 1:
                    m.then_inc(tile_done, 1)

            def project_first(l):
                p0, n = PHASES[0]
                for pair in range(2):
                    for j in range(n):
                        s = slot(l, p0 + j)
                        if pair == 0:
                            wait_piece(l, p0 + j)
                        for t in (2 * pair, 2 * pair + 1):
                            if j == 0:
                                pe.wait_ge(h_lo, at_tile(2 * l, t))
                                if l > 0:
                                    pe.wait_ge(z_done, at_z(l - 1, DN11, t))
                            rows = slice(t * P, (t + 1) * P)
                            for kk in range(CK[0]):
                                k = j * CK[0] + kk
                                cols = slice(kk * CW[0], (kk + 1) * CW[0])
                                m = split_product(bank[BANKS[0] + t][:], hT_hi[:, k, rows], hT_lo[:, k, rows],
                                                  w_hi[:, s, cols], w_lo[:, s, cols], k == 0, k == KD - 1)
                            if t == T - 1:
                                m.then_inc(piece_used, 1)
                            elif j == n - 1:
                                m.then_inc(tile_done, 1)
                        if pair == 0 and j == 1:
                            transpose_x(2 * l, T - 1, 4)

            def project(l, c, j0, j1):
                def wait_tile(t):
                    if c == 1:
                        pe.wait_ge(h_scaled_dve, scaled_dve(2 * l, T - 1))
                        pe.wait_ge(h_scaled_act, at_tile(2 * l, T - 1))
                    else:
                        pe.wait_ge(proj_evac, at_chunk(l, (None, None, 0, 2, 3)[c], t))
                accumulate(l, c, j0, j1, hT_hi, hT_lo, CK[c], CW[c], wait_tile)

            def wait_bank2(l, before):
                kind, n = before
                if kind == "y":
                    pe.wait_ge(yT_hi, at_unit(l, n))
                    pe.wait_ge(yT_lo, at_unit(l, n))
                elif kind == "qb":
                    pe.wait_ge(qk_ready, at_chunk(l, 4, n))
                else:
                    pe.wait_ge(proj_evac, at_chunk(l, 3, T - 1))

            def transpose_qk(l, c, t, before=None):
                pe.wait_ge(roped, at_chunk(l, c, t))
                if c == 0:
                    pe.wait_ge(proj_evac, at_chunk(l, 1, t))
                elif c == 2:
                    pe.wait_ge(relu_done, 24 * (l + 1))
                elif c < 4:
                    pe.wait_ge(qk_ready, at_chunk(l, c - 1, t))
                else:
                    wait_bank2(l, before)
                for j in range((4, 2, 4, 1, 4)[c]):
                    src = pk[:, t, j * P:(j + 1) * P] if c in (1, 3) else pq[:, (c // 2) % 2, t, j * P:(j + 1) * P]
                    m = pe.transpose(bank[qk_bank(c, t)][:, j * P:(j + 1) * P], src, ident[:])
                m.then_inc(qk_transposed, 1)

            def index_scores(l):
                for i, t in enumerate(IDX_TILES):
                    for h in range(HEADS):
                        n = 24 * l + 8 * i + h
                        if i == 0 and h < 4:
                            pe.wait_ge(qk_ready, at_chunk(l, 1, T - 1))
                        else:
                            pe.wait_ge(relu_done, n - 3)
                        g = 64 * (h % 2)
                        pe.matmul(bank[4 + h % 4][:, 0:(t + 1) * P], qT[g:g + HD, 0, h // 2, t * P:(t + 1) * P],
                                  kiT[g:g + HD, 0:(t + 1) * P], start=True, stop=True).then_inc(idx_scored, 1)

            def head_scores(l, u, h):
                kind, t = UNITS[u]
                lo, hi = keys_of(UNITS[u])
                n = 8 * u + h
                if n < 2:
                    pe.wait_ge(qk_ready, at_chunk(l, 3, T - 1))
                    pe.wait_ge(proj_evac, at_chunk(l, 3, T - 1))
                else:
                    pe.wait_ge(masked, at_head(l, u, h) - (2 if n < QB_FREE else 3))
                if n == QB_FREE:
                    pe.wait_ge(proj_evac, at_chunk(l, 4, T - 1))
                if kind == "B" and h == 0:
                    pe.wait_ge(qk_ready, at_chunk(l, 4, t))
                if n == 0:
                    pe.wait_ge(keys_zeroed, 2 * (l + 1))
                a = int(kind == "A")
                pe.matmul(s_bank(n)[:, 0:hi - lo], qT[:, a, h // 2, t * P:(t + 1) * P],
                          kT[:, a, h % 2, lo:hi], start=True, stop=True).then_inc(scored, 1)

            def transpose_p(l, u, h):
                lo, hi = keys_of(UNITS[u])
                pe.wait_ge(probs, at_head(l, u, h))
                if l == 0 and (u, h) < (0, 2):
                    pe.wait_ge(mod_taken, 4)
                if before := back(u, h, 2):
                    wait_pT(pe, l, *before)
                n = 8 * u + h
                for b in range((hi - lo) // P):
                    m = pe.transpose(bank[6 + h % 2][:, b * P:(b + 1) * P],
                                     prob[:, n % P_RING, b * P:(b + 1) * P], ident[:])
                m.then_inc(p_transposed, 1)

            def head_values(l, u, h):
                kind, t = UNITS[u]
                lo, hi = keys_of(UNITS[u])
                wait_pT(pe, l, u, h)
                if h == 0:
                    if u >= 2:
                        pe.wait_ge(y_ready, at_unit(l, u - 2))
                    else:
                        pe.wait_ge(proj_evac, at_chunk(l, 3, T - 1))
                v = v_a if kind == "A" else v_b
                g = 64 * (h % 2)
                nb = (hi - lo) // P
                w = P if h < HEADS - 1 else HD
                for b in range(nb):
                    m = pe.matmul(bank[u % 2][:, h * HD:h * HD + w], pT[:, h % PT_RING, b * P:(b + 1) * P],
                                  v[:, lo // P + b, g:g + w], start=b == 0, stop=b == nb - 1)
                m.then_inc(av_done, 1)

            def transpose_y(l, u, before):
                pe.wait_ge(y_ready, at_unit(l, u))
                wait_bank2(l, before)
                for j in range(4):
                    m = pe.transpose(bank[2][:, j * P:(j + 1) * P], y[:, u % 2, j * P:(j + 1) * P], ident[:])
                m.then_inc(y_transposed, 1)

            def project_qb(l, t, j):
                p = PHASES[4][0] + j
                if t == 0:
                    wait_piece(l, p)
                if j == 0 and t > 0:
                    pe.wait_ge(proj_evac, at_chunk(l, 4, t - 1))
                rows = slice(t * P, (t + 1) * P)
                s = slot(l, p)
                for kk in range(CK[4]):
                    k = j * CK[4] + kk
                    cols = slice(kk * CW[4], (kk + 1) * CW[4])
                    m = split_product(bank[QB_BANK][:], hT_hi[:, k, rows], hT_lo[:, k, rows],
                                      w_hi[:, s, cols], w_lo[:, s, cols], k == 0, k == KD - 1)
                if t == T - 1:
                    m.then_inc(piece_used, 1)
                elif j == CP[4] - 1:
                    m.then_inc(tile_done, 1)

            def out_first(l, t):
                p0, n = PHASES[WO0]
                pe.wait_ge(yT_lo, at_unit(l, UNITS.index(("B", t))))
                if t < 2:
                    pe.wait_ge(y_squared, at_unit(l, 6 + t))
                elif t == 3:
                    pe.wait_ge(masked, at_head(l, 7, 7))
                rows = slice(t * P, (t + 1) * P)
                for j in range(n):
                    if t == WO0_ORDER[0]:
                        wait_piece(l, p0 + j)
                    s = slot(l, p0 + j)
                    for kk in range(2):
                        k = 2 * j + kk
                        cols = slice(kk * 512, (kk + 1) * 512)
                        m = split_product(bank[t][:], hT_hi[:, k, rows], hT_lo[:, k, rows],
                                          w_hi[:, s, cols], w_lo[:, s, cols], k == 0, k == KD - 1)
                    if t == WO0_ORDER[-1]:
                        m.then_inc(piece_used, 1)
                if t != WO0_ORDER[-1]:
                    m.then_inc(tile_done, 1)

            def attention(l):
                in_bank2 = ("chunk", 3)
                for i in range(64 + LAG_Y):
                    if i < 64:
                        head_scores(l, i // 8, i % 8)
                    if 0 <= i - LAG_T < 64:
                        transpose_p(l, (i - LAG_T) // 8, (i - LAG_T) % 8)
                    if i in QB_STEPS:
                        project_qb(l, QB_STEPS.index(i) // CP[4], QB_STEPS.index(i) % CP[4])
                    if 0 <= i - LAG_V < 64:
                        head_values(l, (i - LAG_V) // 8, (i - LAG_V) % 8)
                    if i - 64 - LAG_V in (0, 1):
                        out_first(l, WO0_ORDER[i - 64 - LAG_V])
                    if i in QB_AT:
                        transpose_qk(l, 4, QB_AT.index(i), in_bank2)
                        in_bank2 = ("qb", QB_AT.index(i))
                    if (i - LAG_Y) % 8 == 7 and i > LAG_Y:
                        transpose_y(l, (i - LAG_Y) // 8, in_bank2)
                        in_bank2 = ("y", (i - LAG_Y) // 8)

            def gate_up(l, g):
                s0 = slot(l, GU_P[g])
                b0 = GU_BANK[g]

                def wait_turn(j, i):
                    pe.wait_ge(hi_ready, i * 4 + converted(l, GU_P[g] + j))
                    pe.wait_ge(lo_ready, i * 4 + converted(l, GU_P[g] + j))
                    pe.wait_ge(gate_read if j % 2 == 0 else gu_ready, i * 2 + (gu_before(l, g) + j // 2 + 1))

                def product(j, cols):
                    s = (s0 + j) % RING
                    for k in range(KD):
                        w = slice(k * P, (k + 1) * P)
                        m = split_product(bank[b0 + j][:, cols], w_hi[:, s, w], w_lo[:, s, w],
                                          hT_hi[:, k, cols], hT_lo[:, k, cols], k == 0, k == KD - 1)
                    return m

                def reduce_ada(i):
                    pe.wait_ge(ada_used, i * KD + 6 * KD)
                    for k in range(KD):
                        m = pe.matmul(bank[0][:, k:k + 1], ada_acc[:, 1, k * P:(k + 1) * P], ones[:, 0:1],
                                      start=True, stop=True)
                    m.then_inc(mod_reduced, 1)

                if g == 0:
                    for half in range(2):
                        pe.wait_ge(h_lo, at_tile(2 * l + 1, 2 * half + 1))
                        for j in range(4):
                            if half == 0:
                                wait_turn(j, 0)
                                pe.wait_ge(z_done, at_z(l, WO1, j))
                            m = product(j, slice(half * 256, (half + 1) * 256))
                            if half == 1:
                                m.then_inc(piece_used, 1)
                            elif j == 1:
                                transpose_x(2 * l + 1, T - 1, 0)
                    if l == 0:
                        reduce_ada(0)
                else:
                    pe.wait_ge(z_done, at_z(l, DN00, T - 1))
                with pe.Fori(1 - g, FG[g] // 2) as i:
                    for j in range(4):
                        wait_turn(j, i)
                        product(j, slice(0, SEQ)).then_inc(piece_used, 1)
                    if (l, g) == (0, 0):
                        reduce_ada(i)

            def down(l, g, half):
                q = DN00 + 2 * g + half
                last = (g, half) == (1, 1)

                def wait_tile(t):
                    if half == 0 and t == 0:
                        pe.wait_ge(gu_lo_ready, gu_before(l, g) + FG[g])
                    if q == DN00 and t == 0:
                        pe.wait_ge(h_scaled_dve, scaled_dve(2 * l + 1, T - 1))
                        pe.wait_ge(h_scaled_act, at_tile(2 * l + 1, T - 1))
                        pe.wait_ge(z_done, at_z(l, WO0, T - 1))
                        pe.wait_ge(mod_taken, 5 + FG[0] // 2)
                    elif q in (DN01, DN11) and t == 0:
                        pe.wait_ge(gt_taken, 2 * l + 2)
                        pe.wait_ge(gu_ready, gu_before(l, g) + FG[g] + 2)
                        pe.wait_ge(gate_read, gu_before(l, g) + FG[g] + 2)
                    elif q == DN10:
                        pe.wait_ge(z_done, at_z(l, DN01, t))
                        if t == T - 1:
                            pe.wait_ge(mod_taken, 6 * DEPTH)

                if q == DN00:
                    accumulate(l, q, 0, 2, gu_hi, gu_lo, 2, 512, wait_tile)
                    pe.wait_ge(gu_ready, gu_before(l, g) + FG[g] + 2)
                    pe.wait_ge(gate_read, gu_before(l, g) + FG[g] + 2)
                    spread_gate(l, 1, 4)
                if not last:
                    accumulate(l, q, 2 if q == DN00 else 0, PHASES[q][1], gu_hi, gu_lo, 2, 512, wait_tile)
                    return
                accumulate(l, q, 0, PHASES[q][1] - 4, gu_hi, gu_lo, 2, 512, wait_tile)
                for t in range(T):
                    finish_tile(l, q, t, gu_hi, gu_lo, wait_tile)
                    if l + 1 < DEPTH and t > 0:
                        transpose_x(2 * l + 2, t - 1, 4)

            reduce_mod(0, 0)
            reduce_mod(1, 1)
            for t in range(T - 1):
                transpose_x(0, t, 4)
            for l in range(DEPTH):
                project_first(l)
                project(l, 1, 0, 4)
                project(l, 2, 0, 2)
                for t in range(T):
                    transpose_qk(l, 0, t)
                for t in range(T):
                    transpose_qk(l, 1, t)
                index_scores(l)
                project(l, 2, 2, 4)
                project(l, 3, 0, 2)
                for t in range(T):
                    transpose_qk(l, 2, t)
                for t in range(T):
                    transpose_qk(l, 3, t)
                if l == 0:
                    pe.wait_ge(qk_ready, at_chunk(l, 3, T - 1))
                    reduce_mod(2, 6)
                    reduce_mod(3, 7)
                attention(l)

                def wait_wo1(t):
                    if t == 0:
                        pe.wait_ge(gt_taken, 2 * l + 1)
                        pe.wait_ge(mod_taken, 4)
                        pe.wait_ge(masked, at_head(l, 7, 7))
                        wait_pT(pe, l, 7, 6)
                        wait_pT(pe, l, 7, 7)
                    if l == 0 and t == 3:
                        pe.wait_ge(mod_taken, 5)

                out_first(l, WO0_ORDER[2])
                pe.wait_ge(masked, at_head(l, 7, 7))
                wait_pT(pe, l, 7, 6)
                wait_pT(pe, l, 7, 7)
                spread_gate(l, 0, 5)
                out_first(l, WO0_ORDER[3])
                if l == 0:
                    reduce_mod(4, 7)
                for t in range(T):
                    finish_tile(l, WO1, t, hT_hi, hT_lo, wait_wo1)
                    if t == 0:
                        pe.wait_ge(z_done, at_z(l, WO0, T - 1))
                    else:
                        transpose_x(2 * l + 1, t - 1, 0)
                for g in range(2):
                    gate_up(l, g)
                    if (l, g) == (0, 1):
                        reduce_mod(6 * DEPTH - 1, 7)
                    down(l, g, 0)
                    down(l, g, 1)

        @block.scalar
        def _(act):
            conv = [0]

            def convert(l, upto):
                while conv[0] < min(l * NP + upto, DEPTH * NP):
                    p = conv[0]
                    act.wait_ge(raw_in[p % RING], 16 * (p // RING + 1))
                    act.wait_ge(piece_used, p + 1)
                    if WO_P <= p % NP < WO_P + 8:
                        for cols, gain in gained(p):
                            m = nc.scalar.activation(w_hi[:, p % RING, cols], w_raw[:, p % RING, cols], ACT.Copy,
                                                     scale=gain)
                    else:
                        m = nc.scalar.activation(w_hi[:, p % RING, :], w_raw[:, p % RING, :], ACT.Copy)
                    m.then_inc(hi_ready, 1)
                    conv[0] += 1

            def build_h(stage, t, b0, upto):
                act.wait_ge(coef_ready, stage + 1)
                act.wait_ge(x_transposed, at_tile(stage, t))
                if stage > 0 or t > 0:
                    act.wait_ge(h_lo, at_tile(stage, t) - 1)
                    act.wait_ge(h_hi, at_tile(stage, t) - 1)
                if t == 0 and stage % 2 == 1:
                    act.wait_ge(yT_lo, at_unit(stage // 2, 7))
                    act.wait_ge(gt_spread, 2 * (stage // 2) + 1)
                elif t == 0 and stage > 0:
                    act.wait_ge(gt_spread, stage)
                for k in range(dve_chunks(stage, t), KD):
                    m = nc.scalar.activation(scratch[:, k * P:(k + 1) * P],
                                             bank[b0 + 2 * (t % 2) + k // 4][:, (k % 4) * P:(k % 4 + 1) * P],
                                             ACT.Identity, scale=hcoef[:, stage, 0, k:k + 1],
                                             bias=hcoef[:, stage, 1, k:k + 1])
                m.then_inc(h_scaled_act, 1)
                convert(stage // 2, upto)
                act.wait_ge(h_scaled_act, at_tile(stage, t))
                act.wait_ge(h_scaled_dve, scaled_dve(stage, t))
                nc.scalar.activation(hT_hi[:, :, t * P:(t + 1) * P],
                                     scratch[:].rearrange("p (k s) -> p k s", k=KD), ACT.Copy).then_inc(h_hi, 1)

            def evacuate(l, c, t):
                wait_phase(act, l, c, t)
                src = bank[QB_BANK if c == 4 else BANKS[c] + t]
                if c in (0, 2, 4):
                    if c == 4:
                        act.wait_ge(idx_acc, 24 * (l + 1))
                    elif l > 0 and c == 0:
                        act.wait_ge(qk_transposed, at_chunk(l - 1, 4, t))
                    elif l > 0:
                        act.wait_ge(p_transposed, 64 * l)
                    nc.scalar.activation(pq[:, (c // 2) % 2, t, :], src[:], ACT.Copy).then_inc(proj_evac, 1)
                elif c == 1:
                    if l > 0:
                        act.wait_ge(qk_transposed, at_chunk(l - 1, 3, t))
                    for d in range(2):
                        nc.scalar.activation(pk[:, t, d * HD:(d + 1) * HD], src[:, 0:HD], ACT.Copy)
                    nc.scalar.activation(pk[:, t, P:2 * P], src[:, HD:HD + P], ACT.Copy)
                    nc.scalar.activation(v_b[:, t, 0:P], src[:, HD + P:HD + 2 * P], ACT.Copy)
                    nc.scalar.activation(v_b[:, t, P:P + HD], src[:, HD + P:2 * HD + P], ACT.Copy)
                    nc.scalar.activation(wi[:, t, :], src[:, HD + 2 * P:HD + 2 * P + HEADS], ACT.Copy,
                                         scale=HEADS ** -0.5 * HD ** -0.5).then_inc(proj_evac, 1)
                else:
                    act.wait_ge(qk_transposed, at_chunk(l, 1, t))
                    nc.scalar.activation(pk[:, t, 0:P], src[:, 0:P], ACT.Copy)
                    nc.scalar.activation(v_a[:, t, 0:P], src[:, P:2 * P], ACT.Copy)
                    nc.scalar.activation(v_a[:, t, P:P + HD], src[:, P:P + HD], ACT.Copy).then_inc(proj_evac, 1)

            def copy_qk(l, c, t):
                act.wait_ge(qk_transposed, at_chunk(l, c, t))
                if c == 4 and t == 0:
                    act.wait_ge(idx_scored, 24 * (l + 1))
                n = (4, 2, 4, 1, 4)[c]
                cols = slice(t * P, (t + 1) * P)
                if c in (1, 3):
                    src = bank[qk_bank(c, t)]
                    if c == 1:
                        nc.scalar.activation(kiT[:, cols], src[:, 0:P], ACT.Copy)
                    for g in range(KV_HEADS):
                        half = slice(g * HD, (g + 1) * HD)
                        m = nc.scalar.activation(kT[half, c // 2, g, cols], src[half, (n - 1) * P:n * P], ACT.Copy)
                    m.then_inc(qk_ready, 1)
                    return
                dst = qT[:, (c // 2) % 2, :, cols]
                nc.scalar.activation(dst, bank[qk_bank(c, t)][:, 0:n * P].rearrange("p (j s) -> p j s", j=n), ACT.Copy)\
                    .then_inc(qk_ready, 1)

            def relu(l, i, h):
                n = 24 * l + 8 * i + h
                act.wait_ge(idx_scored, n + 1)
                if 8 * i + h >= P_RING:
                    act.wait_ge(idx_acc, n - P_RING + 1)
                else:
                    act.wait_ge(qk_transposed, at_chunk(l, 0, T - 1))
                w = (IDX_TILES[i] + 1) * P
                nc.scalar.activation(rel[:, (8 * i + h) % P_RING, 0:w], bank[4 + h % 4][:, 0:w], ACT.Relu)\
                    .then_inc(relu_done, 1)

            def exponential(l, u, h):
                lo, hi = keys_of(UNITS[u])
                n = 8 * u + h
                act.wait_ge(masked, at_head(l, u, h))
                p = prob[:, n % P_RING, 0:hi - lo]
                nc.scalar.activation(p, p, ACT.Exp, scale=-1.0, bias=nmax[:, u % 2, h:h + 1],
                                     accum_out=rowsum[:, u % 2, h:h + 1]).then_inc(probs, 1)

            def copy_p(l, u, h):
                lo, hi = keys_of(UNITS[u])
                act.wait_ge(p_transposed, at_head(l, u, h))
                if before := back(u, h, PT_RING):
                    act.wait_ge(av_done, at_head(l, *before))
                nc.scalar.activation(pT[:, h % PT_RING, 0:hi - lo], bank[6 + h % 2][:, 0:hi - lo], ACT.Copy)\
                    .then_inc(pT_act, 1)

            def sink_weight(l, u):
                act.wait_ge(sink_diff, 4 * l + u + 1)
                nc.scalar.activation(es[:, u % 2, :], es[:, u % 2, :], ACT.Exp).then_inc(sink_exp, 1)

            def square_y(l, u):
                act.wait_ge(y_normed, at_unit(l, u))
                nc.scalar.activation(bank[u % 2][:], y[:, u % 2, :], ACT.Square, scale=512 ** -0.5,
                                     accum_out=mean_sq[:, u % 2, :]).then_inc(y_squared, 1)

            def scale_y(l, u):
                n = rs_index(l, u)
                act.wait_ge(rs_done, n + 1)
                act.wait_ge(y_squared, at_unit(l, u))
                nc.scalar.activation(y[:, u % 2, :], y[:, u % 2, :], ACT.Copy, scale=rs_out[:, n:n + 1])\
                    .then_inc(y_ready, 1)

            def split_y(l, u):
                kind, t = UNITS[u]
                act.wait_ge(y_transposed, at_unit(l, u))
                k0 = 0 if kind == "A" else 4
                nc.scalar.activation(hT_hi[:, k0:k0 + 4, t * P:(t + 1) * P],
                                     bank[2][:].rearrange("p (k s) -> p k s", k=4), ACT.Copy).then_inc(yT_hi, 1)

            def attention(l):
                for i in range(64 + LAG_SPLIT):
                    if 0 <= i - LAG_T < 64:
                        u, h = (i - LAG_T) // 8, (i - LAG_T) % 8
                        if not on_dve(u, h):
                            copy_p(l, u, h)
                    if i < 64:
                        exponential(l, i // 8, i % 8)
                        u, h = i // 8, i % 8
                        if h == 7 and UNITS[u][0] == "A":
                            sink_weight(l, u)
                    if i - 1 in QB_STEPS[CP[4] - 1::CP[4]]:
                        evacuate(l, 4, QB_STEPS.index(i - 1) // CP[4])
                    for lag, part in ((LAG_NORM, square_y), (LAG_SCALE, scale_y), (LAG_SPLIT, split_y)):
                        if (i - lag) % 8 == 7 and i > lag:
                            part(l, (i - lag) // 8)
                    if i in QB_AT:
                        copy_qk(l, 4, QB_AT.index(i))
                    if i in WO_AT:
                        convert(l, WO_P + WO_AT.index(i) + 1)

            def feed(l, g):
                p0 = GU_P[g]
                f0 = gu_before(l, g)
                s0 = slot(l, p0)
                with act.Fori(0, FG[g] // 2) as i:
                    for f in range(2):
                        act.wait_ge(piece_used, i * 4 + used(l, p0 + 2 * f))
                        nc.scalar.activation(silu_g[:, f, :], bank[GU_BANK[g] + 2 * f][:], ACT.Silu)\
                            .then_inc(gate_read, 1)
                        for j in (2 * f + 4, 2 * f + 5):
                            s = (s0 + j) % RING
                            act.wait_ge(raw_in[s], i * 16 + 16 * ((l * NP + p0 + j) // RING + 1))
                            act.wait_ge(piece_used, i * 4 + (l * NP + p0 + j + 1))
                            nc.scalar.activation(w_hi[:, s, :], w_raw[:, s, :], ACT.Copy).then_inc(hi_ready, 1)
                        act.wait_ge(gu_ready, i * 2 + (f0 + f + 1 + 2))
                        nc.scalar.activation(gu_hi[:, bass.ds(i * 2 + f, 1), :], gu[:, f:f + 1, :], ACT.Copy)\
                            .then_inc(gu_hi_ready, 1)
                conv[0] += 4 * (FG[g] // 2)

            act.dma_start(cc[:, 0, :], c_col).then_inc(c_in, 16)
            act.wait_ge(c_in, 16)
            nc.scalar.activation(cc[:, 1, :], cc[:, 0, :], ACT.Silu).then_inc(rope_table, 1)
            for dst, src in ((modb[:], b_ada), (lnc[:], ln_col), (gcol[:], g_col)):
                act.dma_start(dst, src).then_inc(small_in, 16)
            act.dma_start(nsink[:], sinks.to_broadcast([P, DEPTH, HEADS])).then_inc(small_in, 16)
            act.dma_start(angles[:, 0, 0:32], inv_freq.to_broadcast([P, 32])).then_inc(small_in, 16)
            act.dma_start(angles[:, 0, 32:36].bitcast(I32), positions).then_inc(small_in, 16)
            nc.scalar.sem_inc(gate_read, 2)
            act.wait_ge(rope_angle, 1)
            nc.scalar.activation(angles[:, 1, 0:256], angles[:, 1, 0:256], ACT.Sin).then_inc(rope_table, 1)
            for t in range(T):
                build_h(0, t, 4, t + 1)
            for l in range(DEPTH):
                for c in range(2):
                    convert(l, C0P[c + 1] + 2)
                    for t in range(T):
                        evacuate(l, c, t)
                    convert(l, C0P[c + 1] + 3)
                for t in range(T):
                    copy_qk(l, 0, t)
                for t in range(T):
                    copy_qk(l, 1, t)
                for i in range(len(IDX_TILES)):
                    for h in range(HEADS):
                        relu(l, i, h)
                convert(l, C0P[4] + 1)
                for t in range(T):
                    evacuate(l, 2, t)
                convert(l, C0P[4] + 2)
                for t in range(T):
                    evacuate(l, 3, t)
                convert(l, C0P[4] + 3)
                for t in range(T):
                    copy_qk(l, 2, t)
                for t in range(T):
                    copy_qk(l, 3, t)
                convert(l, C0P[4] + 4)
                attention(l)
                for t in range(T):
                    convert(l, WO_P + 4 + t + 1)
                for t in range(2):
                    build_h(2 * l + 1, t, 0, 0)
                convert(l, GU_P[0] + 3)
                for t in range(2, T):
                    build_h(2 * l + 1, t, 0, GU_P[0] + 4)
                feed(l, 0)
                convert(l, GU_P[1] + 4)
                feed(l, 1)
                convert(l, NP)
                if l + 1 < DEPTH:
                    for t in range(2):
                        build_h(2 * l + 2, t, 4, 0)
                    convert(l + 1, 3)
                    for t in range(2, T):
                        build_h(2 * l + 2, t, 4, 4)

        @block.vector
        def _(dve):
            steps = [0]
            conv = [0]

            def step(ins):
                steps[0] += 1
                ins.then_inc(dve_step, 1)
                dve.wait_ge(dve_step, steps[0])

            def convert(l, upto):
                while conv[0] < min(l * NP + upto, DEPTH * NP):
                    p = conv[0]
                    dve.wait_ge(hi_ready, p + 1)
                    if WO_P <= p % NP < WO_P + 8:
                        for cols, gain in gained(p):
                            m = nc.vector.scalar_tensor_tensor(out=w_lo[:, p % RING, cols],
                                                               in0=w_raw[:, p % RING, cols], scalar=gain,
                                                               in1=w_hi[:, p % RING, cols].bitcast(F32),
                                                               op0=ALU.mult, op1=ALU.subtract)
                    else:
                        m = nc.vector.tensor_tensor(w_lo[:, p % RING, :], w_raw[:, p % RING, :],
                                                    w_hi[:, p % RING, :].bitcast(F32), ALU.subtract)
                    m.then_inc(lo_ready, 1)
                    conv[0] += 1

            def ada_group(g, k0=0, k1=KD):
                for k in range(k0, k1):
                    n = g * KD + k
                    if k > 0:
                        dve.wait_ge(ada_used, n)
                    ada_piece(n, k, g)

            def ada_piece(n, k, g):
                if n < 2 * KD:
                    dve.wait_ge(ada_first_in[n % RING], 16 * (n // RING + 1))
                else:
                    dve.wait_ge(ada_in[n % RING], 16 * ((n - 2 * KD) // RING + 1))
                if k == 0:
                    if g >= 2:
                        dve.wait_ge(mod_reduced, g - 1)
                    nc.vector.tensor_scalar(ada_acc[:, g % 2, :], ada_w[:, n % RING, :], cc[:, 1, 0:1], None,
                                            ALU.mult).then_inc(ada_used, 1)
                else:
                    nc.vector.scalar_tensor_tensor(out=ada_acc[:, g % 2, :], in0=ada_w[:, n % RING, :],
                                                   scalar=cc[:, 1, k:k + 1], in1=ada_acc[:, g % 2, :],
                                                   op0=ALU.mult, op1=ALU.add).then_inc(ada_used, 1)

            def take_mod(g, b):
                dve.wait_ge(mod_reduced, g + 1)
                nc.vector.tensor_tensor(mod[:, g, :], bank[b][:, 0:KD], modb[:, g, :], ALU.add)\
                    .then_inc(mod_taken, 1)
                dve.wait_ge(mod_taken, g + 1)

            def h_coefficients(stage):
                l, second = stage // 2, stage % 2
                sh, sc = mod[:, 6 * l + 3 * second, :], mod[:, 6 * l + 3 * second + 1, :]
                nc.vector.scalar_tensor_tensor(out=hcoef[:, stage, 0, :], in0=sc, scalar=1.0,
                                               in1=lnc[:, stage, 0, :], op0=ALU.add, op1=ALU.mult)
                step(nc.vector.scalar_tensor_tensor(out=hcoef[:, stage, 1, :], in0=sc, scalar=1.0,
                                                    in1=lnc[:, stage, 1, :], op0=ALU.add, op1=ALU.mult))
                nc.vector.tensor_tensor(hcoef[:, stage, 1, :], hcoef[:, stage, 1, :], sh, ALU.add)\
                    .then_inc(coef_ready, 1)
                dve.wait_ge(coef_ready, stage + 1)

            def gate_diagonal(l, which):
                g = 6 * l + (GT1, GT2)[which]
                if which == 0:
                    dve.wait_ge(roped, at_chunk(l, 4, T - 1))
                else:
                    dve.wait_ge(h_lo, at_tile(2 * l + 1, T - 1))
                step(nc.vector.tensor_scalar(mod[:, g, :], mod[:, g, :], 1.0, None, ALU.add))
                nc.vector.tensor_tensor(scratch[:].rearrange("p (k s) -> p k s", k=KD),
                                        ident[:].unsqueeze(1).to_broadcast([P, KD, P]),
                                        mod[:, g, :].unsqueeze(2).to_broadcast([P, KD, P]), ALU.mult)\
                    .then_inc(gt_diag, 1)

            def take_gate(l, which, b):
                dve.wait_ge(gt_spread, 2 * l + which + 1)
                for half in range(2):
                    m = nc.vector.tensor_copy(gt_row[:, half * 512:(half + 1) * 512], bank[b + half][:])
                m.then_inc(gt_taken, 1)
                dve.wait_ge(gt_taken, 2 * l + which + 1)

            def scale_h(stage, t, b0):
                dve.wait_ge(x_transposed, at_tile(stage, t))
                if stage > 0 or t > 0:
                    dve.wait_ge(h_hi, at_tile(stage, t) - 1)
                    dve.wait_ge(h_lo, at_tile(stage, t) - 1)
                for k in range(dve_chunks(stage, t)):
                    m = nc.vector.tensor_scalar(scratch[:, k * P:(k + 1) * P],
                                                bank[b0 + 2 * (t % 2)][:, k * P:(k + 1) * P],
                                                hcoef[:, stage, 0, k:k + 1], hcoef[:, stage, 1, k:k + 1],
                                                ALU.mult, ALU.add)
                m.then_inc(h_scaled_dve, 1)

            def split_h(stage, t):
                dve.wait_ge(h_hi, at_tile(stage, t))
                cols = slice(t * P, (t + 1) * P)
                nc.vector.tensor_tensor(hT_lo[:, :, cols], scratch[:].rearrange("p (k s) -> p k s", k=KD),
                                        hT_hi[:, :, cols].bitcast(F32), ALU.subtract).then_inc(h_lo, 1)

            def rope(l, c, t):
                dve.wait_ge(proj_evac, at_chunk(l, c, t))
                if at_chunk(l, c, t) > 1:
                    dve.wait_ge(roped, at_chunk(l, c, t) - 1)
                step(rotate(nc.vector, c, t))
                rotate_sum(nc.vector, c, t).then_inc(roped, 1)

            def add_index_head(l, i, h):
                t = IDX_TILES[i]
                w = (t + 1) * P
                n = 24 * l + 8 * i + h
                dve.wait_ge(relu_done, n + 1)
                part = rel[:, (8 * i + h) % P_RING, 0:w]
                sc = scores[:, SC_AT[t]:SC_AT[t] + w]
                weight = wi[:, t, h:h + 1]
                if h == 0:
                    nc.vector.tensor_scalar(sc, part, weight, None, ALU.mult).then_inc(idx_acc, 1)
                else:
                    nc.vector.scalar_tensor_tensor(out=sc, in0=part, scalar=weight, in1=sc, op0=ALU.mult, op1=ALU.add)\
                        .then_inc(idx_acc, 1)
                dve.wait_ge(idx_acc, n + 1)
                if h == HEADS - 1:
                    own = scores[:, SC_AT[t] + t * P:SC_AT[t] + w]
                    step(nc.vector.tensor_tensor(own, own, band[:, P:2 * P], ALU.add))

            def top_rounds(r0, r1):
                for r in range(r0, r1):
                    for t in IDX_TILES:
                        sc = scores[:, SC_AT[t]:SC_AT[t] + (t + 1) * P]
                        steps[0] += 1
                        if r > 0:
                            dve.wait_ge(dve_step, steps[0] - 3)
                        nc.vector.max(top8[:, t, :], sc).then_inc(dve_step, 1)
                    for t in IDX_TILES:
                        sc = scores[:, SC_AT[t]:SC_AT[t] + (t + 1) * P]
                        steps[0] += 1
                        dve.wait_ge(dve_step, steps[0] - 3)
                        nc.vector.match_replace(out=sc, in_to_replace=top8[:, t, :], in_values=sc, imm_value=TAKEN)\
                            .then_inc(dve_step, 1)

            def top_masks():
                dve.wait_ge(dve_step, steps[0])
                step(nc.vector.tensor_scalar(scores[:], scores[:], CUT, NEG, ALU.is_gt, ALU.mult))

            def mask_scores(l, u, h):
                kind, t = UNITS[u]
                lo, hi = keys_of(UNITS[u])
                n = 8 * u + h
                dve.wait_ge(scored, at_head(l, u, h))
                if n >= P_RING:
                    dve.wait_ge(p_transposed, at_head(l, u, h) - P_RING)
                else:
                    dve.wait_ge(qk_transposed, at_chunk(l, 2, T - 1))
                if h == 0 and u >= 2:
                    dve.wait_ge(probs, at_head(l, u - 2, 7))
                if kind == "A":
                    mask = band[:] if t > 0 else band[:, P:2 * P]
                    start = nsink[:, l, h:h + 1]
                else:
                    mask = scores[:, SC_AT[t]:SC_AT[t] + hi - lo] if t > 0 else band[:, P:2 * P]
                    start = 3.0e38
                nc.vector.tensor_tensor_reduce(out=prob[:, n % P_RING, 0:hi - lo], in0=s_bank(n)[:, 0:hi - lo],
                                               in1=mask, scale=-(HD ** -0.5), scalar=start, op0=ALU.add,
                                               op1=ALU.min, accum_out=nmax[:, u % 2, h:h + 1]).then_inc(masked, 1)

            def copy_p(l, u, h):
                lo, hi = keys_of(UNITS[u])
                dve.wait_ge(p_transposed, at_head(l, u, h))
                if before := back(u, h, PT_RING):
                    dve.wait_ge(av_done, at_head(l, *before))
                nc.vector.tensor_copy(pT[:, h % PT_RING, 0:hi - lo], bank[6 + h % 2][:, 0:hi - lo]).then_inc(pT_dve, 1)

            def sink_difference(l, u):
                dve.wait_ge(masked, at_head(l, u, 7))
                nc.vector.tensor_tensor(es[:, u % 2, :], nmax[:, u % 2, :], nsink[:, l, :], ALU.subtract)\
                    .then_inc(sink_diff, 1)

            def norm_y(l, u):
                kind, t = UNITS[u]
                b = u % 2
                dve.wait_ge(probs, at_head(l, u, 7))
                total = rowsum[:, b, :]
                if kind == "A":
                    dve.wait_ge(sink_exp, 4 * l + u + 1)
                    step(nc.vector.tensor_tensor(es[:, b, :], rowsum[:, b, :], es[:, b, :], ALU.add))
                    total = es[:, b, :]
                step(nc.vector.reciprocal(recip[:, b, :], total))
                dve.wait_ge(av_done, at_head(l, u, 7))
                if u >= 2:
                    dve.wait_ge(y_transposed, at_unit(l, u - 2))
                nc.vector.tensor_tensor(y[:, b, :].rearrange("p (h d) -> p h d", h=HEADS),
                                        bank[b][:].rearrange("p (h d) -> p h d", h=HEADS),
                                        recip[:, b, :].unsqueeze(2).to_broadcast([P, HEADS, HD]), ALU.mult)\
                    .then_inc(y_normed, 1)

            def ask_root(l, u):
                n = rs_index(l, u)
                dve.wait_ge(y_squared, at_unit(l, u))
                nc.vector.tensor_scalar(rs_in[:, n:n + 1], mean_sq[:, u % 2, :], RMS_EPS, None, ALU.add)\
                    .then_inc(rs_asked, 1)

            def split_y(l, u):
                kind, t = UNITS[u]
                k0 = 0 if kind == "A" else 4
                dve.wait_ge(yT_hi, at_unit(l, u))
                cols = slice(t * P, (t + 1) * P)
                nc.vector.tensor_tensor(hT_lo[:, k0:k0 + 4, cols], bank[2][:].rearrange("p (k s) -> p k s", k=4),
                                        hT_hi[:, k0:k0 + 4, cols].bitcast(F32), ALU.subtract).then_inc(yT_lo, 1)

            def residual(l, q, t, first):
                half = (q - WO0) % 2
                cols = slice(half * HALF, (half + 1) * HALF)
                wait_phase(dve, l, q, t)
                nc.vector.tensor_tensor(ztmp[:], bank[BANKS[q] + t][:], gt_row[:, cols], ALU.mult)\
                    .then_inc(z_done, 1)
                dve.wait_ge(z_done, at_z(l, q, place(q, t)))
                step(nc.vector.scalar_tensor_tensor(out=xs[:, t, cols], in0=xs[:, t, cols],
                                                    scalar=ALPHA if first else 1.0, in1=ztmp[:],
                                                    op0=ALU.mult, op1=ALU.add))
                if q in (WO0, WO1, DN10, DN11):
                    steps[0] += 1
                    nc.vector.bn_stats(stats[:, t, half, :], xs[:, t, cols]).then_inc(dve_step, 1)

            def moments(l, second, t):
                r = rs_index(l, 8 + 4 * second + t)
                dve.wait_ge(dve_step, steps[0])
                step(nc.vector.bn_aggr(mean_var[:, t, :], stats[:, t, :, :]))
                nc.vector.tensor_scalar(rs_in[:, r:r + 1], mean_var[:, t, 1:2], LN_EPS, None, ALU.add)\
                    .then_inc(rs_asked, 1)

            def normalise(l, second, t):
                r = rs_index(l, 8 + 4 * second + t)
                dve.wait_ge(rs_done, r + 1)
                nc.vector.tensor_scalar(xs[:, t, :], xs[:, t, :], mean_var[:, t, 0:1], rs_out[:, r:r + 1],
                                        ALU.subtract, ALU.mult).then_inc(xhat_ready, 1)

            def output_tile(t):
                r = rs_index(DEPTH - 1, 12 + t)
                dve.wait_ge(row_in, 32 * 2 * DEPTH)
                for half in range(2):
                    cols = slice(half * HALF, (half + 1) * HALF)
                    m = nc.vector.scalar_tensor_tensor(out=xs[:, t, cols], in0=xs[:, t, cols],
                                                       scalar=mean_var[:, t, 0:1], in1=g_row[:, cols],
                                                       op0=ALU.subtract, op1=ALU.mult)
                step(m)
                dve.wait_ge(rs_done, r + 1)
                for half in range(2):
                    cols = slice(half * HALF, (half + 1) * HALF)
                    nc.vector.scalar_tensor_tensor(out=xs[:, t, cols], in0=xs[:, t, cols],
                                                   scalar=rs_out[:, r:r + 1], in1=b_row[:, cols],
                                                   op0=ALU.mult, op1=ALU.add).then_inc(out_ready, 1)

            def last_tiles(l, q, b0):
                second = int(q == DN11)
                stage = 2 * l + 1 + second
                pieces = (l, GU_P[0]) if q == WO1 else (l + 1, 0)

                def convert_next(n):
                    convert(pieces[0], pieces[1] + n)

                for t in range(T):
                    residual(l, q, t, not second)
                    moments(l, second, t)
                    if t == T - 1:
                        convert_next(2)
                    normalise(l, second, t)
                    if 0 < t < T - 1:
                        split_h(stage, t - 1)
                    if t == T - 2:
                        convert_next(1)
                for t in range(2, T):
                    convert_next(t + 1)
                    scale_h(stage, t, b0)
                    if t == 2:
                        convert_next(4)
                    split_h(stage, t)

            def affine(stage, t):
                dve.wait_ge(row_in, 32 * stage)
                dve.wait_ge(x_transposed, at_tile(stage, t))
                step(nc.vector.tensor_tensor(xs[:, t, :], xs[:, t, :], g_row[:], ALU.mult))
                nc.vector.tensor_tensor(xs[:, t, :], xs[:, t, :], b_row[:], ALU.add).then_inc(affine_done, 1)
                dve.wait_ge(affine_done, at_tile(stage - 1, t))

            def rope_tables():
                two_pi = 2.0 * np.pi
                c1 = np.float32(np.round(two_pi * 2 ** 8) / 2 ** 8)
                c2 = np.float32(np.round((two_pi - float(c1)) * 2 ** 20) / 2 ** 20)
                c3 = np.float32(two_pi - float(c1) - float(c2))
                magic = 1.5 * 2 ** 23
                pos_f = top8[:, 0, 0:T]
                step(nc.vector.tensor_copy(pos_f, angles[:, 0, 32:36].bitcast(I32)))
                ang = angles[:, 0, 64:192]
                for t in range(T):
                    m = nc.vector.tensor_scalar(ang[:, t * 32:(t + 1) * 32], angles[:, 0, 0:32],
                                                pos_f[:, t:t + 1], None, ALU.mult)
                step(m)
                turns = angles[:, 0, 192:448]
                nc.vector.tensor_scalar(turns[:, 0:128], ang, 1.0 / two_pi, None, ALU.mult)
                step(nc.vector.tensor_scalar(turns[:, 128:256], ang, 1.0 / two_pi, 0.25, ALU.mult, ALU.add))
                step(nc.vector.tensor_scalar(turns, turns, magic, None, ALU.add))
                step(nc.vector.tensor_scalar(turns, turns, -magic, None, ALU.add))
                r = angles[:, 1, 0:256]
                for i in range(2):
                    m = nc.vector.scalar_tensor_tensor(out=r[:, i * 128:(i + 1) * 128],
                                                       in0=turns[:, i * 128:(i + 1) * 128], scalar=-float(c1),
                                                       in1=ang, op0=ALU.mult, op1=ALU.add)
                step(m)
                for c in (c2, c3):
                    step(nc.vector.scalar_tensor_tensor(out=r, in0=turns, scalar=-float(c), in1=r,
                                                        op0=ALU.mult, op1=ALU.add))
                step(nc.vector.tensor_scalar(r[:, 128:256], r[:, 128:256], float(np.float32(np.pi / 2)), None,
                                             ALU.add))
                pi = float(np.nextafter(np.float32(np.pi), np.float32(0)))
                nc.vector.tensor_scalar(r, r, pi, -pi, ALU.min, ALU.max).then_inc(rope_angle, 1)

            def rope_signs():
                dve.wait_ge(rope_table, 2)
                s = angles[:, 1, 0:128].rearrange("p (t d) -> p t d", t=T)
                c = angles[:, 1, 128:256].rearrange("p (t d) -> p t d", t=T)
                nc.vector.tensor_scalar(sin_t[:, :, 0:32], s, -1.0, None, ALU.mult)
                nc.vector.tensor_copy(sin_t[:, :, 32:64], s)
                nc.vector.tensor_copy(cos_t[:, :, 0:32], c)
                nc.vector.tensor_copy(cos_t[:, :, 32:64], c).then_inc(tables_ready, 1)
                dve.wait_ge(tables_ready, 1)

            def attention(l):
                done = EARLY_ROUNDS
                for i in range(64 + LAG_SPLIT):
                    if i < 64:
                        u, h = i // 8, i % 8
                        mask_scores(l, u, h)
                        if h == 7 and UNITS[u][0] == "A":
                            sink_difference(l, u)
                    if i < MASKS_AT:
                        upto = EARLY_ROUNDS + (TOPK // 8 - EARLY_ROUNDS) * (i + 1) // MASKS_AT
                        top_rounds(done, upto)
                        done = upto
                        if i == MASKS_AT - 1:
                            top_masks()
                    if 0 <= i - LAG_T < 64:
                        u, h = (i - LAG_T) // 8, (i - LAG_T) % 8
                        if on_dve(u, h):
                            copy_p(l, u, h)
                    for lag, part in ((LAG_NORM, norm_y), (LAG_ROOT, ask_root), (LAG_SPLIT, split_y)):
                        if (i - lag) % 8 == 7 and i > lag:
                            part(l, (i - lag) // 8)
                    if i in WO_AT:
                        convert(l, WO_P + WO_AT.index(i) + 1)
                    if i in ASIDE_AT:
                        k = ASIDE_AT.index(i)
                        if l == 0:
                            ada_group(4, k, k + 1)
                        elif k % 2 == 0:
                            affine(2 * l, k // 2)

            def feed(l, g):
                p0 = GU_P[g]
                f0 = gu_before(l, g)
                s0 = slot(l, p0)
                with_ada = (l, g) == (0, 0)

                def low_half(i, j):
                    s = (s0 + j) % RING
                    dve.wait_ge(hi_ready, i * 4 + converted(l, p0 + j))
                    nc.vector.tensor_tensor(w_lo[:, s, :], w_raw[:, s, :], w_hi[:, s, :].bitcast(F32),
                                            ALU.subtract).then_inc(lo_ready, 1)

                def ada_pieces(i, k0, k1):
                    for k in range(k0, k1):
                        n = 5 * KD + k
                        dve.wait_ge(ada_in[n % RING], i * (16 * KD // RING) + 16 * ((n - 2 * KD) // RING + 1))
                        if k == 0:
                            m = nc.vector.tensor_scalar(ada_acc[:, 1, :], ada_w[:, n % RING, :], cc[:, 1, 0:1],
                                                        None, ALU.mult)
                        else:
                            dve.wait_ge(ada_used, i * KD + n)
                            m = nc.vector.scalar_tensor_tensor(
                                out=ada_acc[:, 1, :], in0=ada_w[:, n % RING, :], scalar=cc[:, 1, k:k + 1],
                                in1=ada_acc[:, 1, :], op0=ALU.mult, op1=ALU.add)
                        m.then_inc(ada_used, 1)

                with dve.Fori(0, FG[g] // 2) as i:
                    for f in range(2):
                        if with_ada:
                            ada_pieces(i, 4 * f, 4 * f + 4)
                        low_half(i, 2 * f + 4)
                        dve.wait_ge(piece_used, i * 4 + used(l, p0 + 2 * f + 1))
                        dve.wait_ge(gate_read, i * 2 + (f0 + f + 1 + 2))
                        nc.vector.tensor_tensor(gu[:, f, :], bank[GU_BANK[g] + 2 * f + 1][:], silu_g[:, f, :],
                                                ALU.mult).then_inc(gu_ready, 1)
                        low_half(i, 2 * f + 5)
                        dve.wait_ge(gu_hi_ready, i * 2 + (f0 + f + 1))
                        at = bass.ds(i * 2 + f, 1)
                        nc.vector.tensor_tensor(gu_lo[:, at, :], gu[:, f:f + 1, :],
                                                gu_hi[:, at, :].bitcast(F32), ALU.subtract).then_inc(gu_lo_ready, 1)
                        dve.wait_ge(gu_lo_ready, i * 2 + (f0 + f + 1))
                    if with_ada:
                        dve.wait_ge(mod_reduced, i + 6)
                        nc.vector.tensor_tensor(mod[:, bass.ds(i + 5, 1), :],
                                                bank[0][:, 0:KD].unsqueeze(1),
                                                modb[:, bass.ds(i + 5, 1), :], ALU.add).then_inc(mod_taken, 1)
                if with_ada:
                    dve.wait_ge(mod_taken, 5 + FG[0] // 2)
                conv[0] += 4 * (FG[g] // 2)

            nc.vector.sem_inc(gu_ready, 2)
            dve.wait_ge(consts, 4)
            dve.wait_ge(rope_table, 1)
            ada_group(0)
            ada_group(1)
            dve.wait_ge(small_in, 16 * 6)
            rope_tables()
            step(nc.vector.tensor_scalar(nsink[:], nsink[:], -1.0, None, ALU.mult))
            take_mod(0, 0)
            take_mod(1, 1)
            h_coefficients(0)
            for t in range(T):
                scale_h(0, t, 4)
                convert(0, t + 1)
                split_h(0, t)
                if t == 0:
                    rope_signs()
            for l in range(DEPTH):
                convert(l, 4)
                if l == 0:
                    ada_group(2, 0, 4)
                    convert(l, 5)
                    ada_group(2, 4, KD)
                convert(l, C0P[2] + 1)
                if l == 0:
                    ada_group(3, 0, 2)
                convert(l, C0P[2] + 2)
                if l == 0:
                    ada_group(3, 2, 4)
                for t in range(T):
                    rope(l, 1, t)
                convert(l, C0P[2] + 3)
                for i in range(len(IDX_TILES)):
                    for h in range(HEADS):
                        add_index_head(l, i, h)
                convert(l, C0P[3])
                if l == 0:
                    ada_group(3, 4, 6)
                    convert(l, C0P[3] + 1)
                    ada_group(3, 6, KD)
                top_rounds(0, 1)
                convert(l, C0P[3] + 1)
                top_rounds(1, 2)
                convert(l, C0P[4] + 1)
                for t in range(T):
                    rope(l, 2, t)
                convert(l, C0P[4] + 2)
                for t in range(T):
                    rope(l, 3, t)
                top_rounds(2, EARLY_ROUNDS)
                convert(l, C0P[4] + 4)
                if l == 0:
                    take_mod(2, 6)
                    take_mod(3, 7)
                attention(l)
                gate_diagonal(l, 0)
                take_gate(l, 0, 5)
                convert(l, WO_P + 6)
                for t in WO0_ORDER[:2]:
                    residual(l, WO0, t, True)
                    convert(l, WO_P + 7 + WO0_ORDER.index(t))
                for t in WO0_ORDER[2:]:
                    residual(l, WO0, t, True)
                if l == 0:
                    take_mod(4, 7)
                if l == 0:
                    h_coefficients(1)
                else:
                    h_coefficients(3)
                last_tiles(l, WO1, 0)
                feed(l, 0)
                if l == 0:
                    h_coefficients(2)
                gate_diagonal(l, 1)
                affine(2 * l + 1, 0)
                affine(2 * l + 1, 1)
                convert(l, DN_P[0] + 5)
                take_gate(l, 1, 4)
                for t in range(2, T):
                    affine(2 * l + 1, t)
                    convert(l, DN_P[0] + 4 + t)
                for half in range(2):
                    q = DN00 + half
                    convert(l, PHASES[q][0] + PHASES[q][1] + (3, 2)[half])
                    for t in range(T):
                        residual(l, q, t, True)
                    if (l, half) == (0, 0):
                        ada_group(6 * DEPTH - 1)
                convert(l, GU_P[1] + 4)
                feed(l, 1)
                if l == 0:
                    take_mod(6 * DEPTH - 1, 7)
                convert(l, DN_P[1] + 5)
                for t in range(T):
                    convert(l, DN_P[1] + 5 + t)
                    residual(l, DN10, t, False)
                convert(l, NP)
                if l + 1 < DEPTH:
                    last_tiles(l, DN11, 4)
                else:
                    for t in range(T):
                        residual(l, DN11, t, False)
                        moments(l, 1, t)
                        output_tile(t)


def weight_pieces(w_in, w_o, w_gate, w_up, w_down):
    a_q, a_k, a_v, b_q, b_k, b_v, i_q, i_k, i_w = np.split(
        w_in, np.cumsum([512, 128, 128, 512, 128, 128, 512, 64]), axis=-1)
    chunks = [i_q, np.concatenate([i_k, b_k, b_v, i_w], -1), paired(a_q, -1),
              np.concatenate([a_k, a_v], -1), paired(b_q, -1)]
    out = np.zeros((DEPTH, NP, P, PW), np.float32)
    w_o = np.concatenate([paired(w_o[:, :512], 1), paired(w_o[:, 512:], 1)], 1)
    for c, w in enumerate(chunks):
        for j in range(CP[c]):
            for kk in range(CK[c]):
                k = j * CK[c] + kk
                out[:, C0P[c] + j, :, kk * CW[c]:(kk + 1) * CW[c]] = w[:, k * P:(k + 1) * P]
    for half in range(2):
        cols = slice(half * HALF, (half + 1) * HALF)
        for k in range(KD):
            out[:, WO_P + 4 * half + k // 2, :, (k % 2) * 512:(k % 2 + 1) * 512] = w_o[:, k * P:(k + 1) * P, cols]
    f0 = 0
    for g in range(2):
        for f in range(FG[g]):
            cols = slice((f0 + f) * P, (f0 + f + 1) * P)
            for i, w in enumerate((w_gate, w_up)):
                out[:, GU_P[g] + 2 * f + i] = w[:, :, cols].reshape(DEPTH, KD, P, P).transpose(0, 2, 1, 3)\
                    .reshape(DEPTH, P, PW)
            for half in range(2):
                out[:, DN_P[g] + half * FG[g] // 2 + f // 2, :, (f % 2) * 512:(f % 2 + 1) * 512] = \
                    w_down[:, cols, half * HALF:(half + 1) * HALF]
        f0 += FG[g]
    return out.reshape(DEPTH * NP, P, PW)


def paired(a, axis):
    axis = axis % a.ndim
    n = a.shape[axis] // HEADS
    s = a.shape
    b = a.reshape(s[:axis] + (KV_HEADS, PAIRS, n) + s[axis + 1:])
    return np.swapaxes(b, axis, axis + 1).reshape(s)


def kernel(x, c, positions, w_ada, b_ada, w_in, attn_sinks, g_a, g_b, w_o,
           ln1_g, ln1_b, w_gate, w_up, w_down, ln2_g, ln2_b):
    import concourse.bacc as bacc
    from concourse.bass_utils import run_bass_kernel_spmd

    def columns(a):
        a = np.asarray(a)
        return np.ascontiguousarray(np.moveaxis(a.reshape(a.shape[:-1] + (-1, P)), -1, 0))

    (x, c, positions, w_ada, b_ada, w_in, attn_sinks, g_a, g_b, w_o, ln1_g, ln1_b, w_gate, w_up, w_down,
     ln2_g, ln2_b) = map(np.asarray, (x, c, positions, w_ada, b_ada, w_in, attn_sinks, g_a, g_b, w_o, ln1_g,
                                      ln1_b, w_gate, w_up, w_down, ln2_g, ln2_b))
    one, zero = np.ones((D_MODEL,), np.float32), np.zeros((D_MODEL,), np.float32)
    rows = np.stack([np.stack([g, b]) for l in range(DEPTH)
                     for g, b in ((ln1_g[l], ln1_b[l]), (ln2_g[l], ln2_b[l]))])
    before = np.concatenate([np.stack([one, zero])[None], rows[:-1]])
    arrays = {
        "x": x.reshape(T, P, D_MODEL),
        "c_col": columns(c[0]),
        "positions": positions.reshape(T, P).T,
        "inv_freq": (ROPE_THETA ** (-np.arange(HD // 2) / (HD // 2))).astype(np.float32)[None],
        "weights": weight_pieces(w_in, w_o, w_gate, w_up, w_down),
        "w_ada": w_ada.reshape(DEPTH, KD, P, 6, PW).transpose(0, 3, 1, 2, 4).reshape(6 * DEPTH, KD, P, PW),
        "b_ada": columns(b_ada.reshape(6 * DEPTH, D_MODEL)),
        "ln_col": columns(before),
        "ln_row": rows,
        "sinks": paired(attn_sinks, 1)[None],
        "g_col": columns(np.stack([paired(g_a, 1), paired(g_b, 1)], 1)),
    }
    nc = bacc.Bacc("TRN2", target_bir_lowering=False, num_devices=1)
    ins, aps = {}, {}
    for name, a in arrays.items():
        a = np.ascontiguousarray(a)
        ins[f"in_{name}"] = a
        aps[name] = nc.dram_tensor(f"in_{name}", a.shape, mybir.dt.from_np(a.dtype), kind="ExternalInput").ap()
    out = nc.dram_tensor("trunk_out", (T, P, D_MODEL), F32, kind="ExternalOutput").ap()
    build_trunk(nc, out=out, **aps)
    r = run_bass_kernel_spmd(nc, [ins], core_ids=[0])
    return r.results[0]["trunk_out"].reshape(1, SEQ, D_MODEL)
```
